# Optimizing a Trainium2 kernel written in Bass

```python
import math
import jax, jax.numpy as jnp
from jax import lax
import numpy as np

D_MODEL = 1024
BATCH = 1
SEQ = 256
DEPTH = 2

D_FF = 2816
GDN_HEADS = 8
GDN_DK = 128
GDN_DV = 128
CONV_K = 4
CHUNK = 64
MLA_HEADS = 8
Q_LORA = 384
KV_LORA = 256
QK_NOPE = 128
QK_ROPE = 64
V_HEAD = 128
ROPE_THETA = 10000.0
Q_BLOCK = 128
EPS = 1e-6
N_MOD = 9

GDN_QK = GDN_HEADS * GDN_DK
GDN_V = GDN_HEADS * GDN_DV
GDN_CONV_C = 2 * GDN_QK + GDN_V
MLA_QK = QK_NOPE + QK_ROPE
IN_SIZES = (GDN_CONV_C, GDN_V, GDN_HEADS, GDN_HEADS, Q_LORA, KV_LORA, QK_ROPE, D_MODEL, D_MODEL)
N_IN = GDN_CONV_C + GDN_V + 2 * GDN_HEADS + Q_LORA + KV_LORA + QK_ROPE + 2 * D_MODEL


def rms_norm(x, gain):
    xf = x.astype(jnp.float32)
    y = xf * lax.rsqrt(jnp.mean(xf * xf, axis=-1, keepdims=True) + EPS)
    return (y * gain.astype(jnp.float32)).astype(x.dtype)

def l2_norm(x):
    xf = x.astype(jnp.float32)
    return xf * lax.rsqrt(jnp.sum(xf * xf, axis=-1, keepdims=True) + EPS)

def modulate(x, gain, shift, scale):
    return rms_norm(x, gain) * (1.0 + scale[:, None]) + shift[:, None]

def swiglu(h, w1, w3, w2):
    return (jax.nn.silu(h @ w1) * (h @ w3)) @ w2

def causal_dwconv(x, w):
    S = x.shape[1]
    xp = jnp.pad(x, ((0, 0), (CONV_K - 1, 0), (0, 0)))
    return sum(xp[:, j:j + S] * w[j] for j in range(CONV_K))

def rope_tables(positions):
    half = QK_ROPE // 2
    inv_freq = ROPE_THETA ** (-jnp.arange(half, dtype=jnp.float32) / half)
    ang = positions.astype(jnp.float32)[..., None] * inv_freq
    return jnp.cos(ang), jnp.sin(ang)

def apply_rope(x, cos, sin):
    x1, x2 = jnp.split(x, 2, axis=-1)
    c = cos[:, :, None].astype(x.dtype)
    s = sin[:, :, None].astype(x.dtype)
    return jnp.concatenate([x1 * c - x2 * s, x2 * c + x1 * s], axis=-1)

def gated_delta_rule(q, k, v, g, beta):
    B, S, H, DK = q.shape
    DV = v.shape[-1]
    N = S // CHUNK
    f32 = jnp.float32

    def chunks(t):
        t = t.astype(f32).reshape((B, N, CHUNK, H) + t.shape[3:])
        return jnp.moveaxis(t, (1, 3), (0, 2))

    qc = chunks(q) * (DK ** -0.5)
    kc, vc = chunks(k), chunks(v)
    gc, bc = chunks(g), chunks(beta)
    gcum = jnp.cumsum(gc, axis=-1)
    causal = jnp.tril(jnp.ones((CHUNK, CHUNK), bool))
    strict = jnp.tril(jnp.ones((CHUNK, CHUNK), bool), -1)
    decay = jnp.exp(jnp.where(causal, gcum[..., :, None] - gcum[..., None, :], -jnp.inf))
    kb = kc * bc[..., None]
    m = jnp.where(strict, jnp.einsum('nbhid,nbhjd->nbhij', kb, kc) * decay, 0.0)
    eye = jnp.eye(CHUNK, dtype=f32)
    t_inv = lax.linalg.triangular_solve(eye + m, jnp.broadcast_to(eye, m.shape), left_side=True, lower=True)
    u = t_inv @ (vc * bc[..., None])
    w = t_inv @ (kb * jnp.exp(gcum)[..., None])
    qk = jnp.einsum('nbhid,nbhjd->nbhij', qc, kc) * decay
    q_dec = qc * jnp.exp(gcum)[..., None]
    k_dec = kc * jnp.exp(gcum[..., -1:] - gcum)[..., None]
    g_last = jnp.exp(gcum[..., -1])

    def step(state, inp):
        u_i, w_i, qk_i, qd_i, kd_i, gl_i = inp
        v_new = u_i - w_i @ state
        o_i = qd_i @ state + qk_i @ v_new
        state = state * gl_i[..., None, None] + jnp.swapaxes(kd_i, -1, -2) @ v_new
        return state, o_i

    s0 = jnp.zeros((B, H, DK, DV), f32)
    _, o = lax.scan(step, s0, (u, w, qk, q_dec, k_dec, g_last))
    return jnp.moveaxis(o, (0, 2), (1, 3)).reshape(B, S, H, DV)

def gated_deltanet(qkv, z, b_raw, a_raw, conv_w, a_log, dt_bias, out_gain):
    B, S, _ = qkv.shape
    qkv_c = jax.nn.silu(causal_dwconv(qkv, conv_w))
    q, k, v = jnp.split(qkv_c, [GDN_QK, 2 * GDN_QK], axis=-1)
    q = l2_norm(q.reshape(B, S, GDN_HEADS, GDN_DK))
    k = l2_norm(k.reshape(B, S, GDN_HEADS, GDN_DK))
    v = v.reshape(B, S, GDN_HEADS, GDN_DV)
    beta = jax.nn.sigmoid(b_raw.astype(jnp.float32))
    g = -jnp.exp(a_log.astype(jnp.float32)) * jax.nn.softplus(a_raw.astype(jnp.float32) + dt_bias.astype(jnp.float32))
    o = gated_delta_rule(q, k, v, g, beta)
    o = rms_norm(o, out_gain) * jax.nn.silu(z.astype(jnp.float32).reshape(B, S, GDN_HEADS, GDN_DV))
    return o.reshape(B, S, GDN_V).astype(qkv.dtype)

def causal_block_attention(q, k, v):
    B, S, H, Dqk = q.shape
    nb = S // Q_BLOCK
    scale = Dqk ** -0.5
    qb = jnp.moveaxis(q.reshape(B, nb, Q_BLOCK, H, Dqk), 1, 0)
    kpos = jnp.arange(S)

    def one_block(args):
        i, q_i = args
        s = jnp.einsum('bqhd,bkhd->bhqk', q_i, k, preferred_element_type=jnp.float32) * scale
        qpos = i * Q_BLOCK + jnp.arange(Q_BLOCK)
        s = jnp.where(kpos[None, :] <= qpos[:, None], s, -jnp.inf)
        p = jax.nn.softmax(s, axis=-1)
        return jnp.einsum('bhqk,bkhv->bqhv', p.astype(v.dtype), v)

    o = lax.map(one_block, (jnp.arange(nb), qb))
    return jnp.moveaxis(o, 0, 1).reshape(B, S, H, v.shape[-1])

def mla(q_lat, kv_lat, k_pe, cos, sin, q_lat_gain, kv_lat_gain, w_q_up, w_kv_up, q_norm, k_norm):
    B, S, _ = q_lat.shape
    q = (rms_norm(q_lat, q_lat_gain) @ w_q_up).reshape(B, S, MLA_HEADS, MLA_QK)
    kv = (rms_norm(kv_lat, kv_lat_gain) @ w_kv_up).reshape(B, S, MLA_HEADS, QK_NOPE + V_HEAD)
    k_nope, v = jnp.split(kv, [QK_NOPE], axis=-1)
    k = jnp.concatenate([k_nope, jnp.broadcast_to(k_pe[:, :, None, :], (B, S, MLA_HEADS, QK_ROPE))], axis=-1)
    q = rms_norm(q, q_norm)
    k = rms_norm(k, k_norm)
    q = jnp.concatenate([q[..., :QK_NOPE], apply_rope(q[..., QK_NOPE:], cos, sin)], axis=-1)
    k = jnp.concatenate([k[..., :QK_NOPE], apply_rope(k[..., QK_NOPE:], cos, sin)], axis=-1)
    o = causal_block_attention(q, k, v)
    return o.reshape(B, S, MLA_HEADS * V_HEAD)

def token_mix(h, cos, sin, w_in, gdn_conv, gdn_a_log, gdn_dt_bias, gdn_out_gain, q_lat_gain, kv_lat_gain,
              w_q_up, w_kv_up, q_norm, k_norm, w_branch_a, w_branch_b, w_out):
    offsets = np.cumsum(IN_SIZES)[:-1].tolist()
    qkv, z, b_raw, a_raw, q_lat, kv_lat, k_pe, gate_a, gate_b = jnp.split(h @ w_in, offsets, axis=-1)
    y_a = gated_deltanet(qkv, z, b_raw, a_raw, gdn_conv, gdn_a_log, gdn_dt_bias, gdn_out_gain) @ w_branch_a
    y_b = mla(q_lat, kv_lat, k_pe, cos, sin, q_lat_gain, kv_lat_gain, w_q_up, w_kv_up, q_norm, k_norm) @ w_branch_b
    y = jax.nn.sigmoid(gate_a) * y_a + jax.nn.sigmoid(gate_b) * y_b
    return y @ w_out

def first_inputs(seed: int = 0) -> dict:
    key = jax.random.key(seed)
    ks = iter(jax.random.split(key, 40))
    L, D = DEPTH, D_MODEL

    def normal(shape, fan_in, gain=1.0):
        return jax.random.normal(next(ks), shape, jnp.float32) * (gain * fan_in ** -0.5)

    def ones_noise(shape):
        return 1.0 + 0.05 * jax.random.normal(next(ks), shape, jnp.float32)

    x = jax.random.normal(next(ks), (BATCH, SEQ, D), jnp.float32)
    c = jax.random.normal(next(ks), (BATCH, D), jnp.float32)
    positions = (jax.random.randint(next(ks), (BATCH, 1), 0, 1024, jnp.int32)
                 + jnp.arange(SEQ, dtype=jnp.int32)[None, :])
    ada_w = normal((L, D, N_MOD * D), D, 0.25)
    ada_b = 0.01 * jax.random.normal(next(ks), (L, N_MOD * D), jnp.float32)
    norm_ffn1 = ones_noise((L, D))
    ffn1_w1 = normal((L, D, D_FF), D)
    ffn1_w3 = normal((L, D, D_FF), D)
    ffn1_w2 = normal((L, D_FF, D), D_FF)
    norm_mix = ones_noise((L, D))
    w_in = normal((L, D, N_IN), D)
    gdn_conv = normal((L, CONV_K, GDN_CONV_C), CONV_K)
    gdn_a_log = jnp.log(jax.random.uniform(next(ks), (L, GDN_HEADS), jnp.float32, 1.0, 16.0))
    dt = jnp.exp(jax.random.uniform(next(ks), (L, GDN_HEADS), jnp.float32, math.log(1e-3), math.log(1e-1)))
    gdn_dt_bias = dt + jnp.log(-jnp.expm1(-dt))
    gdn_out_gain = ones_noise((L, GDN_DV))
    mla_q_lat_gain = ones_noise((L, Q_LORA))
    mla_kv_lat_gain = ones_noise((L, KV_LORA))
    mla_w_q_up = normal((L, Q_LORA, MLA_HEADS * MLA_QK), Q_LORA)
    mla_w_kv_up = normal((L, KV_LORA, MLA_HEADS * (QK_NOPE + V_HEAD)), KV_LORA)
    mla_q_norm = ones_noise((L, MLA_QK))
    mla_k_norm = ones_noise((L, MLA_QK))
    w_branch_a = normal((L, GDN_V, D), GDN_V)
    w_branch_b = normal((L, MLA_HEADS * V_HEAD, D), MLA_HEADS * V_HEAD)
    w_out = normal((L, D, D), D)
    norm_ffn2 = ones_noise((L, D))
    ffn2_w1 = normal((L, D, D_FF), D)
    ffn2_w3 = normal((L, D, D_FF), D)
    ffn2_w2 = normal((L, D_FF, D), D_FF)
    return {'x': x, 'c': c, 'positions': positions, 'ada_w': ada_w, 'ada_b': ada_b,
            'norm_ffn1': norm_ffn1, 'ffn1_w1': ffn1_w1, 'ffn1_w3': ffn1_w3, 'ffn1_w2': ffn1_w2,
            'norm_mix': norm_mix, 'w_in': w_in, 'gdn_conv': gdn_conv, 'gdn_a_log': gdn_a_log,
            'gdn_dt_bias': gdn_dt_bias, 'gdn_out_gain': gdn_out_gain, 'mla_q_lat_gain': mla_q_lat_gain,
            'mla_kv_lat_gain': mla_kv_lat_gain, 'mla_w_q_up': mla_w_q_up, 'mla_w_kv_up': mla_w_kv_up,
            'mla_q_norm': mla_q_norm, 'mla_k_norm': mla_k_norm, 'w_branch_a': w_branch_a,
            'w_branch_b': w_branch_b, 'w_out': w_out, 'norm_ffn2': norm_ffn2, 'ffn2_w1': ffn2_w1,
            'ffn2_w3': ffn2_w3, 'ffn2_w2': ffn2_w2}

def first_block(x, c, positions, ada_w, ada_b, norm_ffn1, ffn1_w1, ffn1_w3, ffn1_w2, norm_mix, w_in, gdn_conv,
              gdn_a_log, gdn_dt_bias, gdn_out_gain, mla_q_lat_gain, mla_kv_lat_gain, mla_w_q_up, mla_w_kv_up,
              mla_q_norm, mla_k_norm, w_branch_a, w_branch_b, w_out, norm_ffn2, ffn2_w1, ffn2_w3, ffn2_w2):
    cos, sin = rope_tables(positions)
    cond = jax.nn.silu(c)
    for l in range(DEPTH):
        mod = cond @ ada_w[l] + ada_b[l]
        sh1, sc1, g1, sh2, sc2, g2, sh3, sc3, g3 = jnp.split(mod, N_MOD, axis=-1)
        h = modulate(x, norm_ffn1[l], sh1, sc1)
        x = x + 0.5 * (1.0 + g1)[:, None] * swiglu(h, ffn1_w1[l], ffn1_w3[l], ffn1_w2[l])
        h = modulate(x, norm_mix[l], sh2, sc2)
        y = token_mix(h, cos, sin, w_in[l], gdn_conv[l], gdn_a_log[l], gdn_dt_bias[l], gdn_out_gain[l],
                      mla_q_lat_gain[l], mla_kv_lat_gain[l], mla_w_q_up[l], mla_w_kv_up[l], mla_q_norm[l],
                      mla_k_norm[l], w_branch_a[l], w_branch_b[l], w_out[l])
        x = x + (1.0 + g2)[:, None] * y
        h = modulate(x, norm_ffn2[l], sh3, sc3)
        x = x + 0.5 * (1.0 + g3)[:, None] * swiglu(h, ffn2_w1[l], ffn2_w3[l], ffn2_w2[l])
    return x


GRID_W = 64
CTX_LEN = 256
N_MIXERS = 3

SSD_D_INNER = 2 * D_MODEL
SSD_HEAD_DIM = 64
SSD_N_HEADS = SSD_D_INNER // SSD_HEAD_DIM
SSD_N_GROUPS = 4
SSD_D_STATE = 128
SSD_CONV_W = 5
SSD_CHUNK = 128
SSD_GN = SSD_N_GROUPS * SSD_D_STATE
SSD_CONV_DIM = SSD_D_INNER + 2 * SSD_GN
SSD_IN_DIM = SSD_D_INNER + SSD_CONV_DIM + 2 * SSD_N_HEADS

POOL_WINDOWS = (2, 4, 8, 16)
POOL_GROUPS = 4
POOL_GROUP_DIM = D_MODEL // POOL_GROUPS

HY_ORDER = 2
HY_SHORT_W = 3
HY_EMB_DIM = 33
HY_BANDS = (HY_EMB_DIM - 1) // 2
HY_FILTER_HIDDEN = 64
HY_MAX_DECAY = math.log(1e-2) / 0.3
HY_MIN_DECAY = math.log(1e-2) / 1.5


def rmsnorm(x, g):
    xf = x.astype(jnp.float32)
    y = xf * lax.rsqrt(jnp.mean(xf * xf, axis=-1, keepdims=True) + EPS)
    return (y * g.astype(jnp.float32)).astype(x.dtype)

def modulate_2(x, g, shift, scale):
    return rmsnorm(x, g) * (1 + scale) + shift

def swiglu_2(u, wg, wu, wd):
    return (jax.nn.silu(u @ wg) * (u @ wu)) @ wd

def dwconv_centred(u, w, b):
    K = w.shape[0]
    P = K // 2
    L = u.shape[1]
    up = jnp.pad(u, ((0, 0), (P, P), (0, 0)))
    out = b
    for k in range(K):
        out = out + w[k] * up[:, k:k + L]
    return out

def ssd_scan(x, dt, A, B, C, h0, with_output):
    b, l, H, P = x.shape
    G, N = B.shape[2], B.shape[3]
    E = H // G
    Q = SSD_CHUNK
    nc = l // Q
    xdt = (x.astype(jnp.float32) * dt[..., None]).reshape(b, nc, Q, G, E, P)
    Bc = B.astype(jnp.float32).reshape(b, nc, Q, G, N)
    Cc = C.astype(jnp.float32).reshape(b, nc, Q, G, N)
    a_cum = jnp.cumsum((dt * A).reshape(b, nc, Q, G, E), axis=2)
    a_last = a_cum[:, :, -1]
    decay_to_end = jnp.exp(a_last[:, :, None] - a_cum)
    states = jnp.einsum('bcsgn,bcsge,bcsgep->bcgepn', Bc, decay_to_end, xdt)

    def step(h, inp):
        st, al = inp
        return h * jnp.exp(al)[..., None, None] + st, h

    h_final, h_in = lax.scan(step, h0, (jnp.moveaxis(states, 1, 0), jnp.moveaxis(a_last, 1, 0)))
    if not with_output:
        return None, h_final
    h_in = jnp.moveaxis(h_in, 0, 1)
    seg = a_cum[:, :, :, None] - a_cum[:, :, None, :]
    mask = jnp.tril(jnp.ones((Q, Q), dtype=bool))[:, :, None, None]
    Lmat = jnp.exp(jnp.where(mask, seg, -jnp.inf))
    cb = jnp.einsum('bclgn,bcsgn->bclsg', Cc, Bc)
    y_diag = jnp.einsum('bclsg,bclsge,bcsgep->bclgep', cb, Lmat, xdt)
    y_off = jnp.einsum('bclgn,bcgepn,bclge->bclgep', Cc, h_in, jnp.exp(a_cum))
    y = (y_diag + y_off).reshape(b, l, H, P)
    return y.astype(x.dtype), h_final

def ssd_mixer(u_lat, u_ctx, w_in, conv_w, conv_b, a_log, dt_bias, d_skip, norm_g, w_out, need_ctx_out):
    H, P, G, N = SSD_N_HEADS, SSD_HEAD_DIM, SSD_N_GROUPS, SSD_D_STATE
    A = -jnp.exp(a_log.astype(jnp.float32))

    def project(u):
        b, l, _ = u.shape
        zxbcdt = u @ w_in
        z = zxbcdt[..., :SSD_D_INNER]
        xbc = jax.nn.silu(dwconv_centred(zxbcdt[..., SSD_D_INNER:SSD_D_INNER + SSD_CONV_DIM], conv_w, conv_b))
        dt_raw = zxbcdt[..., SSD_D_INNER + SSD_CONV_DIM:]
        xs = xbc[..., :SSD_D_INNER].reshape(b, l, H, P)
        Bm = xbc[..., SSD_D_INNER:SSD_D_INNER + SSD_GN].reshape(b, l, G, N)
        Cm = xbc[..., SSD_D_INNER + SSD_GN:].reshape(b, l, G, N)
        dt = jax.nn.softplus(dt_raw.reshape(b, l, 2, H).astype(jnp.float32) + dt_bias.astype(jnp.float32))
        return z, xs, Bm, Cm, dt

    def flip(t, d):
        return t[:, ::-1] if d == 1 else t

    zc, xc, Bc, Cc, dtc = project(u_ctx)
    zl, xl, Bl, Cl, dtl = project(u_lat)
    b = u_lat.shape[0]
    h0 = jnp.zeros((b, G, H // G, P, N), jnp.float32)
    y_lat = d_skip[:, None] * xl
    y_ctx = d_skip[:, None] * xc if need_ctx_out else None
    for d in range(2):
        yc, hc = ssd_scan(flip(xc, d), flip(dtc[:, :, d], d), A[d], flip(Bc, d), flip(Cc, d), h0, need_ctx_out)
        yl, _ = ssd_scan(flip(xl, d), flip(dtl[:, :, d], d), A[d], flip(Bl, d), flip(Cl, d), hc, True)
        y_lat = y_lat + flip(yl, d)
        if need_ctx_out:
            y_ctx = y_ctx + flip(yc, d)

    def gate_norm_out(y, z):
        b_, l_ = y.shape[:2]
        gy = (y.reshape(b_, l_, SSD_D_INNER) * jax.nn.silu(z)).reshape(b_, l_, G, SSD_D_INNER // G)
        gy = rmsnorm(gy, norm_g.reshape(G, SSD_D_INNER // G))
        return gy.reshape(b_, l_, SSD_D_INNER) @ w_out

    out_lat = gate_norm_out(y_lat, zl)
    out_ctx = gate_norm_out(y_ctx, zc) if need_ctx_out else None
    return out_lat, out_ctx

def box_sum(v, w, axis):
    L = v.shape[axis]
    cs = jnp.cumsum(v, axis=axis)
    pad = [(0, 0)] * v.ndim
    pad[axis] = (1, 0)
    cs = jnp.pad(cs, pad)
    pos = jnp.arange(L)
    hi = jnp.minimum(pos + (w - w // 2), L)
    lo = jnp.maximum(pos - w // 2, 0)
    s = jnp.take(cs, hi, axis=axis) - jnp.take(cs, lo, axis=axis)
    return s, (hi - lo).astype(jnp.float32)

def pool_grid(v, w):
    b, l, C = v.shape
    rows = l // GRID_W
    v4 = v.astype(jnp.float32).reshape(b, rows, GRID_W, C)
    s, cnt_c = box_sum(v4, w, 2)
    s, cnt_r = box_sum(s, w, 1)
    mean = s / (cnt_r[:, None, None] * cnt_c[None, :, None])
    return mean.reshape(b, l, C).astype(v.dtype) - v

def pool_seq(v, w):
    s, cnt = box_sum(v.astype(jnp.float32), w, 1)
    return (s / cnt[None, :, None]).astype(v.dtype) - v

def pool_mixer(u_lat, u_ctx, w, bias, scale, need_ctx_out):
    def mix(u, pool_fn):
        b, l, _ = u.shape
        grp = u.reshape(b, l, POOL_GROUPS, POOL_GROUP_DIM)
        pooled = jnp.stack([pool_fn(grp[:, :, g], POOL_WINDOWS[g]) for g in range(POOL_GROUPS)], axis=2)
        y = jnp.einsum('blgc,gcd->blgd', pooled, w) + bias
        return y.reshape(b, l, D_MODEL) * scale

    out_lat = mix(u_lat, pool_grid)
    out_ctx = mix(u_ctx, pool_seq) if need_ctx_out else None
    return out_lat, out_ctx

def hyena_filter_fft(L, fw1, fb1, fw2, fb2, fw3, ffreq):
    f32 = jnp.float32
    pos = jnp.arange(L, dtype=f32)
    t = jnp.linspace(0.0, 1.0, L, dtype=f32)
    wpos = 2.0 * math.pi * pos / L
    f = jnp.linspace(1e-4, HY_BANDS - 1, HY_BANDS, dtype=f32)
    ang = wpos[:, None] * f[None, :]
    z = jnp.concatenate([t[:, None], jnp.cos(ang), -jnp.sin(ang)], axis=-1)
    h = jnp.sin(ffreq[0].astype(f32) * (z @ fw1.astype(f32) + fb1.astype(f32)))
    h = jnp.sin(ffreq[1].astype(f32) * (h @ fw2.astype(f32) + fb2.astype(f32)))
    h = (h @ fw3.astype(f32)).reshape(L, HY_ORDER, 2, D_MODEL)
    deltas = jnp.abs(jnp.linspace(HY_MIN_DECAY, HY_MAX_DECAY, D_MODEL, dtype=f32))
    h = h * jnp.exp(-t[:, None, None, None] * deltas)
    h = h * lax.rsqrt(jnp.sum(h * h, axis=(0, 2), keepdims=True) + EPS)
    kern = jnp.concatenate([h[:, :, 0], jnp.zeros((1, HY_ORDER, D_MODEL), f32), h[:0:-1, :, 1]], axis=0)
    return jnp.fft.rfft(kern, axis=0)

def fftconv(u, kf, bias):
    L = u.shape[1]
    uf = u.astype(jnp.float32)
    y = jnp.fft.irfft(jnp.fft.rfft(uf, n=2 * L, axis=1) * kf, n=2 * L, axis=1)[:, :L]
    return (y + uf * bias.astype(jnp.float32)).astype(u.dtype)

def hyena_mixer(u_lat, u_ctx, w_in, conv_w, conv_b, fw1, fb1, fw2, fb2, fw3, ffreq, hbias, w_out, need_ctx_out):
    def run(u):
        kf = hyena_filter_fft(u.shape[1], fw1, fb1, fw2, fb2, fw3, ffreq)
        p = dwconv_centred(u @ w_in, conv_w, conv_b)
        v, x1, x2 = jnp.split(p, 3, axis=-1)
        z = x1 * fftconv(v, kf[:, 0], hbias[0])
        y = x2 * fftconv(z, kf[:, 1], hbias[1])
        return y @ w_out

    out_lat = run(u_lat)
    out_ctx = run(u_ctx) if need_ctx_out else None
    return out_lat, out_ctx

def n_layers_of(kind):
    return len(range(kind, DEPTH, N_MIXERS))

def second_inputs(seed: int = 0) -> dict:
    key = jax.random.key(seed)
    ks = jax.random.split(key, 32)
    f32 = jnp.float32

    def nrm(k, shape, scale):
        return jax.random.normal(k, shape, f32) * scale

    nA, nB, nC = n_layers_of(0), n_layers_of(1), n_layers_of(2)
    D, F = D_MODEL, D_FF
    H = SSD_N_HEADS
    dt0 = jnp.exp(jax.random.uniform(ks[12], (nA, 2, H), f32, math.log(1e-3), math.log(1e-1)))
    return {
        "x": nrm(ks[0], (BATCH, SEQ, D), 1.0),
        "c": nrm(ks[1], (BATCH, D), 1.0),
        "ctx": nrm(ks[2], (BATCH, CTX_LEN, D), 1.0),
        "c_ctx": nrm(ks[3], (D,), 1.0),
        "ada_w": nrm(ks[4], (DEPTH, D, N_MOD * D), 0.5 * D ** -0.5),
        "ada_b": nrm(ks[5], (DEPTH, N_MOD * D), 0.02),
        "norm_g": 1.0 + nrm(ks[6], (DEPTH, 3, D), 0.05),
        "ffn_w_gate": nrm(ks[7], (DEPTH, 2, D, F), D ** -0.5),
        "ffn_w_up": nrm(ks[8], (DEPTH, 2, D, F), D ** -0.5),
        "ffn_w_down": nrm(ks[9], (DEPTH, 2, F, D), F ** -0.5),
        "ssd_w_in": nrm(ks[10], (nA, D, SSD_IN_DIM), D ** -0.5),
        "ssd_conv_w": nrm(ks[11], (nA, SSD_CONV_W, SSD_CONV_DIM), SSD_CONV_W ** -0.5),
        "ssd_conv_b": nrm(ks[13], (nA, SSD_CONV_DIM), 0.02),
        "ssd_a_log": jnp.log(jax.random.uniform(ks[14], (nA, 2, H), f32, 1.0, 16.0)),
        "ssd_dt_bias": dt0 + jnp.log(-jnp.expm1(-dt0)),
        "ssd_d": 1.0 + nrm(ks[15], (nA, H), 0.1),
        "ssd_norm_g": 1.0 + nrm(ks[16], (nA, SSD_D_INNER), 0.05),
        "ssd_w_out": nrm(ks[17], (nA, SSD_D_INNER, D), SSD_D_INNER ** -0.5),
        "pool_w": nrm(ks[18], (nB, POOL_GROUPS, POOL_GROUP_DIM, POOL_GROUP_DIM), POOL_GROUP_DIM ** -0.5),
        "pool_b": nrm(ks[19], (nB, POOL_GROUPS, POOL_GROUP_DIM), 0.02),
        "pool_scale": 1.0 + nrm(ks[20], (nB, D), 0.1),
        "hy_w_in": nrm(ks[21], (nC, D, 3 * D), D ** -0.5),
        "hy_conv_w": nrm(ks[22], (nC, HY_SHORT_W, 3 * D), HY_SHORT_W ** -0.5),
        "hy_conv_b": nrm(ks[23], (nC, 3 * D), 0.02),
        "hy_filt_w1": nrm(ks[24], (nC, HY_EMB_DIM, HY_FILTER_HIDDEN), HY_EMB_DIM ** -0.5),
        "hy_filt_b1": nrm(ks[25], (nC, HY_FILTER_HIDDEN), 0.1),
        "hy_filt_w2": nrm(ks[26], (nC, HY_FILTER_HIDDEN, HY_FILTER_HIDDEN), HY_FILTER_HIDDEN ** -0.5),
        "hy_filt_b2": nrm(ks[27], (nC, HY_FILTER_HIDDEN), 0.1),
        "hy_filt_w3": nrm(ks[28], (nC, HY_FILTER_HIDDEN, HY_ORDER * 2 * D), HY_FILTER_HIDDEN ** -0.5),
        "hy_filt_freq": 1.0 + nrm(ks[29], (nC, 2, HY_FILTER_HIDDEN), 0.1),
        "hy_bias": nrm(ks[30], (nC, HY_ORDER, D), 0.1),
        "hy_w_out": nrm(ks[31], (nC, D, D), D ** -0.5),
        "final_g": 1.0 + nrm(jax.random.fold_in(key, 99), (D,), 0.05),
    }

def second_block(x, c, ctx, c_ctx, ada_w, ada_b, norm_g, ffn_w_gate, ffn_w_up, ffn_w_down,
              ssd_w_in, ssd_conv_w, ssd_conv_b, ssd_a_log, ssd_dt_bias, ssd_d, ssd_norm_g, ssd_w_out,
              pool_w, pool_b, pool_scale,
              hy_w_in, hy_conv_w, hy_conv_b, hy_filt_w1, hy_filt_b1, hy_filt_w2, hy_filt_b2, hy_filt_w3,
              hy_filt_freq, hy_bias, hy_w_out, final_g):
    h = ctx
    sc = jax.nn.silu(c)
    scc = jax.nn.silu(c_ctx)
    for i in range(DEPTH):
        kind = i % N_MIXERS
        j = i // N_MIXERS
        last = i == DEPTH - 1
        ctx_in_needed = (not last) or kind == 0
        m = (sc @ ada_w[i] + ada_b[i]).reshape(-1, N_MOD, D_MODEL)[:, :, None, :]
        mc = (scc @ ada_w[i] + ada_b[i]).reshape(N_MOD, D_MODEL)[:, None, None, :]

        x = x + 0.5 * m[:, 2] * swiglu_2(modulate_2(x, norm_g[i, 0], m[:, 0], m[:, 1]),
                                       ffn_w_gate[i, 0], ffn_w_up[i, 0], ffn_w_down[i, 0])
        if ctx_in_needed:
            h = h + 0.5 * mc[2] * swiglu_2(modulate_2(h, norm_g[i, 0], mc[0], mc[1]),
                                         ffn_w_gate[i, 0], ffn_w_up[i, 0], ffn_w_down[i, 0])

        u = modulate_2(x, norm_g[i, 1], m[:, 3], m[:, 4])
        uc = modulate_2(h, norm_g[i, 1], mc[3], mc[4]) if ctx_in_needed else None
        if kind == 0:
            y, yc = ssd_mixer(u, uc, ssd_w_in[j], ssd_conv_w[j], ssd_conv_b[j], ssd_a_log[j], ssd_dt_bias[j],
                              ssd_d[j], ssd_norm_g[j], ssd_w_out[j], not last)
        elif kind == 1:
            y, yc = pool_mixer(u, uc, pool_w[j], pool_b[j], pool_scale[j], not last)
        else:
            y, yc = hyena_mixer(u, uc, hy_w_in[j], hy_conv_w[j], hy_conv_b[j], hy_filt_w1[j], hy_filt_b1[j],
                                hy_filt_w2[j], hy_filt_b2[j], hy_filt_w3[j], hy_filt_freq[j], hy_bias[j],
                                hy_w_out[j], not last)
        x = x + m[:, 5] * y
        if not last:
            h = h + mc[5] * yc

        x = x + 0.5 * m[:, 8] * swiglu_2(modulate_2(x, norm_g[i, 2], m[:, 6], m[:, 7]),
                                       ffn_w_gate[i, 1], ffn_w_up[i, 1], ffn_w_down[i, 1])
        if not last:
            h = h + 0.5 * mc[8] * swiglu_2(modulate_2(h, norm_g[i, 2], mc[6], mc[7]),
                                         ffn_w_gate[i, 1], ffn_w_up[i, 1], ffn_w_down[i, 1])
    return rmsnorm(x, final_g)


def setup_inputs(seed=0):
    out = dict(first_inputs(seed))
    for name, value in second_inputs(seed + 1).items():
        if name != "x":
            out[name + "_2"] = value
    return out


def reference(
    x, c, positions, ada_w, ada_b, norm_ffn1, ffn1_w1, ffn1_w3, ffn1_w2, norm_mix, w_in,
    gdn_conv, gdn_a_log, gdn_dt_bias, gdn_out_gain, mla_q_lat_gain, mla_kv_lat_gain, mla_w_q_up,
    mla_w_kv_up, mla_q_norm, mla_k_norm, w_branch_a, w_branch_b, w_out, norm_ffn2, ffn2_w1,
    ffn2_w3, ffn2_w2, c_2, ctx_2, c_ctx_2, ada_w_2, ada_b_2, norm_g_2, ffn_w_gate_2, ffn_w_up_2,
    ffn_w_down_2, ssd_w_in_2, ssd_conv_w_2, ssd_conv_b_2, ssd_a_log_2, ssd_dt_bias_2, ssd_d_2,
    ssd_norm_g_2, ssd_w_out_2, pool_w_2, pool_b_2, pool_scale_2, hy_w_in_2, hy_conv_w_2,
    hy_conv_b_2, hy_filt_w1_2, hy_filt_b1_2, hy_filt_w2_2, hy_filt_b2_2, hy_filt_w3_2,
    hy_filt_freq_2, hy_bias_2, hy_w_out_2, final_g_2,
):
    x = first_block(
        x, c, positions, ada_w, ada_b, norm_ffn1, ffn1_w1, ffn1_w3, ffn1_w2, norm_mix, w_in,
        gdn_conv, gdn_a_log, gdn_dt_bias, gdn_out_gain, mla_q_lat_gain, mla_kv_lat_gain,
        mla_w_q_up, mla_w_kv_up, mla_q_norm, mla_k_norm, w_branch_a, w_branch_b, w_out,
        norm_ffn2, ffn2_w1, ffn2_w3, ffn2_w2,
    )
    return second_block(
        x, c_2, ctx_2, c_ctx_2, ada_w_2, ada_b_2, norm_g_2, ffn_w_gate_2, ffn_w_up_2,
        ffn_w_down_2, ssd_w_in_2, ssd_conv_w_2, ssd_conv_b_2, ssd_a_log_2, ssd_dt_bias_2,
        ssd_d_2, ssd_norm_g_2, ssd_w_out_2, pool_w_2, pool_b_2, pool_scale_2, hy_w_in_2,
        hy_conv_w_2, hy_conv_b_2, hy_filt_w1_2, hy_filt_b1_2, hy_filt_w2_2, hy_filt_b2_2,
        hy_filt_w3_2, hy_filt_freq_2, hy_bias_2, hy_w_out_2, final_g_2,
    )


_drawn_inputs = setup_inputs


def setup_inputs(seed=0):
    import zlib

    import numpy as np

    out = dict(_drawn_inputs(seed))
    spreads = {}
    factors = {'ada_b': 2.724,
     'mla_q_lat_gain': 8.0,
     'mla_kv_lat_gain': 4.514,
     'mla_q_norm': 8.0,
     'mla_k_norm': 8.0,
     'ctx_2': 3.927,
     'c_ctx_2': 3.368,
     'ssd_conv_b_2': 8.0,
     'ssd_d_2': 6.351,
     'ssd_norm_g_2': 13.66,
     'pool_b_2': 33.154,
     'pool_scale_2': 7.406}
    for name, (base, spread) in spreads.items():
        noise = np.random.default_rng([zlib.crc32(name.encode()), seed]).standard_normal(out[name].shape)
        drawn = base * np.exp(spread * noise) if base else spread * noise
        out[name] = __import__('jax').numpy.asarray(drawn.astype(out[name].dtype))
    for name, factor in factors.items():
        out[name] = (out[name] * factor).astype(out[name].dtype)
    return out
```

```python
import math
from contextlib import ExitStack

import numpy as np

import concourse.bass as bass
from concourse import mybir
from concourse.alu_op_type import AluOpType as ALU

ACT = mybir.ActivationFunctionType
F32, F32R, I32 = mybir.dt.float32, mybir.dt.float32r, mybir.dt.int32
AX = mybir.AxisListType

P = 128
T = 256
D = 1024
KD = D // P
FT = 2816 // P
EPS = 1e-6
N_MOD = 9
DEPTH = 2

RAW = 4
UNIT = 8
SLOTS = 4
ADA_SLOTS = 2

HEADS = 8
GROUP = 4
LEVELS = 6
NEG = -1.0e30
Q_TILES, K_TILES = 8, 8
LAT_Q, LAT_KV = 3, 2
ROPE = 64

CONST = {}
_at = 0
for _name, _n in (
    ("ident", P), ("ones", P), ("neg", 3 * P), ("first_t", 2 * P), ("masks", LEVELS * P), ("rot", P),
    ("attn", 3 * P), ("inv_freq", 1), ("row", 31), ("row_0", 31), ("row_1", 31), ("half_0", 1), ("half_1", 1),
):
    CONST[_name] = (_at, _n)
    _at += _n
N_CONST = _at

PAR1 = {}
_at = 0
for _name, _n in (
    ("ada_b", N_MOD * KD), ("gain", 3 * KD), ("conv", 24 * 4), ("out_gain", 1), ("lat_gain", 5),
    ("q_norm", 2), ("k_norm", 2), ("a_log", 1), ("dt_bias", 1),
):
    PAR1[_name] = (_at, _n)
    _at += _n
N_PAR1 = _at

PAR2 = {}
_at = 0
for _name, _n in (
    ("ada_b", N_MOD * KD), ("gain", 3 * KD), ("conv", 24 * 5), ("conv_b", 24), ("d_skip", 16), ("norm_g", 16),
    ("a_log", 1), ("dt_bias", 1), ("pool_b", KD), ("pool_scale", KD), ("final_g", KD),
):
    PAR2[_name] = (_at, _n)
    _at += _n
N_PAR2 = _at

WINDOWS = (2, 4, 8, 16)
GRID_W = 64


def constants():
    c = np.zeros((P, N_CONST), np.float32)
    i = np.arange(P)
    put = lambda name, a: c.__setitem__((slice(None), slice(CONST[name][0], sum(CONST[name]))), a)
    put("ident", np.eye(P))
    put("ones", 1.0)
    put("neg", np.concatenate([
        np.where(i[None, :] >= i[:, None], 0.0, NEG), np.zeros((P, P)), np.where(i[None, :] <= i[:, None], 0.0, NEG)], 1))
    pair = (i[None, :] // 2 == i[:, None] // 2) & (i[None, :] > i[:, None])
    put("first_t", np.tile(pair, (1, 2)))
    masks = []
    for level in range(LEVELS):
        s = 2 << level
        masks.append((i[:, None] // (2 * s) == i[None, :] // (2 * s)) & (i[:, None] // s > i[None, :] // s))
    put("masks", np.concatenate(masks, 1))
    rot = np.zeros((P, P))
    for b in (0, ROPE):
        for r in range(ROPE // 2):
            rot[b + ROPE // 2 + r, b + r] = -1.0
            rot[b + r, b + ROPE // 2 + r] = 1.0
    put("rot", rot)
    diag = np.where(i[None, :] <= i[:, None], 0.0, NEG)
    put("attn", np.concatenate([diag, np.zeros((P, P)), diag], 1))
    put("inv_freq", (np.float32(10000.0) ** (-np.arange(32, dtype=np.float32) / 32))[i % 32][:, None])
    c[:, CONST["row"][0] + 15] = 1.0
    for b in range(2):
        half = (i // ROPE == b).astype(np.float32)
        c[:, CONST[f"row_{b}"][0] + 15] = half
        put(f"half_{b}", half[:, None])
    return c


def window_means():
    def box(n, w):
        i = np.arange(n)
        lo, hi = np.maximum(i - w // 2, 0), np.minimum(i + w - w // 2, n)
        return ((i[:, None] >= lo) & (i[:, None] < hi)).astype(np.float64)

    out = []
    for w in WINDOWS:
        rows, cols = box(T // GRID_W, w), box(GRID_W, w)
        m = np.kron(rows / rows.sum(0), cols / cols.sum(0)) - np.eye(T)
        out.append(m.reshape(2, P, T))
    return np.stack(out).transpose(2, 1, 0, 3).astype(np.float32)




def tiles(w):
    k, m = w.shape
    return w.reshape(k // P, P, m // P, P).transpose(0, 2, 1, 3)


def by_tile(w):
    return tiles(w).transpose(1, 2, 0, 3)


def by_row(w):
    return tiles(w).transpose(0, 2, 1, 3)


def ffn_units(w1, w3, w2):
    up = np.stack([by_tile(w1), by_tile(w3)], 1).reshape(-1, P, UNIT, P)
    return [up, by_row(w2)]


def columns(v):
    return v.reshape(-1, P).T


def rows_at(*parts):
    c = np.zeros((P, 1), np.float32)
    for at, v in parts:
        c[at : at + v.shape[0], 0] = v
    return c


def first_mix_units(w_in, q_up, kv_up, branch_a, branch_b, w_out):
    at = np.cumsum([0, 3072, 1024, 8, 8, 384, 256, 64, 1024, 1024])
    part = [w_in[:, a:b] for a, b in zip(at[:-1], at[1:])]
    qkv, z, b_raw, a_raw, q_lat, kv_lat, k_pe, gate_a, gate_b = part
    pad = lambda n: np.zeros((D, n), np.float32)
    ba = np.concatenate([b_raw, pad(24), a_raw, pad(88)], 1)
    proj = np.concatenate([qkv, z, q_lat, kv_lat, k_pe, k_pe, ba, pad(P)], 1)
    out = [by_tile(proj)]
    q = q_up.reshape(384, HEADS, 192)
    q = np.concatenate([q[:, :, :P].reshape(384, -1), q[:, :, P:].reshape(384, -1)], 1)
    q = tiles(np.concatenate([q, np.zeros((P, q.shape[1]), np.float32)], 0))
    out.append(q.transpose(1, 0, 2, 3).reshape(6, 8, P, P).transpose(0, 2, 1, 3))
    kv = kv_up.reshape(256, HEADS, 256)
    k = tiles(kv[:, :, :P].reshape(256, -1)).transpose(1, 0, 2, 3).reshape(2, 8, P, P)
    out.append(k.transpose(0, 2, 1, 3))
    out.append(by_row(kv[:, :, P:].reshape(256, -1)))
    gates = np.stack([by_tile(gate_a), by_tile(branch_a), by_tile(gate_b), by_tile(branch_b)], 1)
    out += [gates.reshape(-1, P, UNIT, P), by_tile(w_out)]
    return out


def ssd_in_units(w_in, context):
    xbc = w_in[:, 2048:5120][:, : (20 if context else 24) * P]
    dt = np.concatenate([w_in[:, 5120:5184], np.zeros((D, (2 if context else 1) * P - 64), np.float32)], 1)
    return [by_tile(np.concatenate([xbc, dt], 1))]


def ssd_out_units(w_in, w_out):
    out = tiles(w_out).transpose(1, 0, 2, 3).reshape(KD * 2, UNIT, P, P).transpose(0, 2, 1, 3)
    return [by_tile(np.concatenate([w_in[:, :2048], np.zeros((D, P), np.float32)], 1)), out]


def pool_units(w):
    w = w.reshape(4, 2, P, 2, P).transpose(0, 3, 1, 2, 4)
    return [w.reshape(2, UNIT, P, P).transpose(0, 2, 1, 3)]


def ada_blocks(w):
    w = w.reshape(KD // 2, 2, P, N_MOD, D)
    return w.transpose(3, 0, 2, 1, 4).reshape(-1, P, 2 * D)




class Stage:

    def __init__(self, kind, block, layer, n=0, on_ctx=False, n_conv=0, vec=0, n_vec=0, n_prep=0,
                 gate_add=0.0, gate_scale=None, what=None):
        self.kind, self.block, self.layer = kind, block, layer
        self.n = n
        self.on_ctx = on_ctx
        self.n_conv = n_conv
        self.vec, self.n_vec, self.n_prep = vec, n_vec, n_prep
        self.gate_add, self.gate_scale = gate_add, gate_scale
        self.what = what

    def x(self, p):
        return p.ctx_x if self.on_ctx else p.x

    def par(self, p, name):
        if self.block == 1:
            at, n = PAR1[name]
            return p.par1[:, self.layer, at : at + n]
        at, n = PAR2[name]
        return p.par2[:, self.layer, at : at + n]

    def at(self, name):
        return self.base.get(name, 0)


UNITS = {"ffn": 2 * FT + FT, "project": 40, "up": 10, "gates": 40, "ssd_out": 33, "pool": 2}


def units_of(st):
    if st.kind == "ssd_in":
        return st.n_conv + (2 if st.on_ctx else 1)
    return UNITS.get(st.kind, 0)


def signals(st):
    kind = st.kind
    n = {}
    if kind == "ada":
        n = dict(ada_step=st.n_vec * KD, ada_cols=st.n_vec, mod_ready=st.n_vec, mod_prep=st.n_prep)
    if kind == "norm":
        n = dict(sq_ready=KD, sum_done=1, norm_step=2, rinv_ready=1, scaled=KD, h_rounded=KD, h_ready=KD)
    if kind == "ffn":
        n = dict(gate_act=FT, mid_step=2 * FT, mid_ready=FT, x_ready=KD)
    if kind == "project":
        n = dict(proj_out=40, conv_step=3 * 24, conv_done=24, act_done=24, sq_done=16, sums_done=16,
                 inv_step=16, inv_ready=16, unit_len=2, normed=16, conv_pad=4)
        n["proj_out"] = 39
    if kind == "gdn":
        n = dict(gdn_step=28, rows_ready=2, cols_ready=2, gate_fn=5, exp_cum=1, cols_done=1, rows_done=8,
                 kb_ready=8, exponent_ready=16, row_exp=8, decay_ready=8, pairs_done=8, pairs_used=16,
                 q_dec_ready=8, inv_grown=8 * (LEVELS + 1), turned_done=8, turned_used=8, first_turned=8,
                 first_both=8, lp_done=8 * LEVELS, lq_done=8 * LEVELS, new_ready=8 * LEVELS, wu_done=8,
                 w_ready=8, v0_ready=8, state_done=8, state_ready=8, v1_done=8, v1_ready=8, o_done=8,
                 out_ready=8, o_sum=8, o_inv=8, o_sq=8, o_root=1, oa_ready=8)
    if kind == "up":
        n = dict(lat_sq=5, kpe_sq=1, up_out=20, up_summed=20, up_sq=20, lat_sum=2, lat_ready=5, lat_var=4,
                 lat_root=2, lat_scaled=5, lat_rounded=5, rope_in=5, rope_out=5, rope_step=10, rope_turned=5,
                 rinv_rows=1, values_out=4, head_normed=16, head_rinv=16, head_var=2)
    if kind == "attn":
        n = dict(masked=8, scored=8, weighed=8, weights_out=8, weights_turned=8, ob_out=8, mixed=8,
                 max_step=16, max_ready=8, exped=8, den_ready=8)
    if kind == "gates":
        n = dict(gate_tanh=16, y_step=16, o_split=2, o_rounded=2, y_split=2, y_rounded=2, y_ready=8, x_ready=8)
    if kind == "ssd_in":
        k = st.n_conv
        n = dict(proj_out=k + 1, conv_step=4 * k, conv_done=k, act_done=k, conv_pad=4,
                 gate_fn=5 if st.on_ctx else 4, dt_step=6 if st.on_ctx else 5, dt_ready=1)
    if kind == "state":
        n = dict(sturned=10, sturn_out=10, cols_done=1, cols_ready=1, xw_ready=4, state_sum=8, state_out=8)
    if kind == "mix":
        n = dict(sturned=8, sturn_out=8, cols_done=1, cols_ready=1, cb_done=4, cb_out=4, g_row=64, sx_ready=64,
                 sx_exp=64, g_exp=64, c_dec=64, sw_ready=64, sy_part=64, sy_out=16)
    if kind == "ssd_out":
        n = dict(gate_act=16, sz_gated=16, sz_sq=16, sz_summed=16, sz_var=2, sz_root=1, sz_rinv=4, gy_scaled=16,
                 gy_rounded=16, gy_split=16, x_ready=8)
    if kind == "pool":
        n = dict(h_whole=1, sturned=4, sturn_out=4, pooled=8, pool_rounded=8, pool_split=8, pool_out=6,
                 pool_factor=1, pool_step=8, x_ready=8)
    if kind == "final":
        n = dict(sq_ready=8, sum_done=1, norm_step=2, rinv_ready=1, y_normed=8)
    return n


def plan_of(stages):
    base, unit, block = {}, 0, 0
    for st in stages:
        st.base = dict(base)
        st.unit0 = unit
        st.block0 = block
        block += KD // 2 * st.n_vec if st.kind == "ada" else 0
        unit += units_of(st)
        for name, k in signals(st).items():
            base[name] = base.get(name, 0) + k
    return unit, block, base


class Program:

    def __init__(self, nc, ctx, stages, dram):
        self.nc, self.stages, self.dram = nc, stages, dram
        self.n_units, self.n_ada, self.total = plan_of(stages)
        self.n_blocks = self.n_units // 2
        self.ctx = ctx
        sb = lambda name, shape, dt=F32: ctx.enter_context(nc.sbuf_tensor(name, shape, dt))
        self.raw = sb("raw", [P, RAW, 2, UNIT * P])
        self.w_hi = sb("w_hi", [P, SLOTS, UNIT, P], F32R)
        self.w_lo = sb("w_lo", [P, SLOTS, UNIT, P], F32R)
        self.ada_w = sb("ada_w", [P, ADA_SLOTS, 2, D])
        self.x = sb("x", [P, KD, T])
        self.h_hi = sb("h_hi", [P, KD, T], F32R)
        self.h_lo = sb("h_lo", [P, KD, T], F32R)
        self.tmp = sb("tmp", [P, KD, T])
        self.ada_acc = self.tmp[:, 0:4].rearrange("p m n -> p (m n)")
        self.rinv = sb("rinv", [P, T])
        self.var = sb("var", [P, T])
        self.const = sb("const", [P, N_CONST])
        self.par1 = sb("par1", [P, DEPTH, N_PAR1])
        self.par2 = sb("par2", [P, DEPTH, N_PAR2])
        self.scols = sb("scols", [P, 2, 2, 64])
        self.c_in = sb("c_in", [P, 4, KD])
        self.c_act = sb("c_act", [P, 4, KD])
        self.mod = sb("mod", [P, N_MOD, KD])
        self.mod_a = sb("mod_a", [P, 3, KD])
        self.mod_g = sb("mod_g", [P, 3, KD])
        self.positions = sb("positions", [P, T], I32)
        self.cos = sb("cos", [P, T])
        self.sin = sb("sin", [P, T])
        self.rows = sb("rows", [P, T])
        self.rows2 = self.rinv
        self.soft = sb("soft", [P, T])
        self.exp_a = sb("exp_a", [P, 1])
        self.cols = sb("cols", [P, 2, 2, HEADS])
        self.exp_cols = sb("exp_cols", [P, HEADS])
        self.beta_exp = sb("beta_exp", [P, HEADS])
        self.mx, self.nmx, self.den, self.rden = (sb(n, [P, 2, 2]) for n in ("mx", "nmx", "den", "rden"))
        self.u_hi = self.over("u_hi", 0, [P, FT, T], F32R)
        self.u_lo = self.over("u_lo", 22528, [P, FT, T], F32R)
        self.mid = self.over("mid", 45056, [P, 2, T])
        self.gate = self.over("gate", 47104, [P, 2, T])
        self.qkv = self.over("qkv", 0, [P, 24, T])
        self.z = self.over("z", 24576, [P, HEADS, T])
        self.lat = self.over("lat", 32768, [P, 7, T])
        self.conv_in = self.over("conv_in", 39936, [P, 4, 264])
        self.inv = self.over("inv", 44160, [P, 16, T])
        self.kb = self.over("kb", 44160, [P, GROUP, T])
        self.decay = self.over("decay", 48256, [P, GROUP, T])
        self.exp_row = self.over("exp_row", 52352, [P, GROUP, P])
        self.a_t = self.over("a_t", 54400, [P, GROUP, T])
        self.qk_t = self.over("qk_t", 58496, [P, GROUP, T])
        self.v_beta = self.over("v_beta", 62592, [P, GROUP, T])
        self.k_tok = self.over("k_tok", 66688, [P, GROUP, T])
        self.w_s = self.over("w_s", 70784, [P, GROUP, T])
        self.lat_hi = self.over("lat_hi", 8192, [P, 5, T], F32R)
        self.lat_lo = self.over("lat_lo", 13312, [P, 5, T], F32R)
        self.lat_sq = self.over("lat_sq", 18432, [P, 5, T])
        self.pt = self.over("pt", 18432, [P, 2, 3 * P])
        self.kn = self.over("kn", 24576, [P, HEADS, T])
        self.qn = self.over("qn", 39936, [P, HEADS, T])
        self.qr = self.over("qr", 48128, [P, HEADS // 2, T])
        self.vt = self.over("vt", 52224, [P, 2, D])
        self.krz = self.over("krz", 60416, [P, HEADS, T])
        self.kr = self.over("kr", 68608, [P, T])
        self.work = self.over("work", 69632, [P, 2, T])
        self.rinv_lat = self.work
        self.rinv16 = self.soft
        self.sm = self.over("sm", 71680, [P, 2, 3 * P])
        self.o_lo = self.over("o_lo", 8192, [P, 16, T], F32R)
        self.o_hi = self.over("o_hi", 48128, [P, 16, T], F32R)
        self.y = self.over("y", 24576, [P, KD, T])
        self.gate_t = self.over("gate_t", 64512, [P, 2, T])
        self.ctx_x = self.over("ctx_x", 49152, [P, KD, T])
        self.xl = self.over("xl", 0, [P, 16, T])
        self.x_tok = self.over("x_tok", 16384, [P, 2, 2048])
        self.sconv_in = self.over("sconv_in", 32768, [P, 4, 264])
        self.bc = self.over("bc", 40960, [P, 8, T])
        self.b_tok = self.over("b_tok", 45056, [P, 2, 512])
        self.xw = self.over("xw", 0, [P, 2, 2048])
        self.state = self.over("state", 49152, [P, 2, 2048])
        self.cbt = self.over("cbt", 32768, [P, 4, 2, T])
        self.g_exp = self.over("g_exp", 40960, [P, 2, T])
        self.c_exp = self.over("c_exp", 43008, [P, 2, T])
        self.sw = self.over("sw", 65536, [P, 3, 3 * P])
        self.gy_hi = self.over("gy_hi", 16384, [P, 16, T], F32R)
        self.gy_lo = self.over("gy_lo", 32768, [P, 16, T], F32R)
        self.sz = self.over("sz", 65536, [P, 2, T])
        self.means = self.over("means", 49152, [P, 2, 4, T])
        self.h_f32 = self.tmp
        self.h_tok = self.over("h_tok", 0, [P, 2, D])
        self.p_hi = self.over("p_hi", 32768, [P, KD, T], F32R)
        self.p_lo = self.over("p_lo", 40960, [P, KD, T], F32R)
        self.angle = self.over("angle", 0, [P, T])
        self.inv_t = self.tmp[:].rearrange("p (i b) n -> p i b n", b=2)
        self.psum = ctx.enter_context(nc.psum_tensor("psum", [P, 8, 512], F32))
        self.sem = {}
        for name in (
            ["loaded", "stored", "c_ready", "trig_step", "angles_ready", "trig_done", "rows_cleared", "hi_ready", "lo_ready", "unit_done", "ctx_loaded", "means_loaded"]
            + [f"raw_full_{s}" for s in range(RAW)]
            + [f"ada_full_{s}" for s in range(ADA_SLOTS)]
            + sorted({n for st in stages for n in signals(st)})
        ):
            self.sem[name] = ctx.enter_context(nc.semaphore(name))

    def over(self, name, offset, shape, dt=F32):
        if not offset:
            with self.nc.sbuf_tensor(name, shape, dt) as t:
                return t
        with self.nc.sbuf_tensor(name + "_before", [P, offset // 4], F32):
            with self.nc.sbuf_tensor(name, shape, dt) as t:
                return t

    def c(self, name):
        at, n = CONST[name]
        return self.const[:, at : at + n]

    def pick(self, name, t):
        at = CONST[name][0]
        return self.const[:, at + 15 - t : at + 31 - t]

    def sxbc(self, t):
        return self.xl[:, t] if t < 16 else self.bc[:, t - 16]

    def up_tile(self, j):
        if j < 8:
            return self.qn[:, j]
        return self.qr[:, j - 8] if j < 12 else self.kn[:, j - 12]


def groups(eng, n, per, body):
    whole = n // per
    for c in range(per):
        body(0, c)
    if whole > 1:
        with eng.Fori(1, whole) as g:
            for c in range(per):
                body(g, c)
    for c in range(n - whole * per):
        body(whole, c)




def split_hi(p, act, s, g=0):
    if isinstance(g, int):
        s, g = s + 8 * g, 0
        if s >= p.n_units:
            return
    slot, turn = (s // 2) % RAW, (s // 2) // RAW
    act.wait_ge(p.sem[f"raw_full_{slot}"], g * 16 + (turn + 1) * 16)
    if not isinstance(g, int) or s >= SLOTS:
        act.wait_ge(p.sem["unit_done"], g * 8 + (s - SLOTS + 1))
    p.nc.scalar.activation(
        p.w_hi[:, s % SLOTS].rearrange("p k m -> p (k m)"), p.raw[:, slot, s % 2], ACT.Copy
    ).then_inc(p.sem["hi_ready"], 1)


def split_lo(p, dve, s, g=0):
    if isinstance(g, int):
        s, g = s + 8 * g, 0
        if s >= p.n_units:
            return
    slot = (s // 2) % RAW
    dve.wait_ge(p.sem["hi_ready"], g * 8 + (s + 1))
    p.nc.vector.tensor_tensor(
        p.w_lo[:, s % SLOTS].rearrange("p k m -> p (k m)"), p.raw[:, slot, s % 2],
        p.w_hi[:, s % SLOTS].rearrange("p k m -> p (k m)").bitcast(F32), ALU.subtract,
    ).then_inc(p.sem["lo_ready"], 1)


def load_units(p, sp):
    w = p.dram["stream"]

    def load(g, c):
        if not isinstance(g, int) or g > 0:
            sp.wait_ge(p.sem["lo_ready"], g * (2 * RAW) + 2 * (c - RAW + 1))
        sp.dma_start(
            p.raw[:, c].rearrange("p h n -> p (h n)"), w[g * RAW + c]
        ).then_inc(p.sem[f"raw_full_{c}"], 16)

    for c in range(RAW):
        load(0, c)
    turns = p.n_blocks // RAW
    with sp.Fori(1, turns) as g:
        for c in range(RAW):
            load(g, c)
    for c in range(p.n_blocks - turns * RAW):
        load(turns, c)


def ada_gpsimd(p, pool, st):
    w, first = p.dram["ada"], st.block0

    def load(g, c):
        if not isinstance(g, int) or first:
            pool.wait_ge(p.sem["ada_step"], g * (2 * ADA_SLOTS) + 2 * (first + c - ADA_SLOTS + 1))
        pool.dma_start(
            p.ada_w[:, c].rearrange("p k n -> p (k n)"), w[g * ADA_SLOTS + (first + c)]
        ).then_inc(p.sem[f"ada_full_{c}"], 16)

    for c in range(ADA_SLOTS):
        load(0, c)
    with pool.Fori(1, st.n_vec * KD // 2 // ADA_SLOTS) as g:
        for c in range(ADA_SLOTS):
            load(g, c)


def three_pass(p, out, slot, k, hi, lo, start, stop, skip=False):
    mm = p.nc.tensor.matmul
    mm(out, p.w_hi[:, slot, k], hi, start=start, stop=False, skip_group_check=skip)
    mm(out, p.w_lo[:, slot, k], hi, start=False, stop=False, skip_group_check=skip)
    return mm(out, p.w_hi[:, slot, k], lo, start=False, stop=stop, skip_group_check=skip)




def ada_vector(p, dve, st):
    nc, a = p.nc, st.at
    for j in range(st.n_vec):
        ada_one(p, dve, st, j)
    g, mod, gain = st.gate_scale, p.mod, st.par(p, "gain").rearrange("p (n m) -> p n m", m=KD)
    for n in range(st.n_vec // 3 if st.n_vec != 5 else 2):
        dve.wait_ge(p.sem["mod_ready"], a("mod_ready") + 3 * n + 2)
        nc.vector.scalar_tensor_tensor(
            p.mod_a[:, n], mod[:, 3 * n + 1], 1.0, gain[:, n], ALU.add, ALU.mult
        ).then_inc(p.sem["mod_prep"], 1)
        if 3 * n + 2 < st.n_vec:
            dve.wait_ge(p.sem["mod_ready"], a("mod_ready") + 3 * n + 3)
            nc.vector.tensor_scalar(
                p.mod_g[:, n], mod[:, 3 * n + 2], st.gate_add, g[n], ALU.add, ALU.mult
            ).then_inc(p.sem["mod_prep"], 1)
    dve.wait_ge(p.sem["mod_prep"], a("mod_prep") + st.n_prep)


def ada_one(p, dve, st, j):
    nc, a = p.nc, st.at
    for k in range(KD):
        slot = (k // 2) % ADA_SLOTS
        turn = (st.block0 + 4 * j + k // 2) // ADA_SLOTS
        if k % 2 == 0:
            dve.wait_ge(p.sem[f"ada_full_{slot}"], (turn + 1) * 16)
        w, scalar = p.ada_w[:, slot, k % 2], p.c_act[:, st.vec, k : k + 1]
        step = a("ada_step") + j * KD + k
        if k == 0:
            dve.wait_ge(p.sem["ada_cols"], a("ada_cols") + j)
            dve.wait_ge(p.sem["c_ready"], 1)
            ins = nc.vector.tensor_scalar(p.ada_acc[:], w, scalar, None, ALU.mult)
        else:
            dve.wait_ge(p.sem["ada_step"], step)
            ins = nc.vector.scalar_tensor_tensor(p.ada_acc[:], w, scalar, p.ada_acc[:], ALU.mult, ALU.add)
        ins.then_inc(p.sem["ada_step"], 1)
    dve.wait_ge(p.sem["ada_cols"], a("ada_cols") + j + 1)
    nc.vector.tensor_tensor(
        p.mod[:, j], p.psum[:, 3, 0:KD], st.par(p, "ada_b")[:, j * KD : j * KD + KD], ALU.add
    ).then_inc(p.sem["mod_ready"], 1)


def ada_tensor(p, pe, st):
    nc, a = p.nc, st.at
    ones = p.c("ones")
    for j in range(st.n_vec):
        pe.wait_ge(p.sem["ada_step"], a("ada_step") + (j + 1) * KD)
        if a("mod_ready") + j:
            pe.wait_ge(p.sem["mod_ready"], a("mod_ready") + j)
        for m in range(KD):
            ins = nc.tensor.matmul(
                p.psum[:, 3, m : m + 1], p.ada_acc[:, m * P : m * P + P], ones[:, 0:1], start=True, stop=True
            )
        ins.then_inc(p.sem["ada_cols"], 1)




def norm_scalar(p, act, st):
    nc, a, x = p.nc, st.at, st.x(p)
    act.wait_ge(p.sem["ada_cols"], a("ada_cols"))
    if st.on_ctx:
        act.wait_ge(p.sem["ctx_loaded"], 16)
    for m in range(KD):
        if a("x_ready"):
            act.wait_ge(p.sem["x_ready"], a("x_ready") - KD + m + 1)
        nc.scalar.activation(p.tmp[:, m], x[:, m], ACT.Square).then_inc(p.sem["sq_ready"], 1)
    act.wait_ge(p.sem["norm_step"], a("norm_step") + 2)
    nc.scalar.activation(p.rinv[:], p.var[:], ACT.Sqrt).then_inc(p.sem["rinv_ready"], 1)
    for m in range(KD):
        act.wait_ge(p.sem["scaled"], a("scaled") + m + 1)
        nc.scalar.activation(
            p.h_hi[:, m], p.tmp[:, m], ACT.Identity, bias=p.mod[:, 3 * st.n, m : m + 1]
        ).then_inc(p.sem["h_rounded"], 1)


def norm_tensor(p, pe, st):
    a = st.at
    for m in range(KD):
        pe.wait_ge(p.sem["sq_ready"], a("sq_ready") + m + 1)
        ins = p.nc.tensor.matmul(p.psum[:, 2, 0:T], p.c("ones"), p.tmp[:, m], start=m == 0, stop=m == KD - 1)
    ins.then_inc(p.sem["sum_done"], 1)


def norm_vector(p, dve, st):
    nc, a, x = p.nc, st.at, st.x(p)
    if st.on_ctx:
        dve.wait_ge(p.sem["ctx_loaded"], 16)
    if st.unit0:
        dve.wait_ge(p.sem["unit_done"], st.unit0)
    dve.wait_ge(p.sem["sum_done"], a("sum_done") + 1)
    nc.vector.tensor_scalar(p.var[:], p.psum[:, 2, 0:T], 1.0 / D, EPS, ALU.mult, ALU.add).then_inc(p.sem["norm_step"], 1)
    dve.wait_ge(p.sem["norm_step"], a("norm_step") + 1)
    nc.vector.reciprocal(p.var[:], p.var[:]).then_inc(p.sem["norm_step"], 1)
    dve.wait_ge(p.sem["rinv_ready"], a("rinv_ready") + 1)
    for m in range(KD):
        nc.vector.scalar_tensor_tensor(
            p.tmp[:, m], x[:, m], p.mod_a[:, st.n, m : m + 1], p.rinv[:], ALU.mult, ALU.mult
        ).then_inc(p.sem["scaled"], 1)
        if m:
            norm_lo(p, dve, st, m - 1)
    norm_lo(p, dve, st, KD - 1)


def norm_lo(p, dve, st, m):
    dve.wait_ge(p.sem["h_rounded"], st.at("h_rounded") + m + 1)
    p.nc.vector.scalar_tensor_tensor(
        p.h_lo[:, m], p.tmp[:, m], p.mod[:, 3 * st.n, m : m + 1], p.h_hi[:, m].bitcast(F32), ALU.add, ALU.subtract
    ).then_inc(p.sem["h_ready"], 1)




def ffn_tensor(p, pe, st):
    a, u0 = st.at, st.unit0

    def up(g, c):
        for b in range(2):
            s = u0 + 2 * c + b
            if b == 0 and (not isinstance(g, int) or g * 4 + c >= 2):
                pe.wait_ge(p.sem["mid_ready"], g * 4 + (a("mid_ready") + c - 1))
            pe.wait_ge(p.sem["lo_ready"], g * 8 + (s + 1))
            for k in range(UNIT):
                if isinstance(g, int) and g == 0 and c == 0 and b == 0:
                    pe.wait_ge(p.sem["h_ready"], a("h_ready") - KD + k + 1)
                ins = three_pass(p, p.psum[:, c % 2, b * T : b * T + T], s % SLOTS, k,
                                 p.h_hi[:, k], p.h_lo[:, k], k == 0, k == UNIT - 1)
            ins.then_inc(p.sem["unit_done"], 1)

    for c in range(4):
        up(0, c)
    with pe.Fori(1, FT // 4) as g:
        for c in range(4):
            up(g, c)
    for c in range(FT % 4):
        up(FT // 4, c)

    def down(g, c, first, last):
        for b in range(2):
            s = u0 + 2 * FT + 2 * c + b
            k = g * 8 + (2 * c + b)
            pe.wait_ge(p.sem["mid_ready"], k + (a("mid_ready") + 1))
            pe.wait_ge(p.sem["lo_ready"], g * 8 + (s + 1))
            for m in range(KD):
                new = first and b == 0 and m % 2 == 0
                ins = three_pass(p, p.psum[:, 4 + m // 2, m % 2 * T : m % 2 * T + T], s % SLOTS, m,
                                 p.u_hi[:, k], p.u_lo[:, k], new, last and b == 1, skip=True)
            ins.then_inc(p.sem["unit_done"], 1)

    down(0, 0, True, False)
    with pe.Fori(0, 2) as g:
        for c in range(1, 5):
            down(g, c, False, False)
    down(0, 9, False, False)
    down(0, 10, False, True)


def ffn_scalar(p, act, st):
    a, u0, nc = st.at, st.unit0, p.nc

    def up(g, c):
        split_hi(p, act, u0 + 2 * c + 2, g)
        split_hi(p, act, u0 + 2 * c + 3, g)
        act.wait_ge(p.sem["unit_done"], g * 8 + (u0 + 2 * c + 2))
        if not isinstance(g, int) or g * 4 + c >= 2:
            act.wait_ge(p.sem["mid_step"], g * 8 + (a("mid_step") + 2 * c - 3))
        nc.scalar.activation(p.gate[:, c % 2], p.psum[:, c % 2, 0:T], ACT.Silu).then_inc(p.sem["gate_act"], 1)

    groups(act, FT, 4, up)
    for s in range(2):
        split_hi(p, act, u0 + 2 * FT + 2 + s)

    def down(g, c):
        split_hi(p, act, u0 + 2 * FT + 4 + 2 * c, g)
        split_hi(p, act, u0 + 2 * FT + 5 + 2 * c, g)

    groups(act, FT // 2 - 1, 4, down)


def ffn_vector(p, dve, st):
    a, u0, nc, x = st.at, st.unit0, p.nc, st.x(p)

    def up(g, c):
        t = g * 4 + c
        split_lo(p, dve, u0 + 2 * c + 2, g)
        dve.wait_ge(p.sem["gate_act"], t + (a("gate_act") + 1))
        dve.wait_ge(p.sem["unit_done"], g * 8 + (u0 + 2 * c + 2))
        if not isinstance(g, int) or g * 4 + c >= 2:
            dve.wait_ge(p.sem["mid_ready"], t + (a("mid_ready") - 1))
        nc.vector.tensor_tensor(
            p.mid[:, c % 2], p.gate[:, c % 2], p.psum[:, c % 2, T : 2 * T], ALU.mult
        ).then_inc(p.sem["mid_step"], 1)
        split_lo(p, dve, u0 + 2 * c + 3, g)
        dve.wait_ge(p.sem["mid_step"], g * 8 + (a("mid_step") + 2 * c + 1))
        nc.vector.tensor_scalar(p.u_hi[:, t], p.mid[:, c % 2], 1.0, None, ALU.mult).then_inc(p.sem["mid_step"], 1)
        dve.wait_ge(p.sem["mid_step"], g * 8 + (a("mid_step") + 2 * c + 2))
        nc.vector.tensor_tensor(
            p.u_lo[:, t], p.mid[:, c % 2], p.u_hi[:, t].bitcast(F32), ALU.subtract
        ).then_inc(p.sem["mid_ready"], 1)

    groups(dve, FT, 4, up)
    for s in range(2):
        split_lo(p, dve, u0 + 2 * FT + 2 + s)

    def down(g, c):
        split_lo(p, dve, u0 + 2 * FT + 4 + 2 * c, g)
        split_lo(p, dve, u0 + 2 * FT + 5 + 2 * c, g)

    groups(dve, FT // 2 - 1, 4, down)
    dve.wait_ge(p.sem["unit_done"], u0 + 3 * FT)
    for m in range(KD):
        nc.vector.scalar_tensor_tensor(
            x[:, m], p.psum[:, 4 + m // 2, m % 2 * T : m % 2 * T + T], p.mod_g[:, st.n, m : m + 1], x[:, m],
            ALU.mult, ALU.add,
        ).then_inc(p.sem["x_ready"], 1)



PROJ_BANKS = (0, 1, 4, 5)


def project_tensor(p, pe, st):
    a, u0, nc = st.at, st.unit0, p.nc

    def one(g, c):
        if not isinstance(g, int) or 8 * g + c >= 4:
            pe.wait_ge(p.sem["proj_out"], g * 8 + (a("proj_out") + c - 3))
        pe.wait_ge(p.sem["lo_ready"], g * 8 + (u0 + c + 1))
        for k in range(UNIT):
            if isinstance(g, int) and g == 0 and c == 0:
                pe.wait_ge(p.sem["h_ready"], a("h_ready") - KD + k + 1)
            ins = three_pass(p, p.psum[:, PROJ_BANKS[c % 4], 0:T], (u0 + c) % SLOTS, k,
                             p.h_hi[:, k], p.h_lo[:, k], k == 0, k == UNIT - 1)
        ins.then_inc(p.sem["unit_done"], 1)

    for c in range(8):
        one(0, c)
    with pe.Fori(1, 5) as g:
        for c in range(8):
            one(g, c)

    def total(g, c):
        t = g * 4 + c
        pe.wait_ge(p.sem["sq_done"], t + (a("sq_done") + 1))
        if not isinstance(g, int) or t >= 2:
            pe.wait_ge(p.sem["inv_step"], t + (a("inv_step") - 1))
        nc.tensor.matmul(p.psum[:, 6 + c % 2, 0:T], p.c("ones"), p.inv[:, t], start=True, stop=True).then_inc(
            p.sem["sums_done"], 1)

    groups(pe, 16, 4, total)


def project_scalar(p, act, st):
    a, u0, nc = st.at, st.unit0, p.nc

    def head(g, c):
        split_hi(p, act, u0 + c + 2, g)
        act.wait_ge(p.sem["unit_done"], g * 8 + (u0 + c + 1))
        if not isinstance(g, int) or 8 * g + c >= 4:
            act.wait_ge(p.sem["conv_done"], g * 8 + (a("conv_done") + c - 3))
        nc.scalar.activation(p.conv_in[:, c % 4, 3 : 3 + T], p.psum[:, PROJ_BANKS[c % 4], 0:T], ACT.Copy).then_inc(
            p.sem["proj_out"], 1)
        if not isinstance(g, int) or 8 * g + c >= 1:
            silu(g, c - 1)

    def silu(g, c):
        act.wait_ge(p.sem["conv_done"], g * 8 + (a("conv_done") + c + 1))
        act.wait_ge(p.sem["loaded"], p.n_loads)
        t = g * 8 + c
        nc.scalar.activation(p.qkv[:, t], p.qkv[:, t], ACT.Silu).then_inc(p.sem["act_done"], 1)

    for c in range(8):
        head(0, c)
    with act.Fori(1, 3) as g:
        for c in range(8):
            head(g, c)
    for t in range(24, 39):
        split_hi(p, act, u0 + t + 2)
        if t == 24:
            silu(0, 23)
        act.wait_ge(p.sem["unit_done"], u0 + t + 1)
        out, func = (p.z[:, t - 24], ACT.Silu) if t < 32 else (p.lat[:, t - 32], ACT.Copy)
        nc.scalar.activation(out, p.psum[:, PROJ_BANKS[t % 4], 0:T], func).then_inc(p.sem["proj_out"], 1)
    split_hi(p, act, u0 + 41)
    act.wait_ge(p.sem["inv_ready"], a("inv_ready") + 16)
    for i in range(2):
        part = p.inv[:, 8 * i : 8 * i + 8]
        nc.scalar.activation(part, part, ACT.Sqrt, scale=(1.0 / P, 1.0)[i]).then_inc(p.sem["unit_len"], 1)


def project_gpsimd(p, pool, st):
    a, nc = st.at, p.nc

    def one(g, c):
        t = g * 4 + c
        pool.wait_ge(p.sem["act_done"], t + (a("act_done") + 1))
        nc.gpsimd.tensor_tensor(p.inv[:, t], p.qkv[:, t], p.qkv[:, t], ALU.mult).then_inc(p.sem["sq_done"], 1)

    if st.unit0:
        pool.wait_ge(p.sem["unit_done"], st.unit0)
    for s in range(4):
        nc.gpsimd.memset(p.conv_in[:, s, 0:3], 0.0).then_inc(p.sem["conv_pad"], 1)
    groups(pool, 16, 4, one)


def project_vector(p, dve, st):
    a, u0, nc = st.at, st.unit0, p.nc
    w = st.par(p, "conv").rearrange("p (t j) -> p t j", j=4)
    dve.wait_ge(p.sem["conv_pad"], a("conv_pad") + 4)

    def conv(g, c):
        t = g * 8 + c
        split_lo(p, dve, u0 + c + 2, g)
        dve.wait_ge(p.sem["proj_out"], g * 8 + (a("proj_out") + c + 1))
        out, src = p.qkv[:, t], p.conv_in[:, c % 4]
        nc.vector.tensor_scalar(out, src[:, 0:T], w[:, t, 0:1], None, ALU.mult).then_inc(p.sem["conv_step"], 1)
        for j in range(1, 4):
            dve.wait_ge(p.sem["conv_step"], g * 24 + (a("conv_step") + 3 * c + j))
            nc.vector.scalar_tensor_tensor(
                out, src[:, j : j + T], w[:, t, j : j + 1], out, ALU.mult, ALU.add
            ).then_inc(p.sem["conv_step" if j < 3 else "conv_done"], 1)

    groups(dve, 24, 8, conv)
    for t in range(24, 40):
        split_lo(p, dve, u0 + t + 2)

    def invert(g, c):
        t = g * 4 + c
        dve.wait_ge(p.sem["sums_done"], t + (a("sums_done") + 1))
        nc.vector.tensor_scalar(p.inv[:, t], p.psum[:, 6 + c % 2, 0:T], 1.0, EPS, ALU.mult, ALU.add).then_inc(
            p.sem["inv_step"], 1)
        dve.wait_ge(p.sem["inv_step"], t + (a("inv_step") + 1))
        nc.vector.reciprocal(p.inv[:, t], p.inv[:, t]).then_inc(p.sem["inv_ready"], 1)

    for t in range(16):
        invert(t // 4, t % 4)

    def scale(g, c):
        t = g * 4 + c
        dve.wait_ge(p.sem["act_done"], a("act_done") + 24)
        nc.vector.tensor_tensor(p.qkv[:, t], p.qkv[:, t], p.inv[:, t], ALU.mult).then_inc(p.sem["normed"], 1)

    dve.wait_ge(p.sem["unit_len"], a("unit_len") + 2)
    groups(dve, 16, 4, scale)




GROWN = GROUP * (LEVELS + 1)


def gdn_vector(p, dve, st):
    a, nc, v = st.at, p.nc, p.nc.vector
    step = a("gdn_step")

    def link(ins):
        nonlocal step
        step += 1
        ins.then_inc(p.sem["gdn_step"], 1)
        dve.wait_ge(p.sem["gdn_step"], step)

    beta, raw_g, cum = p.rows[0:HEADS], p.rows2[32 : 32 + HEADS], p.rows[32 : 32 + HEADS]
    dt_bias = st.par(p, "dt_bias")[32 : 32 + HEADS]
    dve.wait_ge(p.sem["gate_fn"], a("gate_fn") + 1)
    link(v.tensor_scalar(beta, beta, 0.5, 0.5, ALU.mult, ALU.add))
    dve.wait_ge(p.sem["gate_fn"], a("gate_fn") + 5)
    link(v.tensor_scalar(raw_g, p.lat[32 : 32 + HEADS, 6], dt_bias, 0.0, ALU.add, ALU.max))
    link(v.tensor_tensor(raw_g, raw_g, p.soft[32 : 32 + HEADS], ALU.add))
    link(v.tensor_scalar(raw_g, raw_g, p.exp_a[32 : 32 + HEADS], -1.0, ALU.mult, ALU.mult))
    for c in range(2):
        part = slice(c * P, c * P + P)
        v.tensor_tensor_scan(
            cum[:, part], p.c("ones")[32 : 32 + HEADS], raw_g[:, part], 0.0, ALU.mult, ALU.add
        ).then_inc(p.sem["rows_ready"], 1)
    dve.wait_ge(p.sem["cols_done"], a("cols_done") + 1)
    v.tensor_copy(p.cols[:].rearrange("p c b h -> p (c b h)"), p.psum[:, 2, 0 : 4 * HEADS]).then_inc(
        p.sem["cols_ready"], 1)
    dve.wait_ge(p.sem["cols_ready"], a("cols_ready") + 1)
    dve.wait_ge(p.sem["exp_cum"], a("exp_cum") + 1)
    v.tensor_tensor(p.beta_exp[:], p.cols[:, 1, 0], p.exp_cols[:], ALU.mult).then_inc(p.sem["cols_ready"], 1)
    dve.wait_ge(p.sem["cols_ready"], a("cols_ready") + 2)

    for gq in range(HEADS // GROUP):
        at = lambda name, per: a(name) + gq * per
        for i in range(GROUP):
            h = gq * GROUP + i
            dve.wait_ge(p.sem["rows_done"], at("rows_done", 4) + i + 1)
            if gq:
                dve.wait_ge(p.sem["out_ready"], a("out_ready") + gq * GROUP)
            v.tensor_tensor(p.kb[:, i], p.qkv[:, 8 + h], p.psum[:, i, T : 2 * T], ALU.mult).then_inc(
                p.sem["kb_ready"], 1)
            for c in range(2):
                v.scalar_tensor_tensor(
                    p.decay[:, i, c * P : c * P + P], p.psum[:, i, c * P : c * P + P],
                    p.cols[:, c, 1, h : h + 1], p.c("neg")[:, 0:P], ALU.subtract, ALU.add,
                ).then_inc(p.sem["exponent_ready"], 1)
        for i in range(GROUP):
            h = gq * GROUP + i
            dve.wait_ge(p.sem["pairs_done"], at("pairs_done", 4) + i + 1)
            dve.wait_ge(p.sem["decay_ready"], at("decay_ready", 4) + i + 1)
            v.tensor_tensor(p.a_t[:, i], p.psum[:, 4 + i, 0:T], p.decay[:, i], ALU.mult).then_inc(
                p.sem["pairs_used"], 1)
            v.tensor_tensor(p.qk_t[:, i], p.psum[:, 4 + i, T : 2 * T], p.decay[:, i], ALU.mult).then_inc(
                p.sem["pairs_used"], 1)
            v.tensor_tensor(p.qkv[:, h, P:T], p.qkv[:, h, P:T], p.exp_row[:, i], ALU.mult).then_inc(
                p.sem["q_dec_ready"], 1)
            dve.wait_ge(p.sem["pairs_used"], at("pairs_used", 8) + 2 * i + 1)
            link(v.tensor_tensor(p.kb[:, i], p.a_t[:, i], p.c("first_t"), ALU.mult))
            v.tensor_tensor(
                p.inv_t[:, i, 0].rearrange("p (c j) -> p c j", c=2),
                p.c("ident").unsqueeze(1).broadcast_to([P, 2, P]),
                p.kb[:, i].rearrange("p (c j) -> p c j", c=2), ALU.subtract,
            ).then_inc(p.sem["inv_grown"], 1)
        for i in range(GROUP):
            h = gq * GROUP + i
            dve.wait_ge(p.sem["turned_done"], at("turned_done", 4) + i + 1)
            k0, k1, v0, v1 = (p.psum[:, i, n * P : n * P + P] for n in range(4))
            v.tensor_scalar(p.v_beta[:, i, 0:P], v0, p.cols[:, 0, 0, h : h + 1], None, ALU.mult)
            v.tensor_scalar(p.v_beta[:, i, P:T], v1, p.cols[:, 1, 0, h : h + 1], None, ALU.mult)
            v.tensor_scalar(p.k_tok[:, i, P:T], k1, p.beta_exp[:, h : h + 1], None, ALU.mult)
            v.tensor_scalar(p.k_tok[:, i, 0:P], k0, p.decay[:, i, P - 1 : P], None, ALU.mult).then_inc(
                p.sem["turned_used"], 1)
        masks = p.c("masks").rearrange("p (l n) -> p l n", n=P)
        with dve.Fori(0, LEVELS) as level:
            for i in range(GROUP):
                dve.wait_ge(p.sem["lp_done"], level * GROUP + (at("lp_done", 4 * LEVELS) + i + 1))
                v.tensor_tensor(
                    p.kb[:, i].rearrange("p (c j) -> p c j", c=2),
                    p.psum[:, i, 0:T].rearrange("p (c j) -> p c j", c=2),
                    masks[:, level].unsqueeze(1).broadcast_to([P, 2, P]), ALU.mult,
                ).then_inc(p.sem["new_ready"], 1)
            for i in range(GROUP):
                dve.wait_ge(p.sem["lq_done"], level * GROUP + (at("lq_done", 4 * LEVELS) + i + 1))
                both = p.inv_t[:, i].rearrange("p b n -> p (b n)")
                v.tensor_tensor(both, both, p.psum[:, 4 + i], ALU.subtract).then_inc(p.sem["inv_grown"], 1)
        for i in range(GROUP):
            dve.wait_ge(p.sem["v1_done"], at("v1_done", 4) + i + 1)
            v.tensor_copy(p.decay[:, i, P:T], p.psum[:, i, 0:P]).then_inc(p.sem["v1_ready"], 1)
    for h in range(HEADS):
        dve.wait_ge(p.sem["o_sum"], a("o_sum") + h + 1)
        link(v.tensor_scalar(p.inv[:, h], p.psum[:, h % 2, 0:T], 1.0 / P, EPS, ALU.mult, ALU.add))
        v.reciprocal(p.inv[:, h], p.inv[:, h]).then_inc(p.sem["o_inv"], 1)
    for h in range(HEADS):
        dve.wait_ge(p.sem["o_root"], a("o_root") + 1)
        link(v.scalar_tensor_tensor(
            p.qkv[:, h], p.qkv[:, h], st.par(p, "out_gain"), p.inv[:, h], ALU.mult, ALU.mult))
        v.tensor_tensor(p.qkv[:, h], p.qkv[:, h], p.z[:, h], ALU.mult).then_inc(p.sem["oa_ready"], 1)


def gdn_scalar(p, act, st):
    a, nc, f = st.at, p.nc, p.nc.scalar.activation
    ba, dt_bias = p.lat[:, 6], st.par(p, "dt_bias")[32 : 32 + HEADS]
    soft, fn = p.soft[32 : 32 + HEADS], a("gate_fn")
    act.wait_ge(p.sem["proj_out"], a("proj_out"))
    f(p.rows[0:HEADS], ba[0:HEADS], ACT.Tanh, scale=0.5).then_inc(p.sem["gate_fn"], 1)
    f(p.exp_a[32 : 32 + HEADS], st.par(p, "a_log")[32 : 32 + HEADS], ACT.Exp).then_inc(p.sem["gate_fn"], 1)
    f(soft, ba[32 : 32 + HEADS], ACT.Abs, bias=dt_bias).then_inc(p.sem["gate_fn"], 1)
    act.wait_ge(p.sem["gate_fn"], fn + 3)
    f(soft, soft, ACT.Exp, scale=-1.0).then_inc(p.sem["gate_fn"], 1)
    act.wait_ge(p.sem["gate_fn"], fn + 4)
    f(soft, soft, ACT.Ln, bias=1.0).then_inc(p.sem["gate_fn"], 1)
    act.wait_ge(p.sem["cols_ready"], a("cols_ready") + 1)
    f(p.exp_cols[:], p.cols[:, 1, 1], ACT.Exp).then_inc(p.sem["exp_cum"], 1)
    for gq in range(HEADS // GROUP):
        at = lambda name, per: a(name) + gq * per
        for i in range(GROUP):
            act.wait_ge(p.sem["exponent_ready"], at("exponent_ready", 8) + 2 * i + 2)
            f(p.exp_row[:, i], p.psum[:, i, P:T], ACT.Exp).then_inc(p.sem["row_exp"], 1)
            f(p.decay[:, i], p.decay[:, i], ACT.Exp).then_inc(p.sem["decay_ready"], 1)
        for i in range(GROUP):
            act.wait_ge(p.sem["first_turned"], at("first_turned", 4) + i + 1)
            f(p.inv_t[:, i, 1], p.psum[:, 4 + i, 0:T], ACT.Copy).then_inc(p.sem["first_both"], 1)
        for i in range(GROUP):
            act.wait_ge(p.sem["wu_done"], at("wu_done", 4) + i + 1)
            f(p.w_s[:, i, 0:P], p.psum[:, 4 + i, 0:P], ACT.Copy, scale=-1.0).then_inc(p.sem["w_ready"], 1)
            f(p.decay[:, i, 0:P], p.psum[:, 4 + i, P:T], ACT.Copy).then_inc(p.sem["v0_ready"], 1)
        for i in range(GROUP):
            act.wait_ge(p.sem["state_done"], at("state_done", 4) + i + 1)
            f(p.w_s[:, i, P:T], p.psum[:, 4 + i, T : T + P], ACT.Copy).then_inc(p.sem["state_ready"], 1)
        for i in range(GROUP):
            h = gq * GROUP + i
            act.wait_ge(p.sem["o_done"], at("o_done", 4) + i + 1)
            f(p.qkv[:, h], p.psum[:, 4 + i, 0:T], ACT.Copy).then_inc(p.sem["out_ready"], 1)
    for h in range(HEADS):
        act.wait_ge(p.sem["out_ready"], a("out_ready") + HEADS)
        f(p.inv[:, h], p.qkv[:, h], ACT.Square).then_inc(p.sem["o_sq"], 1)
    act.wait_ge(p.sem["o_inv"], a("o_inv") + HEADS)
    f(p.inv[:, 0:HEADS], p.inv[:, 0:HEADS], ACT.Sqrt).then_inc(p.sem["o_root"], 1)


def gdn_tensor(p, pe, st):
    a, nc, mm = st.at, p.nc, p.nc.tensor.matmul
    ident = p.c("ident")
    rows = p.rows[0 : 32 + HEADS]
    pe.wait_ge(p.sem["rows_ready"], a("rows_ready") + 2)
    pe.wait_ge(p.sem["rows_cleared"], 1)
    for c in range(2):
        for b in range(2):
            ins = mm(p.psum[:, 2, (2 * c + b) * HEADS : (2 * c + b + 1) * HEADS], rows[:, c * P : c * P + P],
                     ident[0 : 32 + HEADS, 32 * b : 32 * b + HEADS], start=True, stop=True)
    ins.then_inc(p.sem["cols_done"], 1)
    pe.wait_ge(p.sem["normed"], a("normed"))
    pe.wait_ge(p.sem["cols_ready"], a("cols_ready") + 1)
    for gq in range(HEADS // GROUP):
        at = lambda name, per: a(name) + gq * per
        if gq:
            pe.wait_ge(p.sem["out_ready"], a("out_ready") + gq * GROUP)
        for i in range(GROUP):
            h = gq * GROUP + i
            for b in range(2):
                pick = ident[0 : 32 + HEADS, 32 - 32 * b + h : 33 - 32 * b + h].to_broadcast([32 + HEADS, P])
                ins = mm(p.psum[:, i, b * T : b * T + T], pick, rows, start=True, stop=True)
            ins.then_inc(p.sem["rows_done"], 1)
        for i in range(GROUP):
            h = gq * GROUP + i
            pe.wait_ge(p.sem["kb_ready"], at("kb_ready", 4) + i + 1)
            for c in range(2):
                part = slice(c * P, c * P + P)
                k = p.qkv[:, 8 + h, part]
                mm(p.psum[:, 4 + i, part], k, p.kb[:, i, part], start=True, stop=True)
                ins = mm(p.psum[:, 4 + i, T + c * P : T + c * P + P], k, p.qkv[:, h, part], start=True, stop=True)
            ins.then_inc(p.sem["pairs_done"], 1)
        for i in range(GROUP):
            h = gq * GROUP + i
            pe.wait_ge(p.sem["row_exp"], at("row_exp", 4) + i + 1)
            for n, src in enumerate((8 + h, 8 + h, 16 + h, 16 + h)):
                part = slice(n % 2 * P, n % 2 * P + P)
                ins = nc.tensor.transpose(p.psum[:, i, n * P : n * P + P], p.qkv[:, src, part], ident)
            ins.then_inc(p.sem["turned_done"], 1)
        for i in range(GROUP):
            pe.wait_ge(p.sem["inv_grown"], at("inv_grown", GROWN) + i + 1)
            for c in range(2):
                part = slice(c * P, c * P + P)
                ins = nc.tensor.transpose(p.psum[:, 4 + i, part], p.inv_t[:, i, 0, part], ident)
            ins.then_inc(p.sem["first_turned"], 1)
        pe.wait_ge(p.sem["turned_used"], at("turned_used", 4) + 4)
        pe.wait_ge(p.sem["first_both"], at("first_both", 4) + 4)
        with pe.Fori(0, LEVELS) as level:
            for i in range(GROUP):
                pe.wait_ge(p.sem["inv_grown"], level * GROUP + (at("inv_grown", GROWN) + i + 1))
                for c in range(2):
                    part = slice(c * P, c * P + P)
                    ins = mm(p.psum[:, i, part], p.a_t[:, i, part], p.inv_t[:, i, 1, part], start=True, stop=True)
                ins.then_inc(p.sem["lp_done"], 1)
            for i in range(GROUP):
                pe.wait_ge(p.sem["new_ready"], level * GROUP + (at("new_ready", 4 * LEVELS) + i + 1))
                for c in range(2):
                    part = slice(c * P, c * P + P)
                    t_t, t = p.inv_t[:, i, 0, part], p.inv_t[:, i, 1, part]
                    mm(p.psum[:, 4 + i, part], p.kb[:, i, part], t_t, start=True, stop=True)
                    ins = mm(p.psum[:, 4 + i, T + c * P : T + c * P + P], t_t, p.kb[:, i, part], start=True, stop=True)
                ins.then_inc(p.sem["lq_done"], 1)
        grown = at("inv_grown", GROWN) + GROWN
        for i in range(GROUP):
            pe.wait_ge(p.sem["inv_grown"], grown - GROUP + i + 1)
            t0, t1 = p.inv_t[:, i, 0, 0:P], p.inv_t[:, i, 0, P:T]
            mm(p.psum[:, 4 + i, 0:P], p.k_tok[:, i, P:T], t1, start=True, stop=True)
            mm(p.psum[:, 4 + i, P:T], t0, p.v_beta[:, i, 0:P], start=True, stop=True).then_inc(p.sem["wu_done"], 1)
        for i in range(GROUP):
            pe.wait_ge(p.sem["v0_ready"], at("v0_ready", 4) + i + 1)
            mm(p.psum[:, 4 + i, T : T + P], p.k_tok[:, i, 0:P], p.decay[:, i, 0:P], start=True, stop=True).then_inc(
                p.sem["state_done"], 1)
        for i in range(GROUP):
            pe.wait_ge(p.sem["state_ready"], at("state_ready", 4) + i + 1)
            mm(p.psum[:, i, 0:P], p.inv_t[:, i, 0, P:T], p.v_beta[:, i, P:T], start=True, stop=False)
            mm(p.psum[:, i, 0:P], p.w_s[:, i, 0:P], p.w_s[:, i, P:T], start=False, stop=True).then_inc(
                p.sem["v1_done"], 1)
        for i in range(GROUP):
            h = gq * GROUP + i
            pe.wait_ge(p.sem["v1_ready"], at("v1_ready", 4) + i + 1)
            mm(p.psum[:, 4 + i, 0:P], p.decay[:, i, 0:P], p.qk_t[:, i, 0:P], start=True, stop=True)
            mm(p.psum[:, 4 + i, P:T], p.w_s[:, i, P:T], p.qkv[:, h, P:T], start=True, stop=False)
            mm(p.psum[:, 4 + i, P:T], p.decay[:, i, P:T], p.qk_t[:, i, P:T], start=False, stop=True).then_inc(
                p.sem["o_done"], 1)
    for h in range(HEADS):
        pe.wait_ge(p.sem["o_sq"], a("o_sq") + h + 1)
        if h >= 2:
            pe.wait_ge(p.sem["o_inv"], a("o_inv") + h - 1)
        mm(p.psum[:, h % 2, 0:T], p.c("ones"), p.inv[:, h], start=True, stop=True).then_inc(p.sem["o_sum"], 1)



TWO_PI = (6.28125, 0.0019350051879882812, 3.0199159819567e-07)
ROUND = 12582912.0


def trig_vector(p, dve):
    v, step = p.nc.vector, 0

    def link(ins):
        nonlocal step
        step += 1
        ins.then_inc(p.sem["trig_step"], 1)
        dve.wait_ge(p.sem["trig_step"], step)

    link(v.tensor_copy(p.angle[:], p.positions[:]))
    link(v.tensor_scalar(p.angle[:], p.angle[:], p.c("inv_freq"), None, ALU.mult))
    for out, shift in ((p.sin, 0.0), (p.cos, 0.25)):
        turns = p.var
        link(v.tensor_scalar(turns[:], p.angle[:], 1.0 / (2 * math.pi), shift, ALU.mult, ALU.add))
        link(v.tensor_scalar(turns[:], turns[:], ROUND, None, ALU.add))
        link(v.tensor_scalar(turns[:], turns[:], -ROUND, None, ALU.add))
        src = p.angle
        for part in TWO_PI:
            link(v.scalar_tensor_tensor(out[:], turns[:], -part, src[:], ALU.mult, ALU.add))
            src = out
        link(v.tensor_scalar(out[:], out[:], 2 * math.pi * shift, 3.1415925, ALU.add, ALU.min))
        v.tensor_scalar(out[:], out[:], -3.1415925, None, ALU.max).then_inc(p.sem["angles_ready"], 1)
    dve.wait_ge(p.sem["trig_done"], 1)


def trig_scalar(p, act):
    act.wait_ge(p.sem["angles_ready"], 2)
    p.nc.scalar.activation(p.sin[:], p.sin[:], ACT.Sin)
    p.nc.scalar.activation(p.cos[:], p.cos[:], ACT.Sin).then_inc(p.sem["trig_done"], 1)



N_UP = 12 + 8


def up_gpsimd(p, pool, st):
    a, nc = st.at, p.nc
    pool.wait_ge(p.sem["oa_ready"], a("oa_ready"))
    for t in range(LAT_Q + LAT_KV):
        nc.gpsimd.tensor_tensor(p.lat_sq[:, t], p.lat[:, t], p.lat[:, t], ALU.mult).then_inc(p.sem["lat_sq"], 1)
    nc.gpsimd.tensor_tensor(p.kr[:], p.lat[:, 5], p.lat[:, 5], ALU.mult).then_inc(p.sem["kpe_sq"], 1)
    for j in range(N_UP):
        pool.wait_ge(p.sem["up_out"], a("up_out") + j + 1)
        if j >= 8:
            pool.wait_ge(p.sem["up_summed"], a("up_summed") + j - 7)
        src = p.up_tile(j)
        nc.gpsimd.tensor_tensor(p.tmp[:, j % 8], src, src, ALU.mult).then_inc(p.sem["up_sq"], 1)


def up_tensor(p, pe, st):
    a, u0, nc, mm = st.at, st.unit0, p.nc, p.nc.tensor.matmul
    ones, halves = p.c("ones"), (p.c("half_0"), p.c("half_1"))
    for b, (t0, n) in enumerate(((0, LAT_Q), (LAT_Q, LAT_KV))):
        for k in range(n):
            pe.wait_ge(p.sem["lat_sq"], a("lat_sq") + t0 + k + 1)
            ins = mm(p.psum[:, 6 + b, 0:T], ones, p.lat_sq[:, t0 + k], start=k == 0, stop=k == n - 1)
        ins.then_inc(p.sem["lat_sum"], 1)

    def tile(j, n_k, chunk, t0):
        for k in range(n_k):
            if j == 0:
                pe.wait_ge(p.sem["lat_ready"], a("lat_ready") + LAT_Q)
            if j == 12:
                pe.wait_ge(p.sem["lat_ready"], a("lat_ready") + LAT_Q + LAT_KV)
            if k == 0 and j >= 4:
                pe.wait_ge(p.sem["up_out"], a("up_out") + j - 3)
            ins = three_pass(p, p.psum[:, j % 4, 0:T], (u0 + chunk // UNIT) % SLOTS, (chunk + k) % UNIT,
                             p.lat_hi[:, t0 + k], p.lat_lo[:, t0 + k], k == 0, k == n_k - 1)
        return ins

    def total(j):
        pe.wait_ge(p.sem["up_sq"], a("up_sq") + j + 1)
        sq = p.tmp[:, j % 8]
        if j < 8:
            ins = mm(rows, p.pick("row", j), sq, start=j == 0, stop=False, skip_group_check=True)
        elif j < 12:
            for b in range(2):
                ins = mm(rows, p.pick(f"row_{b}", 2 * (j - 8) + b), sq, start=False, stop=False, skip_group_check=True)
        else:
            h = j - 12
            mm(rows, p.pick("row_0", 8 + h), p.kr[:], start=False, stop=False, skip_group_check=True)
            ins = mm(rows, p.pick("row", 8 + h), sq, start=False, stop=j == N_UP - 1, skip_group_check=True)
        ins.then_inc(p.sem["up_summed"], 1)

    rows = p.psum[0:16, 6, 0:T]
    pe.wait_ge(p.sem["lat_var"], a("lat_var") + 4)
    for u in range(6):
        pe.wait_ge(p.sem["lo_ready"], u0 + u + 1)
        for b in range(2):
            ins = tile(2 * u + b, LAT_Q, u * UNIT + 4 * b, 0)
        ins.then_inc(p.sem["unit_done"], 1)
        if u:
            total(2 * u - 2)
            total(2 * u - 1)
    pe.wait_ge(p.sem["kpe_sq"], a("kpe_sq") + 1)
    for u in range(2):
        pe.wait_ge(p.sem["lo_ready"], u0 + 6 + u + 1)
        for b in range(4):
            ins = tile(12 + 4 * u + b, LAT_KV, (6 + u) * UNIT + 2 * b, LAT_Q)
        ins.then_inc(p.sem["unit_done"], 1)
        for j in ((10, 11), (12, 13, 14, 15))[u]:
            total(j)
    for k in range(LAT_KV):
        s = (u0 + 8 + k) % SLOTS
        pe.wait_ge(p.sem["lo_ready"], u0 + 8 + k + 1)
        for c in range(2):
            hi, lo = (x[:, LAT_Q + k, c * P : c * P + P] for x in (p.lat_hi, p.lat_lo))
            for b in range(2):
                out = p.psum[:, (4, 5, 2, 3)[2 * c + b]]
                if k == 0 and c == 1 and b == 0:
                    pe.wait_ge(p.sem["up_out"], a("up_out") + N_UP)
                w_hi, w_lo = (w[:, s, 4 * b : 4 * b + 4].rearrange("p k m -> p (k m)") for w in (p.w_hi, p.w_lo))
                mm(out, hi, w_hi, start=k == 0, stop=False)
                mm(out, hi, w_lo, start=False, stop=False)
                ins = mm(out, lo, w_hi, start=False, stop=k == LAT_KV - 1)
        ins.then_inc(p.sem["unit_done"], 1)
    for j in range(16, N_UP):
        total(j)
    for j in range(5):
        pe.wait_ge(p.sem["rope_in"], a("rope_in") + j + 1)
        if j >= 2:
            pe.wait_ge(p.sem["rope_out"], a("rope_out") + j - 1)
        src = p.kr[:] if j == 4 else p.qr[:, j]
        mm(p.psum[:, j % 2, 0:T], p.c("rot"), src, start=True, stop=True).then_inc(p.sem["rope_turned"], 1)
    pe.wait_ge(p.sem["rinv_rows"], a("rinv_rows") + 1)
    pe.wait_ge(p.sem["values_out"], a("values_out") + 4)
    ident = p.c("ident")
    for t in range(2 * HEADS):
        if t >= 4:
            pe.wait_ge(p.sem["head_normed"], a("head_normed") + t - 3)
        else:
            pe.wait_ge(p.sem["rope_out"], a("rope_out") + 5)
        mm(p.psum[:, t % 4, 0:T], ident[0:16, t : t + 1].to_broadcast([16, P]), p.rinv16[0:16],
           start=True, stop=True).then_inc(p.sem["head_rinv"], 1)


def up_scalar(p, act, st):
    a, u0, nc, f = st.at, st.unit0, p.nc, p.nc.scalar.activation
    for b in range(2):
        act.wait_ge(p.sem["lat_var"], a("lat_var") + 2 * b + 2)
        f(p.rinv_lat[:, b], p.rinv_lat[:, b], ACT.Sqrt).then_inc(p.sem["lat_root"], 1)
    for t in range(LAT_Q + LAT_KV):
        act.wait_ge(p.sem["lat_scaled"], a("lat_scaled") + t + 1)
        f(p.lat_hi[:, t], p.lat[:, t], ACT.Copy).then_inc(p.sem["lat_rounded"], 1)
    for j in range(N_UP):
        if j < 12:
            if j % 2 == 0:
                split_hi(p, act, u0 + j // 2 + 2)
        elif j % 4 == 0:
            split_hi(p, act, u0 + 6 + (j - 12) // 4 + 2)
        act.wait_ge(p.sem["unit_done"], u0 + (j // 2 if j < 12 else 6 + (j - 12) // 4) + 1)
        f(p.up_tile(j), p.psum[:, j % 4, 0:T], ACT.Copy).then_inc(p.sem["up_out"], 1)
    split_hi(p, act, u0 + 10)
    split_hi(p, act, u0 + 11)
    act.wait_ge(p.sem["unit_done"], u0 + 10)
    for c in range(2):
        for b in range(2):
            f(p.vt[:, c, b * 512 : b * 512 + 512], p.psum[:, (4, 5, 2, 3)[2 * c + b]], ACT.Copy).then_inc(
                p.sem["values_out"], 1)
    act.wait_ge(p.sem["head_var"], a("head_var") + 2)
    f(p.rinv16[0:16], p.rinv16[0:16], ACT.Sqrt).then_inc(p.sem["rinv_rows"], 1)


def up_vector(p, dve, st):
    a, u0, nc, v = st.at, st.unit0, p.nc, p.nc.vector
    gain = st.par(p, "lat_gain")
    for b, n in enumerate((LAT_Q, LAT_KV)):
        dve.wait_ge(p.sem["lat_sum"], a("lat_sum") + b + 1)
        v.tensor_scalar(p.rinv_lat[:, b], p.psum[:, 6 + b, 0:T], 1.0 / (n * P), EPS, ALU.mult, ALU.add).then_inc(
            p.sem["lat_var"], 1)
        dve.wait_ge(p.sem["lat_var"], a("lat_var") + 2 * b + 1)
        v.reciprocal(p.rinv_lat[:, b], p.rinv_lat[:, b]).then_inc(p.sem["lat_var"], 1)
    for t in range(LAT_Q + LAT_KV):
        b = t // LAT_Q
        dve.wait_ge(p.sem["lat_root"], a("lat_root") + b + 1)
        v.scalar_tensor_tensor(
            p.lat[:, t], p.lat[:, t], gain[:, t : t + 1], p.rinv_lat[:, b], ALU.mult, ALU.mult
        ).then_inc(p.sem["lat_scaled"], 1)
    for t in range(LAT_Q + LAT_KV):
        dve.wait_ge(p.sem["lat_rounded"], a("lat_rounded") + t + 1)
        v.tensor_tensor(p.lat_lo[:, t], p.lat[:, t], p.lat_hi[:, t].bitcast(F32), ALU.subtract).then_inc(
            p.sem["lat_ready"], 1)
    for s in range(10):
        split_lo(p, dve, u0 + 2 + s)
    dve.wait_ge(p.sem["up_summed"], a("up_summed") + N_UP)
    v.tensor_scalar(p.rinv16[0:16], p.psum[0:16, 6, 0:T], 1.0 / 192, EPS, ALU.mult, ALU.add).then_inc(
        p.sem["head_var"], 1)
    dve.wait_ge(p.sem["head_var"], a("head_var") + 1)
    v.reciprocal(p.rinv16[0:16], p.rinv16[0:16]).then_inc(p.sem["head_var"], 1)
    q_norm, k_norm = st.par(p, "q_norm"), st.par(p, "k_norm")
    for j in range(5):
        out, src, g = (p.kr[:], p.lat[:, 5], k_norm) if j == 4 else (p.qr[:, j], p.qr[:, j], q_norm)
        v.tensor_scalar(out, src, g[:, 1:2], None, ALU.mult).then_inc(p.sem["rope_in"], 1)
    for j in range(5):
        out = p.kr[:] if j == 4 else p.qr[:, j]
        dve.wait_ge(p.sem["rope_turned"], a("rope_turned") + j + 1)
        v.tensor_tensor(out, out, p.cos[:], ALU.mult).then_inc(p.sem["rope_step"], 1)
        v.tensor_tensor(p.work[:, j % 2], p.psum[:, j % 2, 0:T], p.sin[:], ALU.mult).then_inc(p.sem["rope_step"], 1)
        dve.wait_ge(p.sem["rope_step"], a("rope_step") + 2 * j + 2)
        v.tensor_tensor(out, out, p.work[:, j % 2], ALU.add).then_inc(p.sem["rope_out"], 1)
    dve.wait_ge(p.sem["rope_out"], a("rope_out") + 5)
    for t in range(2 * HEADS):
        dve.wait_ge(p.sem["head_rinv"], a("head_rinv") + t + 1)
        rinv, h = p.psum[:, t % 4, 0:T], t % HEADS
        if t < HEADS:
            v.scalar_tensor_tensor(p.qn[:, h], p.qn[:, h], q_norm[:, 0:1], rinv, ALU.mult, ALU.mult)
            half = slice(ROPE * (h % 2), ROPE * (h % 2) + ROPE)
            ins = v.tensor_tensor(p.qr[half, h // 2], p.qr[half, h // 2], p.psum[half, t % 4, 0:T], ALU.mult)
        else:
            v.scalar_tensor_tensor(p.kn[:, h], p.kn[:, h], k_norm[:, 0:1], rinv, ALU.mult, ALU.mult)
            ins = v.scalar_tensor_tensor(
                p.krz[:, h], p.kr[:], p.c(f"half_{h % 2}"), rinv, ALU.mult, ALU.mult)
        ins.then_inc(p.sem["head_normed"], 1)



SCALE = 192.0 ** -0.5


def attn_tensor(p, pe, st):
    a, nc, mm = st.at, p.nc, p.nc.tensor.matmul
    pe.wait_ge(p.sem["head_normed"], a("head_normed"))
    q0, q1, both = slice(0, P), slice(P, T), slice(0, T)
    for i in range(HEADS + 2):
        if i < HEADS:
            h = i
            if h >= 2:
                pe.wait_ge(p.sem["masked"], a("masked") + h - 1)
            for part, keys, lo, hi in ((q0, q0, 0, P), (q1, both, P, 3 * P)):
                out = p.psum[:, h % 2, lo:hi]
                mm(out, p.qn[:, h, part], p.kn[:, h, keys], start=True, stop=False)
                ins = mm(out, p.qr[:, h // 2, part], p.krz[:, h, keys], start=False, stop=True)
            ins.then_inc(p.sem["scored"], 1)
        if 1 <= i <= HEADS:
            h = i - 1
            pe.wait_ge(p.sem["weighed"], a("weighed") + h + 1)
            if h >= 2:
                pe.wait_ge(p.sem["weights_out"], a("weights_out") + h - 1)
            for n in range(3):
                part = slice(n * P, n * P + P)
                ins = nc.tensor.transpose(p.psum[:, 2 + h % 2, part], p.sm[:, h % 2, part], p.c("ident"))
            ins.then_inc(p.sem["weights_turned"], 1)
        if i >= 2:
            h = i - 2
            pe.wait_ge(p.sem["weights_out"], a("weights_out") + h + 1)
            if h >= 2:
                pe.wait_ge(p.sem["ob_out"], a("ob_out") + h - 1)
            out, cols = p.psum[:, 4 + h % 2], slice(h * P, h * P + P)
            mm(out[:, 0:T], p.vt[:, 0, cols], p.pt[:, h % 2, 0:T], start=True, stop=False)
            mm(out[:, P:T], p.vt[:, 1, cols], p.pt[:, h % 2, T : 3 * P], start=False, stop=True).then_inc(
                p.sem["mixed"], 1)


def attn_vector(p, dve, st):
    a, v = st.at, p.nc.vector
    for i in range(HEADS + 1):
        if i < HEADS:
            h = i
            dve.wait_ge(p.sem["scored"], a("scored") + h + 1)
            if h >= 2:
                dve.wait_ge(p.sem["weights_turned"], a("weights_turned") + h - 1)
            sm = p.sm[:, h % 2]
            v.tensor_tensor(sm, p.psum[:, h % 2, 0 : 3 * P], p.c("attn"), ALU.add).then_inc(p.sem["masked"], 1)
            dve.wait_ge(p.sem["masked"], a("masked") + h + 1)
            v.tensor_reduce(p.mx[:, h % 2, 0:1], sm[:, 0:P], AX.X, ALU.max).then_inc(p.sem["max_step"], 1)
            v.tensor_reduce(p.mx[:, h % 2, 1:2], sm[:, P : 3 * P], AX.X, ALU.max).then_inc(p.sem["max_step"], 1)
            dve.wait_ge(p.sem["max_step"], a("max_step") + 2 * h + 2)
            v.tensor_scalar(p.nmx[:, h % 2], p.mx[:, h % 2], -SCALE, None, ALU.mult).then_inc(p.sem["max_ready"], 1)
        if i:
            h = i - 1
            dve.wait_ge(p.sem["exped"], a("exped") + h + 1)
            v.reciprocal(p.rden[:, h % 2], p.den[:, h % 2]).then_inc(p.sem["den_ready"], 1)
            dve.wait_ge(p.sem["den_ready"], a("den_ready") + h + 1)
            sm = p.sm[:, h % 2]
            v.tensor_scalar(sm[:, 0:P], sm[:, 0:P], p.rden[:, h % 2, 0:1], None, ALU.mult)
            v.tensor_scalar(sm[:, P : 3 * P], sm[:, P : 3 * P], p.rden[:, h % 2, 1:2], None, ALU.mult).then_inc(
                p.sem["weighed"], 1)


def attn_scalar(p, act, st):
    a, f = st.at, p.nc.scalar.activation
    for i in range(HEADS + 2):
        if i < HEADS:
            h = i
            act.wait_ge(p.sem["max_ready"], a("max_ready") + h + 1)
            sm = p.sm[:, h % 2]
            f(sm[:, 0:P], sm[:, 0:P], ACT.Exp, bias=p.nmx[:, h % 2, 0:1], scale=SCALE, accum_out=p.den[:, h % 2, 0:1])
            f(sm[:, P : 3 * P], sm[:, P : 3 * P], ACT.Exp, bias=p.nmx[:, h % 2, 1:2], scale=SCALE,
              accum_out=p.den[:, h % 2, 1:2]).then_inc(p.sem["exped"], 1)
        if 1 <= i <= HEADS:
            h = i - 1
            act.wait_ge(p.sem["weights_turned"], a("weights_turned") + h + 1)
            if h >= 2:
                act.wait_ge(p.sem["mixed"], a("mixed") + h - 1)
            f(p.pt[:, h % 2], p.psum[:, 2 + h % 2, 0 : 3 * P], ACT.Copy).then_inc(p.sem["weights_out"], 1)
        if i >= 2:
            h = i - 2
            act.wait_ge(p.sem["mixed"], a("mixed") + h + 1)
            f(p.qn[:, h], p.psum[:, 4 + h % 2, 0:T], ACT.Copy).then_inc(p.sem["ob_out"], 1)




def gates_tensor(p, pe, st):
    a, u0 = st.at, st.unit0
    banks = (0, 1, 2, 3)
    pe.wait_ge(p.sem["ob_out"], a("ob_out"))

    def product(g, c):
        b = c % 4
        src = ((p.h_hi, p.h_lo, 0), (p.o_hi, p.o_lo, 0), (p.h_hi, p.h_lo, 0), (p.o_hi, p.o_lo, 8))[b]
        if not isinstance(g, int) or 8 * g + c >= 4:
            sem = ("gate_tanh", "y_step")[b % 2]
            pe.wait_ge(p.sem[sem], g * 4 + (a(sem) + c // 2 - 1))
        pe.wait_ge(p.sem["lo_ready"], g * 8 + (u0 + c + 1))
        if isinstance(g, int) and g == 0 and c == 1:
            pe.wait_ge(p.sem["o_split"], a("o_split") + 1)
        if isinstance(g, int) and g == 0 and c == 3:
            pe.wait_ge(p.sem["o_split"], a("o_split") + 2)
        for k in range(UNIT):
            ins = three_pass(p, p.psum[:, banks[b], 0:T], (u0 + c) % SLOTS, k, src[0][:, src[2] + k],
                             src[1][:, src[2] + k], k == 0, k == UNIT - 1)
        ins.then_inc(p.sem["unit_done"], 1)

    for c in range(8):
        product(0, c)
    with pe.Fori(1, 4) as g:
        for c in range(8):
            product(g, c)
    for m in range(KD):
        s = u0 + 32 + m
        pe.wait_ge(p.sem["lo_ready"], s + 1)
        if m >= 4:
            pe.wait_ge(p.sem["x_ready"], a("x_ready") + m - 3)
        for k in range(UNIT):
            if m == 0 and k % 4 == 0:
                pe.wait_ge(p.sem["y_split"], a("y_split") + k // 4 + 1)
            ins = three_pass(p, p.psum[:, 4 + m % 4, 0:T], s % SLOTS, k, p.h_hi[:, k], p.h_lo[:, k], k == 0, k == UNIT - 1)
        ins.then_inc(p.sem["unit_done"], 1)


def gates_scalar(p, act, st):
    a, u0, f = st.at, st.unit0, p.nc.scalar.activation
    act.wait_ge(p.sem["ob_out"], a("ob_out"))
    act.wait_ge(p.sem["mixed"], a("mixed"))
    for b, src in enumerate((p.qkv[:, 0:HEADS], p.qn[:])):
        f(p.o_hi[:, 8 * b : 8 * b + 8], src, ACT.Copy).then_inc(p.sem["o_rounded"], 1)

    def gate(g, c):
        split_hi(p, act, u0 + 2 * c + 2, g)
        split_hi(p, act, u0 + 2 * c + 3, g)
        act.wait_ge(p.sem["unit_done"], g * 8 + (u0 + 2 * c + 1))
        if not isinstance(g, int) or 4 * g + c >= 2:
            act.wait_ge(p.sem["y_step"], g * 4 + (a("y_step") + c - 1))
        f(p.gate_t[:, c % 2], p.psum[:, 2 * (c % 2), 0:T], ACT.Tanh, scale=0.5).then_inc(p.sem["gate_tanh"], 1)

    groups(act, 16, 4, gate)
    for b in range(2):
        act.wait_ge(p.sem["y_ready"], a("y_ready") + 4 * b + 4)
        act.wait_ge(p.sem["unit_done"], u0 + 31)
        half = slice(4 * b, 4 * b + 4)
        f(p.h_hi[:, half], p.y[:, half], ACT.Copy).then_inc(p.sem["y_rounded"], 1)
    for m in range(KD):
        split_hi(p, act, u0 + 34 + m)


def gates_vector(p, dve, st):
    a, u0, v, x = st.at, st.unit0, p.nc.vector, st.x(p)
    for b, src in enumerate((p.qkv[:, 0:HEADS], p.qn[:])):
        dve.wait_ge(p.sem["o_rounded"], a("o_rounded") + b + 1)
        part = slice(8 * b, 8 * b + 8)
        v.tensor_tensor(p.o_lo[:, part], src, p.o_hi[:, part].bitcast(F32), ALU.subtract).then_inc(p.sem["o_split"], 1)

    def branch(g, c):
        split_lo(p, dve, u0 + 2 * c + 2, g)
        split_lo(p, dve, u0 + 2 * c + 3, g)
        m = g * 2 + c // 2
        dve.wait_ge(p.sem["unit_done"], g * 8 + (u0 + 2 * c + 2))
        dve.wait_ge(p.sem["gate_tanh"], g * 4 + (a("gate_tanh") + c + 1))
        out = p.work[:, 0] if c % 2 else p.y[:, m]
        v.scalar_tensor_tensor(
            out, p.gate_t[:, c % 2], 1.0, p.psum[:, 2 * (c % 2) + 1, 0:T], ALU.add, ALU.mult
        ).then_inc(p.sem["y_step"], 1)
        if c % 2:
            dve.wait_ge(p.sem["y_step"], g * 4 + (a("y_step") + c + 1))
            v.tensor_tensor(p.y[:, m], p.y[:, m], p.work[:, 0], ALU.add).then_inc(p.sem["y_ready"], 1)

    groups(dve, 16, 4, branch)
    for b in range(2):
        dve.wait_ge(p.sem["y_rounded"], a("y_rounded") + b + 1)
        half = slice(4 * b, 4 * b + 4)
        v.tensor_tensor(p.h_lo[:, half], p.y[:, half], p.h_hi[:, half].bitcast(F32), ALU.subtract).then_inc(
            p.sem["y_split"], 1)
    for m in range(KD):
        split_lo(p, dve, u0 + 34 + m)
        dve.wait_ge(p.sem["unit_done"], u0 + 33 + m)
        v.scalar_tensor_tensor(
            x[:, m], p.psum[:, 4 + m % 4, 0:T], p.mod_g[:, 1, m : m + 1], x[:, m], ALU.mult, ALU.add
        ).then_inc(p.sem["x_ready"], 1)



SH = 32
ROWS = 2 * SH
N_X, N_BC = 16, 4


def ssd_in_tensor(p, pe, st):
    a, u0 = st.at, st.unit0

    def one(g, c):
        if not isinstance(g, int) or 8 * g + c >= 4:
            pe.wait_ge(p.sem["proj_out"], g * 8 + (a("proj_out") + c - 3))
        pe.wait_ge(p.sem["lo_ready"], g * 8 + (u0 + c + 1))
        for k in range(UNIT):
            if isinstance(g, int) and g == 0 and c == 0:
                pe.wait_ge(p.sem["h_ready"], a("h_ready") - KD + k + 1)
            ins = three_pass(p, p.psum[:, PROJ_BANKS[c % 4], 0:T], (u0 + c) % SLOTS, k,
                             p.h_hi[:, k], p.h_lo[:, k], k == 0, k == UNIT - 1)
        ins.then_inc(p.sem["unit_done"], 1)

    for c in range(8):
        one(0, c)
    if st.n_conv >= 24:
        with pe.Fori(1, 3) as g:
            for c in range(8):
                one(g, c)
    else:
        for c in range(8):
            one(1, c)
    for c in range(st.n_conv % 8 + 1):
        one(st.n_conv // 8, c)
    if st.on_ctx:
        skip_unit(p, pe, u0 + 21)


def skip_unit(p, pe, s):
    pe.wait_ge(p.sem["lo_ready"], s + 1)
    p.nc.tensor.matmul(p.psum[:, 7, 0:T], p.w_hi[:, s % SLOTS, 0], p.h_hi[:, 0], start=True, stop=True).then_inc(
        p.sem["unit_done"], 1)


def ssd_in_scalar(p, act, st):
    a, u0, f = st.at, st.unit0, p.nc.scalar.activation

    def silu(g, c):
        act.wait_ge(p.sem["conv_done"], g * 4 + (a("conv_done") + c + 1))
        act.wait_ge(p.sem["loaded"], p.n_loads)
        t = g * 4 + c
        tile = p.sxbc(t)
        f(tile, tile, ACT.Silu).then_inc(p.sem["act_done"], 1)

    for t in range(st.n_conv):
        split_hi(p, act, u0 + t + 2)
        act.wait_ge(p.sem["unit_done"], u0 + t + 1)
        if t >= 4:
            act.wait_ge(p.sem["conv_done"], a("conv_done") + t - 3)
        f(p.sconv_in[:, t % 4, 2 : 2 + T], p.psum[:, PROJ_BANKS[t % 4], 0:T], ACT.Copy).then_inc(p.sem["proj_out"], 1)
        if t:
            silu(0, t - 1)
    t = st.n_conv
    split_hi(p, act, u0 + t + 2)
    silu(0, t - 1)
    act.wait_ge(p.sem["unit_done"], u0 + t + 1)
    f(p.rows[0:ROWS], p.psum[0:ROWS, PROJ_BANKS[t % 4], 0:T], ACT.Copy).then_inc(p.sem["proj_out"], 1)
    if st.on_ctx:
        split_hi(p, act, u0 + t + 3)
    fn, e = a("gate_fn"), p.var[0:ROWS]
    act.wait_ge(p.sem["proj_out"], a("proj_out") + t + 1)
    f(p.exp_a[0:ROWS], st.par(p, "a_log")[0:ROWS], ACT.Exp).then_inc(p.sem["gate_fn"], 1)
    f(e, p.rows[0:ROWS], ACT.Abs, bias=st.par(p, "dt_bias")[0:ROWS]).then_inc(p.sem["gate_fn"], 1)
    act.wait_ge(p.sem["gate_fn"], fn + 2)
    f(e, e, ACT.Exp, scale=-1.0).then_inc(p.sem["gate_fn"], 1)
    act.wait_ge(p.sem["gate_fn"], fn + 3)
    f(e, e, ACT.Ln, bias=1.0).then_inc(p.sem["gate_fn"], 1)
    if st.on_ctx:
        act.wait_ge(p.sem["dt_step"], a("dt_step") + 6)
        f(e, e, ACT.Exp).then_inc(p.sem["gate_fn"], 1)


def ssd_in_gpsimd(p, pool, st):
    pool.wait_ge(p.sem["unit_done"], st.unit0)
    for s in range(4):
        p.nc.gpsimd.memset(p.sconv_in[:, s, 0:2], 0.0)
        p.nc.gpsimd.memset(p.sconv_in[:, s, 2 + T : 4 + T], 0.0).then_inc(p.sem["conv_pad"], 1)


def ssd_in_vector(p, dve, st):
    a, u0, v = st.at, st.unit0, p.nc.vector
    w = st.par(p, "conv").rearrange("p (t j) -> p t j", j=5)
    bias = st.par(p, "conv_b")
    dve.wait_ge(p.sem["conv_pad"], a("conv_pad") + 4)
    for t in range(st.n_conv):
        split_lo(p, dve, u0 + t + 2)
        dve.wait_ge(p.sem["proj_out"], a("proj_out") + t + 1)
        out, src = p.sxbc(t), p.sconv_in[:, t % 4]
        v.tensor_scalar(out, src[:, 0:T], w[:, t, 0:1], bias[:, t : t + 1], ALU.mult, ALU.add).then_inc(
            p.sem["conv_step"], 1)
        for j in range(1, 5):
            dve.wait_ge(p.sem["conv_step"], a("conv_step") + 4 * t + j)
            v.scalar_tensor_tensor(out, src[:, j : j + T], w[:, t, j : j + 1], out, ALU.mult, ALU.add).then_inc(
                p.sem["conv_step" if j < 4 else "conv_done"], 1)
    split_lo(p, dve, u0 + st.n_conv + 2)
    if st.on_ctx:
        split_lo(p, dve, u0 + st.n_conv + 3)
    step = a("dt_step")

    def link(ins):
        nonlocal step
        step += 1
        ins.then_inc(p.sem["dt_step"], 1)
        dve.wait_ge(p.sem["dt_step"], step)

    rows, dt, decay, e = p.rows[0:ROWS], p.soft[0:ROWS], p.rinv[0:ROWS], p.var
    fwd, bwd = slice(0, SH), slice(SH, ROWS)
    dve.wait_ge(p.sem["gate_fn"], a("gate_fn") + 4)
    link(v.tensor_scalar(dt, rows, st.par(p, "dt_bias")[0:ROWS], 0.0, ALU.add, ALU.max))
    link(v.tensor_tensor(dt, dt, e[0:ROWS], ALU.add))
    link(v.tensor_scalar(decay, dt, p.exp_a[0:ROWS], -1.0, ALU.mult, ALU.mult))
    link(v.tensor_tensor_scan(rows, p.c("ones")[0:ROWS, 0:1].to_broadcast([ROWS, T]), decay, 0.0, ALU.mult, ALU.add))
    left = v.tensor_scalar
    if st.on_ctx:
        link(left(e[fwd], p.rows[fwd], p.rows[fwd, T - 1 : T], -1.0, ALU.subtract, ALU.mult))
        link(v.tensor_tensor(e[bwd], p.rows[bwd], p.rinv[bwd], ALU.subtract))
        dve.wait_ge(p.sem["gate_fn"], a("gate_fn") + 5)
        v.tensor_tensor(p.rows[0:ROWS], e[0:ROWS], dt, ALU.mult).then_inc(p.sem["dt_ready"], 1)
    else:
        link(left(e[bwd], p.rows[bwd], p.rows[bwd, T - 1 : T], -1.0, ALU.subtract, ALU.mult))
        v.tensor_tensor(p.rows[bwd], e[bwd], p.rinv[bwd], ALU.add).then_inc(p.sem["dt_ready"], 1)




def turn_tiles(p, pe, st, sources, sem_done, sem_out):
    a = st.at
    for i, (s0, s1) in enumerate(sources):
        if i >= 4:
            pe.wait_ge(p.sem[sem_out], a(sem_out) + i - 3)
        for n in range(4):
            src = (s0, s1)[n // 2][:, n % 2 * P : n % 2 * P + P]
            ins = p.nc.tensor.transpose(p.psum[:, i % 4, n * P : n * P + P], src, p.c("ident"))
        ins.then_inc(p.sem[sem_done], 1)


def state_tensor(p, pe, st):
    a, mm = st.at, p.nc.tensor.matmul
    pe.wait_ge(p.sem["act_done"], a("act_done"))
    pe.wait_ge(p.sem["proj_out"], a("proj_out"))
    pairs = [(p.sxbc(2 * i), p.sxbc(2 * i + 1)) for i in range(10)]
    turn_tiles(p, pe, st, pairs, "sturned", "sturn_out")
    pe.wait_ge(p.sem["dt_ready"], a("dt_ready"))
    for c in range(2):
        ins = mm(p.psum[:, 4, c * ROWS : c * ROWS + ROWS], p.rows[0:ROWS, c * P : c * P + P],
                 p.c("ident")[0:ROWS, 0:ROWS], start=True, stop=True)
    ins.then_inc(p.sem["cols_done"], 1)
    pe.wait_ge(p.sem["sturn_out"], a("sturn_out") + 10)
    for d in range(2):
        pe.wait_ge(p.sem["xw_ready"], a("xw_ready") + 2 * d + 2)
        for g in range(4):
            if d:
                pe.wait_ge(p.sem["state_out"], a("state_out") + g + 1)
            for c in range(2):
                ins = mm(p.psum[:, g], p.b_tok[:, c, g * P : g * P + P], p.xw[:, c, g * 512 : g * 512 + 512],
                         start=c == 0, stop=c == 1)
            ins.then_inc(p.sem["state_sum"], 1)
    pe.wait_ge(p.sem["state_out"], a("state_out") + 8)


def state_scalar(p, act, st):
    a, f = st.at, p.nc.scalar.activation
    for i in range(10):
        act.wait_ge(p.sem["sturned"], a("sturned") + i + 1)
        to = p.x_tok[:, :, 2 * i * P : 2 * i * P + 2 * P] if i < 8 else p.b_tok[:, :, 2 * (i - 8) * P : 2 * (i - 7) * P]
        for c in range(2):
            ins = f(to[:, c].rearrange("p (j n) -> p j n", j=2),
                    p.psum[:, i % 4].rearrange("p (j c n) -> p j c n", j=2, c=2)[:, :, c], ACT.Copy)
        ins.then_inc(p.sem["sturn_out"], 1)
    for d in range(2):
        for g in range(4):
            act.wait_ge(p.sem["state_sum"], a("state_sum") + 4 * d + g + 1)
            f(p.state[:, d, g * 512 : g * 512 + 512], p.psum[:, g], ACT.Copy).then_inc(p.sem["state_out"], 1)


def state_vector(p, dve, st):
    a, v = st.at, p.nc.vector
    dve.wait_ge(p.sem["cols_done"], a("cols_done") + 1)
    v.tensor_copy(p.scols[:, 0].rearrange("p c r -> p (c r)"), p.psum[:, 4, 0 : 2 * ROWS]).then_inc(
        p.sem["cols_ready"], 1)
    dve.wait_ge(p.sem["cols_ready"], a("cols_ready") + 1)
    dve.wait_ge(p.sem["sturn_out"], a("sturn_out") + 10)
    for d in range(2):
        if d:
            dve.wait_ge(p.sem["state_sum"], a("state_sum") + 4)
        for c in range(2):
            v.tensor_tensor(
                p.xw[:, c].rearrange("p (h n) -> p h n", h=SH), p.x_tok[:, c].rearrange("p (h n) -> p h n", h=SH),
                p.scols[:, 0, c, d * SH : d * SH + SH].unsqueeze(2).broadcast_to([P, SH, 64]), ALU.mult,
            ).then_inc(p.sem["xw_ready"], 1)




def spans(d):
    if d == 0:
        return ((0, 0, T, 0, 0), (1, P, T, 0, T))
    return ((1, 0, T, P, 0), (0, 0, P, 2 * P, T))


def mix_tensor(p, pe, st):
    a, mm, ident = st.at, p.nc.tensor.matmul, p.c("ident")
    pe.wait_ge(p.sem["act_done"], a("act_done"))
    pe.wait_ge(p.sem["proj_out"], a("proj_out"))
    turn_tiles(p, pe, st, [(p.sxbc(2 * i), p.sxbc(2 * i + 1)) for i in range(8)], "sturned", "sturn_out")
    pe.wait_ge(p.sem["dt_ready"], a("dt_ready"))
    for b, rows in enumerate((p.rows, p.soft)):
        for c in range(2):
            at = (2 * b + c) * ROWS
            ins = mm(p.psum[:, 4, at : at + ROWS], rows[0:ROWS, c * P : c * P + P], ident[0:ROWS, 0:ROWS],
                     start=True, stop=True)
    ins.then_inc(p.sem["cols_done"], 1)
    for g in range(4):
        for s in range(2):
            ins = mm(p.psum[:, 5 + g % 2, s * T : s * T + T], p.sxbc(N_X + g)[:, s * P : s * P + P],
                     p.sxbc(N_X + N_BC + g), start=True, stop=True)
        ins.then_inc(p.sem["cb_done"], 1)
        if g >= 1:
            pe.wait_ge(p.sem["cb_out"], a("cb_out") + g)
    pe.wait_ge(p.sem["cb_out"], a("cb_out") + 4)
    pe.wait_ge(p.sem["sturn_out"], a("sturn_out") + 8)
    n = 2 * SH
    for i in range(n + 2):
        if i < n:
            h, d = i // 2, i % 2
            if i >= 4:
                pe.wait_ge(p.sem["g_exp"], a("g_exp") + i - 3)
            r = d * SH + h
            mm(p.psum[:, i % 4, 0:T], ident[0:ROWS, r : r + 1].to_broadcast([ROWS, P]), p.rows[0:ROWS],
               start=True, stop=True).then_inc(p.sem["g_row"], 1)
        if i >= 2:
            k = i - 2
            h, d = k // 2, k % 2
            part = slice(64 * (h % 2), 64 * (h % 2) + 64)
            bank = 5 + h // 2 % 2
            if h % 2 == 0 and d == 0 and h >= 4:
                pe.wait_ge(p.sem["sy_out"], a("sy_out") + h // 2 - 1)
            pe.wait_ge(p.sem["sw_ready"], a("sw_ready") + k + 1)
            pe.wait_ge(p.sem["c_dec"], a("c_dec") + k + 1)
            heads = slice(64 * h, 64 * h + 64)
            for j, (s, lo, hi, _, at) in enumerate(spans(d)):
                mm(p.psum[part, bank, lo:hi], p.x_tok[:, s, heads], p.sw[:, k % 3, at : at + hi - lo],
                   start=d == 0 and j == 0, stop=False)
            mm(p.psum[part, bank, 0:T], p.state[:, d, heads], p.c_exp[:, k % 2], start=False,
               stop=d == 1).then_inc(p.sem["sy_part"], 1)


def mix_scalar(p, act, st):
    a, f = st.at, p.nc.scalar.activation
    for i in range(8):
        act.wait_ge(p.sem["sturned"], a("sturned") + i + 1)
        for c in range(2):
            ins = f(p.x_tok[:, c, 2 * i * P : 2 * i * P + 2 * P].rearrange("p (j n) -> p j n", j=2),
                    p.psum[:, i % 4].rearrange("p (j c n) -> p j c n", j=2, c=2)[:, :, c], ACT.Copy)
        ins.then_inc(p.sem["sturn_out"], 1)
    for g in range(4):
        act.wait_ge(p.sem["cb_done"], a("cb_done") + g + 1)
        f(p.cbt[:, g].rearrange("p s t -> p (s t)"), p.psum[:, 5 + g % 2], ACT.Copy).then_inc(p.sem["cb_out"], 1)
    for i in range(2 * SH):
        act.wait_ge(p.sem["sx_ready"], a("sx_ready") + i + 1)
        f(p.sw[:, i % 3], p.sw[:, i % 3], ACT.Exp).then_inc(p.sem["sx_exp"], 1)
        if i >= 2:
            act.wait_ge(p.sem["c_dec"], a("c_dec") + i - 1)
        f(p.g_exp[:, i % 2], p.psum[:, i % 4, 0:T], ACT.Exp).then_inc(p.sem["g_exp"], 1)


def mix_gpsimd(p, pool, st):
    a = st.at
    for i in range(2 * SH):
        pool.wait_ge(p.sem["g_exp"], a("g_exp") + i + 1)
        if i >= 2:
            pool.wait_ge(p.sem["sy_part"], a("sy_part") + i - 1)
        p.nc.gpsimd.tensor_tensor(p.c_exp[:, i % 2], p.sxbc(N_X + N_BC + i // 16), p.g_exp[:, i % 2], ALU.mult).then_inc(
            p.sem["c_dec"], 1)


def mix_vector(p, dve, st):
    a, v = st.at, p.nc.vector
    dve.wait_ge(p.sem["cols_done"], a("cols_done") + 1)
    v.tensor_copy(p.scols[:].rearrange("p b c r -> p (b c r)"), p.psum[:, 4, 0 : 4 * ROWS]).then_inc(
        p.sem["cols_ready"], 1)
    dve.wait_ge(p.sem["cols_ready"], a("cols_ready") + 1)
    dve.wait_ge(p.sem["cb_out"], a("cb_out") + 4)
    n = 2 * SH
    for i in range(n + 2):
        if i < n:
            h, d = i // 2, i % 2
            dve.wait_ge(p.sem["g_row"], a("g_row") + i + 1)
            if i >= 3:
                dve.wait_ge(p.sem["sy_part"], a("sy_part") + i - 2)
            for j, (s, lo, hi, mask, at) in enumerate(spans(d)):
                ins = v.scalar_tensor_tensor(
                    p.sw[:, i % 3, at : at + hi - lo], p.psum[:, i % 4, lo:hi],
                    p.scols[:, 0, s, d * SH + h : d * SH + h + 1], p.c("neg")[:, mask : mask + hi - lo],
                    ALU.subtract, ALU.add)
            ins.then_inc(p.sem["sx_ready"], 1)
        if 1 <= i <= n:
            k = i - 1
            h, d = k // 2, k % 2
            dve.wait_ge(p.sem["sx_exp"], a("sx_exp") + k + 1)
            for j, (s, lo, hi, mask, at) in enumerate(spans(d)):
                part = p.sw[:, k % 3, at : at + hi - lo]
                ins = v.scalar_tensor_tensor(
                    part, part, p.scols[:, 1, s, d * SH + h : d * SH + h + 1], p.cbt[:, h // 8, s, lo:hi],
                    ALU.mult, ALU.mult)
            ins.then_inc(p.sem["sw_ready"], 1)
        if i >= 5 and (i - 5) % 4 == 0:
            j = (i - 5) // 4
            sy_out(p, dve, st, j)
    for j in range((n + 1 - 5) // 4 + 1, N_X):
        sy_out(p, dve, st, j)


def sy_out(p, dve, st, j):
    dve.wait_ge(p.sem["sy_part"], st.at("sy_part") + 4 * j + 4)
    p.nc.vector.scalar_tensor_tensor(
        p.sxbc(j), p.sxbc(j), st.par(p, "d_skip")[:, j : j + 1], p.psum[:, 5 + j % 2, 0:T], ALU.mult, ALU.add
    ).then_inc(p.sem["sy_out"], 1)




def ssd_out_tensor(p, pe, st):
    a, u0, mm = st.at, st.unit0, p.nc.tensor.matmul
    pe.wait_ge(p.sem["sy_out"], a("sy_out"))
    for t in range(N_X):
        s = u0 + t
        if t >= 2:
            pe.wait_ge(p.sem["gate_act"], a("gate_act") + t - 1)
        pe.wait_ge(p.sem["lo_ready"], s + 1)
        for k in range(UNIT):
            ins = three_pass(p, p.psum[:, t % 2, 0:T], s % SLOTS, k, p.h_hi[:, k], p.h_lo[:, k], k == 0, k == UNIT - 1)
        ins.then_inc(p.sem["unit_done"], 1)
        if t >= 2:
            sz_sum(p, pe, st, t - 2)
    skip_unit(p, pe, u0 + N_X)
    sz_sum(p, pe, st, N_X - 2)
    sz_sum(p, pe, st, N_X - 1)
    pe.wait_ge(p.sem["sz_root"], a("sz_root") + 1)
    for g in range(4):
        mm(p.psum[:, g, 0:T], p.c("ident")[0:16, g : g + 1].to_broadcast([16, P]), p.rinv16[0:16],
           start=True, stop=True).then_inc(p.sem["sz_rinv"], 1)
    for m in range(KD):
        if m >= 2:
            pe.wait_ge(p.sem["x_ready"], a("x_ready") + m - 1)
        for b in range(2):
            s = u0 + N_X + 1 + 2 * m + b
            pe.wait_ge(p.sem["lo_ready"], s + 1)
            for k in range(UNIT):
                if m == 0:
                    pe.wait_ge(p.sem["gy_split"], a("gy_split") + 8 * b + k + 1)
                ins = three_pass(p, p.psum[:, 4 + m % 2, 0:T], s % SLOTS, k, p.gy_hi[:, 8 * b + k], p.gy_lo[:, 8 * b + k],
                                 k == 0 and b == 0, k == UNIT - 1 and b == 1)
            ins.then_inc(p.sem["unit_done"], 1)


def sz_sum(p, pe, st, t):
    pe.wait_ge(p.sem["sz_sq"], st.at("sz_sq") + t + 1)
    p.nc.tensor.matmul(p.psum[0:16, 6, 0:T], p.pick("row", t // 4), p.tmp[:, t % 8], start=t == 0, stop=t == N_X - 1,
                       skip_group_check=True).then_inc(p.sem["sz_summed"], 1)


def ssd_out_scalar(p, act, st):
    a, u0, f = st.at, st.unit0, p.nc.scalar.activation
    for t in range(N_X):
        split_hi(p, act, u0 + t + 2)
        act.wait_ge(p.sem["unit_done"], u0 + t + 1)
        if t >= 2:
            act.wait_ge(p.sem["sz_gated"], a("sz_gated") + t - 1)
        f(p.sz[:, t % 2], p.psum[:, t % 2, 0:T], ACT.Silu).then_inc(p.sem["gate_act"], 1)
    split_hi(p, act, u0 + N_X + 2)
    act.wait_ge(p.sem["sz_var"], a("sz_var") + 2)
    f(p.rinv16[0:16], p.rinv16[0:16], ACT.Sqrt).then_inc(p.sem["sz_root"], 1)
    for t in range(N_X):
        act.wait_ge(p.sem["gy_scaled"], a("gy_scaled") + t + 1)
        f(p.gy_hi[:, t], p.sxbc(t), ACT.Copy).then_inc(p.sem["gy_rounded"], 1)
        if t < 2:
            split_hi(p, act, u0 + N_X + 3 + t)
    for t in range(2, N_X):
        split_hi(p, act, u0 + N_X + 3 + t)


def ssd_out_gpsimd(p, pool, st):
    a = st.at
    for t in range(N_X):
        pool.wait_ge(p.sem["sz_gated"], a("sz_gated") + t + 1)
        if t >= 8:
            pool.wait_ge(p.sem["sz_summed"], a("sz_summed") + t - 7)
        p.nc.gpsimd.tensor_tensor(p.tmp[:, t % 8], p.sxbc(t), p.sxbc(t), ALU.mult).then_inc(p.sem["sz_sq"], 1)


def ssd_out_vector(p, dve, st):
    a, u0, v, x = st.at, st.unit0, p.nc.vector, st.x(p)
    for t in range(N_X):
        split_lo(p, dve, u0 + t + 2)
        dve.wait_ge(p.sem["gate_act"], a("gate_act") + t + 1)
        v.tensor_tensor(p.sxbc(t), p.sxbc(t), p.sz[:, t % 2], ALU.mult).then_inc(p.sem["sz_gated"], 1)
    split_lo(p, dve, u0 + N_X + 2)
    dve.wait_ge(p.sem["sz_summed"], a("sz_summed") + N_X)
    v.tensor_scalar(p.rinv16[0:16], p.psum[0:16, 6, 0:T], 1.0 / 512, EPS, ALU.mult, ALU.add).then_inc(p.sem["sz_var"], 1)
    dve.wait_ge(p.sem["sz_var"], a("sz_var") + 1)
    v.reciprocal(p.rinv16[0:16], p.rinv16[0:16]).then_inc(p.sem["sz_var"], 1)
    gain = st.par(p, "norm_g")

    def low(t):
        dve.wait_ge(p.sem["gy_rounded"], a("gy_rounded") + t + 1)
        v.tensor_tensor(p.gy_lo[:, t], p.sxbc(t), p.gy_hi[:, t].bitcast(F32), ALU.subtract).then_inc(p.sem["gy_split"], 1)

    for t in range(N_X):
        dve.wait_ge(p.sem["sz_rinv"], a("sz_rinv") + t // 4 + 1)
        v.scalar_tensor_tensor(
            p.sxbc(t), p.sxbc(t), gain[:, t : t + 1], p.psum[:, t // 4, 0:T], ALU.mult, ALU.mult
        ).then_inc(p.sem["gy_scaled"], 1)
        if t:
            low(t - 1)
        if t % 8 == 7:
            split_lo(p, dve, u0 + N_X + 3 + t // 8)
    low(N_X - 1)
    for t in range(2, N_X):
        split_lo(p, dve, u0 + N_X + 3 + t)
        if t % 2:
            out_x(p, dve, st, x, t // 2 - 1)
    out_x(p, dve, st, x, KD - 1)


def out_x(p, dve, st, x, m):
    dve.wait_ge(p.sem["unit_done"], st.unit0 + N_X + 1 + 2 * m + 2)
    p.nc.vector.scalar_tensor_tensor(
        x[:, m], p.psum[:, 4 + m % 2, 0:T], p.mod_g[:, 1, m : m + 1], x[:, m], ALU.mult, ALU.add
    ).then_inc(p.sem["x_ready"], 1)




def pool_tensor(p, pe, st):
    a, u0, mm = st.at, st.unit0, p.nc.tensor.matmul
    pe.wait_ge(p.sem["h_whole"], a("h_whole") + 1)
    turn_tiles(p, pe, st, [(p.h_f32[:, 2 * i], p.h_f32[:, 2 * i + 1]) for i in range(4)], "sturned", "sturn_out")
    pe.wait_ge(p.sem["sturn_out"], a("sturn_out") + 4)
    pe.wait_ge(p.sem["means_loaded"], 16)
    for t in range(KD):
        for c in range(2):
            ins = mm(p.psum[:, 4 + t % 4, 0:T], p.h_tok[:, c, t * P : t * P + P], p.means[:, c, t // 2],
                     start=c == 0, stop=c == 1)
        ins.then_inc(p.sem["pooled"], 1)
        if t >= 3:
            pe.wait_ge(p.sem["pool_split"], a("pool_split") + t - 2)
    pe.wait_ge(p.sem["pool_split"], a("pool_split") + KD)
    for t in range(KD):
        g, b = t // 2, t % 2
        s = u0 + g // 2
        if t % 4 == 0:
            pe.wait_ge(p.sem["lo_ready"], s + 1)
        if t >= 4:
            pe.wait_ge(p.sem["x_ready"], a("x_ready") + t - 3)
        for k in range(2):
            ins = three_pass(p, p.psum[:, PROJ_BANKS[t % 4], 0:T], s % SLOTS, 4 * (g % 2) + 2 * b + k,
                             p.p_hi[:, 2 * g + k], p.p_lo[:, 2 * g + k], k == 0, k == 1)
        if t % 4 == 3:
            ins.then_inc(p.sem["unit_done"], 1)
        else:
            ins.then_inc(p.sem["pool_out"], 1)


def pool_scalar(p, act, st):
    a, u0, f = st.at, st.unit0, p.nc.scalar.activation
    for i in range(4):
        act.wait_ge(p.sem["sturned"], a("sturned") + i + 1)
        for c in range(2):
            ins = f(p.h_tok[:, c, 2 * i * P : 2 * i * P + 2 * P].rearrange("p (j n) -> p j n", j=2),
                    p.psum[:, i % 4].rearrange("p (j c n) -> p j c n", j=2, c=2)[:, :, c], ACT.Copy)
        ins.then_inc(p.sem["sturn_out"], 1)
    for t in range(KD):
        act.wait_ge(p.sem["pooled"], a("pooled") + t + 1)
        f(p.p_hi[:, t], p.psum[:, 4 + t % 4, 0:T], ACT.Copy).then_inc(p.sem["pool_rounded"], 1)
    split_hi(p, act, u0 + 2)
    split_hi(p, act, u0 + 3)


def pool_vector(p, dve, st):
    a, u0, v, x = st.at, st.unit0, p.nc.vector, st.x(p)
    dve.wait_ge(p.sem["h_ready"], a("h_ready"))
    v.tensor_tensor(p.h_f32[:], p.h_hi[:].bitcast(F32), p.h_lo[:].bitcast(F32), ALU.add).then_inc(p.sem["h_whole"], 1)
    for t in range(KD):
        dve.wait_ge(p.sem["pool_rounded"], a("pool_rounded") + t + 1)
        v.tensor_tensor(p.p_lo[:, t], p.psum[:, 4 + t % 4, 0:T], p.p_hi[:, t].bitcast(F32), ALU.subtract).then_inc(
            p.sem["pool_split"], 1)
    v.tensor_tensor(p.mod_g[:, 1], p.mod_g[:, 1], st.par(p, "pool_scale"), ALU.mult).then_inc(p.sem["pool_factor"], 1)
    dve.wait_ge(p.sem["pool_factor"], a("pool_factor") + 1)
    bias = st.par(p, "pool_b")
    for t in range(KD):
        if t % 4 == 3:
            dve.wait_ge(p.sem["unit_done"], u0 + t // 4 + 1)
        else:
            dve.wait_ge(p.sem["pool_out"], a("pool_out") + t - t // 4 + 1)
        v.tensor_scalar(
            p.sz[:, t % 2], p.psum[:, PROJ_BANKS[t % 4], 0:T], bias[:, t : t + 1], p.mod_g[:, 1, t : t + 1], ALU.add, ALU.mult
        ).then_inc(p.sem["pool_step"], 1)
        dve.wait_ge(p.sem["pool_step"], a("pool_step") + t + 1)
        v.tensor_tensor(x[:, t], x[:, t], p.sz[:, t % 2], ALU.add).then_inc(p.sem["x_ready"], 1)
    split_lo(p, dve, u0 + 2)
    split_lo(p, dve, u0 + 3)




def final_scalar(p, act, st):
    a, f = st.at, p.nc.scalar.activation
    for m in range(KD):
        act.wait_ge(p.sem["x_ready"], a("x_ready") - KD + m + 1)
        f(p.tmp[:, m], p.x[:, m], ACT.Square).then_inc(p.sem["sq_ready"], 1)
    act.wait_ge(p.sem["norm_step"], a("norm_step") + 2)
    f(p.rinv[:], p.var[:], ACT.Sqrt).then_inc(p.sem["rinv_ready"], 1)


def final_vector(p, dve, st):
    a, v = st.at, p.nc.vector
    dve.wait_ge(p.sem["sum_done"], a("sum_done") + 1)
    v.tensor_scalar(p.var[:], p.psum[:, 2, 0:T], 1.0 / D, EPS, ALU.mult, ALU.add).then_inc(p.sem["norm_step"], 1)
    dve.wait_ge(p.sem["norm_step"], a("norm_step") + 1)
    v.reciprocal(p.var[:], p.var[:]).then_inc(p.sem["norm_step"], 1)
    dve.wait_ge(p.sem["rinv_ready"], a("rinv_ready") + 1)
    for m in range(KD):
        v.scalar_tensor_tensor(
            p.tmp[:, m], p.x[:, m], st.par(p, "final_g")[:, m : m + 1], p.rinv[:], ALU.mult, ALU.mult
        ).then_inc(p.sem["y_normed"], 1)


final_tensor = norm_tensor




def fetch_scalar(p, act, st):
    if st.at("x_ready"):
        act.wait_ge(p.sem["x_ready"], st.at("x_ready"))
    if st.what == "ctx":
        act.dma_start(p.ctx_x[:], p.dram["ctx"]).then_inc(p.sem["ctx_loaded"], 16)
    else:
        act.dma_start(p.means[:], p.dram["means"]).then_inc(p.sem["means_loaded"], 16)


STAGES = {
    "tensor": dict(ada=ada_tensor, norm=norm_tensor, ffn=ffn_tensor, project=project_tensor, gdn=gdn_tensor,
                   up=up_tensor, attn=attn_tensor, gates=gates_tensor, ssd_in=ssd_in_tensor, state=state_tensor,
                   mix=mix_tensor, ssd_out=ssd_out_tensor, pool=pool_tensor, final=final_tensor),
    "scalar": dict(norm=norm_scalar, ffn=ffn_scalar, project=project_scalar, gdn=gdn_scalar, up=up_scalar,
                   attn=attn_scalar, gates=gates_scalar, ssd_in=ssd_in_scalar, state=state_scalar, mix=mix_scalar,
                   ssd_out=ssd_out_scalar, pool=pool_scalar, final=final_scalar, fetch=fetch_scalar),
    "vector": dict(ada=ada_vector, norm=norm_vector, ffn=ffn_vector, project=project_vector, gdn=gdn_vector,
                   up=up_vector, attn=attn_vector, gates=gates_vector, ssd_in=ssd_in_vector, state=state_vector,
                   mix=mix_vector, ssd_out=ssd_out_vector, pool=pool_vector, final=final_vector),
    "gpsimd": dict(ada=ada_gpsimd, project=project_gpsimd, up=up_gpsimd, ssd_in=ssd_in_gpsimd, mix=mix_gpsimd, ssd_out=ssd_out_gpsimd),
}


def second_plan():
    more = dict(block=2, layer=0, gate_add=0.0, gate_scale=(0.5, 1.0, 0.5))
    ctx = dict(on_ctx=True, **more)
    stages = [Stage("ada", vec=2, n_vec=5, n_prep=3, **more)]
    stages += [Stage(kind, n=n, n_conv=20, **ctx) for kind, n in (
        ("norm", 0), ("ffn", 0), ("norm", 1), ("ssd_in", 1), ("state", 1))]
    stages.append(Stage("ada", vec=1, n_vec=9, n_prep=6, **more))
    stages += [Stage(kind, n=n, n_conv=24, **more) for kind, n in (
        ("norm", 0), ("ffn", 0), ("norm", 1), ("ssd_in", 1), ("mix", 1), ("ssd_out", 1))]
    stages.append(Stage("fetch", what="means", **more))
    stages += [Stage(kind, n=2, **more) for kind in ("norm", "ffn")]
    more["layer"] = 1
    stages.append(Stage("ada", vec=1, n_vec=9, n_prep=6, **more))
    stages += [Stage(kind, n=n, **more) for kind, n in (
        ("norm", 0), ("ffn", 0), ("norm", 1), ("pool", 1), ("norm", 2), ("ffn", 2), ("final", 0))]
    return stages


def plan():
    stages = []
    for layer in range(DEPTH):
        more = dict(block=1, layer=layer)
        stages.append(Stage("ada", vec=0, n_vec=9, n_prep=6, gate_add=1.0, gate_scale=(0.5, 0.5, 0.5), **more))
        stages += [Stage(kind, n=n, **more) for kind, n in (
            ("norm", 0), ("ffn", 0), ("norm", 1), ("project", 1), ("gdn", 1), ("up", 1), ("attn", 1), ("gates", 1),
            ("norm", 2), ("ffn", 2))]
    last = max(i for i, st in enumerate(stages) if st.kind == "gates")
    stages.insert(last + 1, Stage("fetch", what="ctx", block=1, layer=1))
    return stages + second_plan()


def build(nc, dram, out, stages):
    with ExitStack() as ctx:
        p = Program(nc, ctx, stages, dram)
        loads = [(p.const[:], dram["const"]), (p.c_in[:], dram["c"]), (p.par1[:], dram["par1"]), (p.par2[:], dram["par2"]), (p.x[:], dram["x"]), (p.positions[:], dram["positions"])]
        n_loads = p.n_loads = 16 * len(loads)
        block = ctx.enter_context(nc.Block())

        def walk(eng, which):
            for st in stages:
                if st.kind in STAGES[which]:
                    STAGES[which][st.kind](p, eng, st)

        @block.sync
        def _(sp):
            for to, src in loads:
                sp.dma_start(to, src).then_inc(p.sem["loaded"], 16)
            load_units(p, sp)
            if "x_ready" in p.total:
                sp.wait_ge(p.sem["x_ready"], p.total["x_ready"])
            if "y_normed" in p.total:
                sp.wait_ge(p.sem["y_normed"], p.total["y_normed"])
            sp.dma_start(out, (p.tmp if "y_normed" in p.total else p.x)[:]).then_inc(p.sem["stored"], 16)
            sp.wait_ge(p.sem["stored"], 16)

        @block.gpsimd
        def _(pool):
            nc.gpsimd.memset(p.rows[:], 0.0).then_inc(p.sem["rows_cleared"], 1)
            pool.wait_ge(p.sem["loaded"], n_loads)
            walk(pool, "gpsimd")

        @block.scalar
        def _(act):
            act.wait_ge(p.sem["loaded"], n_loads)
            act.wait_ge(p.sem["rows_cleared"], 1)
            nc.scalar.activation(p.c_act[:], p.c_in[:], ACT.Silu).then_inc(p.sem["c_ready"], 1)
            trig_scalar(p, act)
            split_hi(p, act, 0)
            split_hi(p, act, 1)
            walk(act, "scalar")

        @block.vector
        def _(dve):
            dve.wait_ge(p.sem["loaded"], n_loads)
            dve.wait_ge(p.sem["rows_cleared"], 1)
            trig_vector(p, dve)
            split_lo(p, dve, 0)
            split_lo(p, dve, 1)
            walk(dve, "vector")

        @block.tensor
        def _(pe):
            pe.wait_ge(p.sem["loaded"], n_loads)
            walk(pe, "tensor")


def gather_inputs(i):
    layers = range(DEPTH)
    f = lambda name: np.asarray(i[name])
    units = []
    for l in layers:
        units += ffn_units(f("ffn1_w1")[l], f("ffn1_w3")[l], f("ffn1_w2")[l])
        units += first_mix_units(*(f(n)[l] for n in (
            "w_in", "mla_w_q_up", "mla_w_kv_up", "w_branch_a", "w_branch_b", "w_out")))
        units += ffn_units(f("ffn2_w1")[l], f("ffn2_w3")[l], f("ffn2_w2")[l])
    g = lambda name: np.asarray(i[name + "_2"])
    ffn = lambda l, n: ffn_units(g("ffn_w_gate")[l, n], g("ffn_w_up")[l, n], g("ffn_w_down")[l, n])
    w_in = g("ssd_w_in")[0]
    units += ffn(0, 0) + ssd_in_units(w_in, True) + ffn(0, 0) + ssd_in_units(w_in, False)
    units += ssd_out_units(w_in, g("ssd_w_out")[0]) + ffn(0, 1) + ffn(1, 0) + pool_units(g("pool_w")[0]) + ffn(1, 1)
    stream = np.concatenate(units, 0)
    stream = stream.reshape(-1, 2, P, UNIT * P).transpose(0, 2, 1, 3).reshape(-1, P, 2 * UNIT * P)
    ada = np.concatenate([ada_blocks(f("ada_w")[l]) for l in layers] + [
        ada_blocks(g("ada_w")[0])[: 5 * KD // 2], ada_blocks(g("ada_w")[0]), ada_blocks(g("ada_w")[1])], 0)
    par1 = np.stack([np.concatenate([
        columns(f("ada_b")[l]), columns(f("norm_ffn1")[l]), columns(f("norm_mix")[l]), columns(f("norm_ffn2")[l]),
        f("gdn_conv")[l].reshape(4, 24, P).transpose(2, 1, 0).reshape(P, 96),
        f("gdn_out_gain")[l][:, None], columns(f("mla_q_lat_gain")[l]), columns(f("mla_kv_lat_gain")[l]),
        f("mla_q_norm")[l][:P, None], np.tile(f("mla_q_norm")[l][P:], 2)[:, None],
        f("mla_k_norm")[l][:P, None], np.tile(f("mla_k_norm")[l][P:], 2)[:, None],
        rows_at((32, f("gdn_a_log")[l])), rows_at((32, f("gdn_dt_bias")[l])),
    ], 1) for l in layers], 1)
    par2 = np.stack([np.concatenate([
        columns(g("ada_b")[l]), columns(g("norm_g")[l].reshape(-1)),
        g("ssd_conv_w")[0].reshape(5, 24, P).transpose(2, 1, 0).reshape(P, 120), columns(g("ssd_conv_b")[0]),
        columns(np.repeat(g("ssd_d")[0], 64)), columns(g("ssd_norm_g")[0]),
        rows_at((0, g("ssd_a_log")[0].reshape(-1))), rows_at((0, g("ssd_dt_bias")[0].reshape(-1))),
        columns(g("pool_b")[0].reshape(-1)), columns(g("pool_scale")[0]), columns(g("final_g")),
    ], 1) for l in layers], 1)
    c = np.stack([columns(f("c")[0]), columns(f("c_2")[0]), columns(f("c_ctx_2")), columns(f("c_ctx_2"))], 1)
    tokens = lambda x: x.T.reshape(KD, P, T).transpose(1, 0, 2)
    return dict(stream=stream, ada=ada, par1=par1, par2=par2, c=c, x=tokens(f("x")[0]), ctx=tokens(g("ctx")[0]), means=window_means(), const=constants(),
                positions=np.broadcast_to(f("positions").astype(np.int32), (P, T)))


def kernel(**inputs):
    from concourse import bacc
    from concourse.bass_utils import run_bass_kernel_spmd

    arrays = {k: np.ascontiguousarray(v) for k, v in gather_inputs(inputs).items()}
    nc = bacc.Bacc("TRN2", target_bir_lowering=False, num_devices=1)
    dram = {
        k: nc.dram_tensor(k + "_dram", v.shape, mybir.dt.from_np(v.dtype), kind="ExternalInput").ap()
        for k, v in arrays.items()
    }
    out = nc.dram_tensor("out_dram", (P, KD, T), F32, kind="ExternalOutput").ap()
    build(nc, dram, out, plan())
    r = run_bass_kernel_spmd(nc, [{k + "_dram": v for k, v in arrays.items()}], core_ids=[0])
    y = r.results[0]["out_dram"]
    return y.transpose(1, 0, 2).reshape(D, T).T.reshape(1, T, D)
```

```python
import math
from contextlib import ExitStack

import numpy as np

import concourse.bass as bass
from concourse import mybir
from concourse.alu_op_type import AluOpType as ALU

ACT = mybir.ActivationFunctionType
F32, F32R, I32 = mybir.dt.float32, mybir.dt.float32r, mybir.dt.int32
AX = mybir.AxisListType

P = 128
T = 256
D = 1024
KD = D // P
FT = 2816 // P
EPS = 1e-6
N_MOD = 9
DEPTH = 2

RAW = 4
UNIT = 8
SLOTS = 4
ADA_SLOTS = 4

HEADS = 8
GROUP = 4
LEVELS = 6
NEG = -1.0e30
Q_TILES, K_TILES = 8, 8
LAT_Q, LAT_KV = 3, 2
ROPE = 64

CONST = {}
_at = 0
for _name, _n in (
    ("ident", P), ("ones", P), ("neg", 3 * P), ("first_t", 2 * P), ("masks", LEVELS * P), ("rot", P),
    ("attn", 3 * P), ("inv_freq", 1), ("row", 31), ("row_0", 31), ("row_1", 31), ("half_0", 1), ("half_1", 1), ("q_scale", 1),
):
    CONST[_name] = (_at, _n)
    _at += _n
N_CONST = _at

PAR1 = {}
_at = 0
for _name, _n in (
    ("ada_b", N_MOD * KD), ("gain", 3 * KD), ("conv", 24 * 4), ("out_gain", 1), ("lat_gain", 5),
    ("q_norm", 2), ("k_norm", 2), ("a_log", 1), ("dt_bias", 1),
):
    PAR1[_name] = (_at, _n)
    _at += _n
N_PAR1 = _at

PAR2 = {}
_at = 0
for _name, _n in (
    ("ada_b", N_MOD * KD), ("gain", 3 * KD), ("conv", 24 * 5), ("conv_b", 24), ("d_skip", 16), ("norm_g", 16),
    ("a_log", 1), ("dt_bias", 1), ("pool_b", KD), ("pool_scale", KD), ("final_g", KD),
):
    PAR2[_name] = (_at, _n)
    _at += _n
N_PAR2 = _at

WINDOWS = (2, 4, 8, 16)
GRID_W = 64


def constants():
    c = np.zeros((P, N_CONST), np.float32)
    i = np.arange(P)
    put = lambda name, a: c.__setitem__((slice(None), slice(CONST[name][0], sum(CONST[name]))), a)
    put("ident", np.eye(P))
    put("ones", 1.0)
    put("neg", np.concatenate([
        np.where(i[None, :] >= i[:, None], 0.0, NEG), np.zeros((P, P)), np.where(i[None, :] <= i[:, None], 0.0, NEG)], 1))
    pair = (i[None, :] // 2 == i[:, None] // 2) & (i[None, :] > i[:, None])
    put("first_t", np.tile(pair, (1, 2)))
    masks = []
    for level in range(LEVELS):
        s = 2 << level
        masks.append((i[:, None] // (2 * s) == i[None, :] // (2 * s)) & (i[:, None] // s > i[None, :] // s))
    put("masks", np.concatenate(masks, 1))
    rot = np.zeros((P, P))
    for b in (0, ROPE):
        for r in range(ROPE // 2):
            rot[b + ROPE // 2 + r, b + r] = -1.0
            rot[b + r, b + ROPE // 2 + r] = 1.0
    put("rot", rot)
    diag = np.where(i[None, :] <= i[:, None], 0.0, NEG)
    put("attn", np.concatenate([diag, np.zeros((P, P)), diag], 1))
    put("inv_freq", (np.float32(10000.0) ** (-np.arange(32, dtype=np.float32) / 32))[i % 32][:, None])
    put("q_scale", np.where(i < HEADS, 1.0 / P, 1.0)[:, None])
    c[:, CONST["row"][0] + 15] = 1.0
    for b in range(2):
        half = (i // ROPE == b).astype(np.float32)
        c[:, CONST[f"row_{b}"][0] + 15] = half
        put(f"half_{b}", half[:, None])
    return c


def window_means():
    def box(n, w):
        i = np.arange(n)
        lo, hi = np.maximum(i - w // 2, 0), np.minimum(i + w - w // 2, n)
        return ((i[:, None] >= lo) & (i[:, None] < hi)).astype(np.float64)

    out = []
    for w in WINDOWS:
        rows, cols = box(T // GRID_W, w), box(GRID_W, w)
        m = np.kron(rows / rows.sum(0), cols / cols.sum(0)) - np.eye(T)
        out.append(m.reshape(2, P, T))
    return np.stack(out).transpose(2, 1, 0, 3).astype(np.float32)




def tiles(w):
    k, m = w.shape
    return w.reshape(k // P, P, m // P, P).transpose(0, 2, 1, 3)


def by_tile(w):
    return tiles(w).transpose(1, 2, 0, 3)


def by_row(w):
    return tiles(w).transpose(0, 2, 1, 3)


def ffn_units(w1, w3, w2):
    up = np.stack([by_tile(w1), by_tile(w3)], 1).reshape(-1, P, UNIT, P)
    down = tiles(w2).transpose(1, 0, 2, 3).reshape(FT, UNIT, P, P).transpose(0, 2, 1, 3)
    return [up, down]


def columns(v):
    return v.reshape(-1, P).T


def rows_at(*parts):
    c = np.zeros((P, 1), np.float32)
    for at, v in parts:
        c[at : at + v.shape[0], 0] = v
    return c


def first_mix_units(w_in, q_up, kv_up, branch_a, branch_b, w_out):
    at = np.cumsum([0, 3072, 1024, 8, 8, 384, 256, 64, 1024, 1024])
    part = [w_in[:, a:b] for a, b in zip(at[:-1], at[1:])]
    qkv, z, b_raw, a_raw, q_lat, kv_lat, k_pe, gate_a, gate_b = part
    pad = lambda n: np.zeros((D, n), np.float32)
    ba = np.concatenate([b_raw, pad(24), a_raw, pad(88)], 1)
    proj = np.concatenate([qkv, z, q_lat, kv_lat, k_pe, k_pe, ba, pad(P)], 1)
    out = [by_tile(proj)]
    q = q_up.reshape(384, HEADS, 192)
    q = np.concatenate([q[:, :, :P].reshape(384, -1), q[:, :, P:].reshape(384, -1)], 1)
    q = tiles(np.concatenate([q, np.zeros((P, q.shape[1]), np.float32)], 0))
    out.append(q.transpose(1, 0, 2, 3).reshape(6, 8, P, P).transpose(0, 2, 1, 3))
    kv = kv_up.reshape(256, HEADS, 256)
    k = tiles(kv[:, :, :P].reshape(256, -1)).transpose(1, 0, 2, 3).reshape(2, 8, P, P)
    out.append(k.transpose(0, 2, 1, 3))
    out.append(by_row(kv[:, :, P:].reshape(256, -1)))
    gates = np.stack([by_tile(gate_a), by_tile(branch_a), by_tile(gate_b), by_tile(branch_b)], 1)
    out += [gates.reshape(-1, P, UNIT, P), by_tile(w_out)]
    return out


def ssd_in_units(w_in, context):
    xbc = w_in[:, 2048:5120][:, : (20 if context else 24) * P]
    dt = np.concatenate([w_in[:, 5120:5184], np.zeros((D, (2 if context else 1) * P - 64), np.float32)], 1)
    return [by_tile(np.concatenate([xbc, dt], 1))]


def ssd_out_units(w_in, w_out):
    out = tiles(w_out).transpose(1, 0, 2, 3).reshape(KD * 2, UNIT, P, P).transpose(0, 2, 1, 3)
    return [by_tile(np.concatenate([w_in[:, :2048], np.zeros((D, P), np.float32)], 1)), out]


def pool_units(w):
    w = w.reshape(4, 2, P, 2, P).transpose(0, 3, 1, 2, 4)
    return [w.reshape(2, UNIT, P, P).transpose(0, 2, 1, 3)]


def ada_tiles(w):
    return w.T.reshape(-1, P, D)




class Stage:

    def __init__(self, kind, block, layer, n=0, on_ctx=False, n_conv=0, vec=0, n_vec=3, ada0=0, ada_n=0,
                 gate_add=0.0, gate_scale=None, what=None):
        self.kind, self.block, self.layer = kind, block, layer
        self.n = n
        self.on_ctx = on_ctx
        self.n_conv = n_conv
        self.vec, self.ada0, self.ada_n = vec, ada0, ada_n
        self.n_vec = n_vec
        self.gate_add, self.gate_scale = gate_add, gate_scale
        self.what = what

    def x(self, p):
        return p.ctx_x if self.on_ctx else p.x

    def par(self, p, name):
        if self.block == 1:
            at, n = PAR1[name]
            return p.par1[:, self.layer, at : at + n]
        at, n = PAR2[name]
        return p.par2[:, self.layer, at : at + n]

    def at(self, name):
        return self.base.get(name, 0)


UNITS = {"ffn": 2 * FT + FT, "project": 40, "up": 10, "gates": 40, "ssd_out": 33, "pool": 2}


def units_of(st):
    if st.kind == "ssd_in":
        return st.n_conv + (2 if st.on_ctx else 1)
    return UNITS.get(st.kind, 0)


def signals(st):
    kind = st.kind
    n = {}
    if kind == "prep":
        n = dict(mod_prep=st.n_vec)
    if kind == "norm":
        n = dict(sq_ready=KD, sum_done=1, norm_step=2, root_ready=1, rinv_ready=1, scaled=KD, h_rounded=KD, h_ready=KD)
    if kind == "ffn":
        n = dict(gate_act=FT, mid_step=2 * FT, mid_ready=FT, x_ready=KD)
    if kind == "project":
        n = dict(proj_out=40, conv_step=2 * 24, conv_done=24, act_done=24, sq_done=16, sums_done=1,
                 inv_step=2, inv_ready=1, unit_len=1, len_row=16, normed=16, conv_pad=4)
        n["proj_out"] = 39
    if kind == "gdn":
        n = dict(gdn_step=13, rows_ready=2, cols_ready=2, gate_fn=5, exp_cum=1, cols_done=1, rows_done=8,
                 kb_ready=8, exponent_ready=16, row_exp=8, decay_ready=8, pairs_done=8, pairs_used=16,
                 q_dec_ready=8, inv_grown=8 * (LEVELS + 1), turned_done=8, turned_used=8, first_turned=8,
                 first_both=8, lp_done=8 * LEVELS, lq_done=8 * LEVELS, new_ready=8 * LEVELS, wu_done=8,
                 w_ready=8, v0_ready=8, state_done=8, state_ready=8, v1_done=8, v1_ready=8, o_done=8,
                 out_ready=8, o_sum=1, o_inv=1, o_sq=8, o_root=1, len_row=8, o_gated=8, oa_ready=8)
    if kind == "up":
        n = dict(lat_sq=5, kpe_sq=1, up_out=20, up_summed=20, up_sq=20, lat_sum=2, lat_ready=5, lat_var=4,
                 lat_root=2, lat_scaled=5, lat_rounded=5, rope_in=5, rope_out=5, rope_step=10, rope_turned=5,
                 rinv_rows=1, values_out=4, head_normed=16, head_rinv=16, head_var=2)
    if kind == "attn":
        n = dict(masked=8, scored=8, weighed=8, weights_out=8, weights_turned=8, ob_out=8, mixed=8,
                 max_step=16, max_ready=8, exped=8, den_ready=8)
    if kind == "gates":
        n = dict(gate_tanh=16, y_step=16, o_split=2, o_rounded=2, y_split=2, y_rounded=2, y_ready=8, x_ready=8)
    if kind == "ssd_in":
        k = st.n_conv
        n = dict(proj_out=k + 1, conv_step=3 * k, conv_done=k, act_done=k, conv_pad=4,
                 gate_fn=5 if st.on_ctx else 4, dt_step=6 if st.on_ctx else 5, dt_ready=1)
    if kind == "state":
        n = dict(sturned=10, sturn_out=10, cols_done=1, cols_ready=1, xw_ready=4, state_sum=8, state_out=8)
    if kind == "mix":
        n = dict(sturned=8, sturn_out=8, cols_done=1, cols_ready=1, cb_done=4, cb_out=4, g_row=64, sx_ready=64,
                 sx_exp=64, g_exp=64, c_dec=64, sw_ready=64, sy_part=64, sy_out=16)
    if kind == "ssd_out":
        n = dict(gate_act=16, sz_gated=16, sz_sq=16, sz_summed=16, sz_var=2, o_root=1, len_row=4, gy_scaled=16,
                 gy_rounded=16, gy_split=16, x_ready=8)
    if kind == "pool":
        n = dict(h_whole=1, sturned=4, sturn_out=4, pooled=8, pool_rounded=8, pool_split=8, pool_out=6,
                 pool_factor=1, pool_step=8, x_ready=8)
    if kind == "final":
        n = dict(sq_ready=8, sum_done=1, norm_step=2, root_ready=1, rinv_ready=1, y_normed=8)
    if st.ada_n:
        n |= dict(ada_product=st.ada_n, ada_summed=st.ada_n, c_row_full=16, c_row_ready=1)
    return n


def plan_of(stages):
    base, unit, tile = {}, 0, 0
    for st in stages:
        st.base = dict(base)
        st.unit0 = unit
        tile += st.ada_n
        unit += units_of(st)
        for name, k in signals(st).items():
            base[name] = base.get(name, 0) + k
    return unit, tile, base


class Program:

    def __init__(self, nc, ctx, stages, dram):
        self.nc, self.stages, self.dram = nc, stages, dram
        self.n_units, self.n_ada, self.total = plan_of(stages)
        self.n_blocks = self.n_units // 2
        self.ctx = ctx
        sb = lambda name, shape, dt=F32: ctx.enter_context(nc.sbuf_tensor(name, shape, dt))
        self.raw = sb("raw", [P, RAW, 2, UNIT * P])
        self.w_hi = sb("w_hi", [P, SLOTS, UNIT, P], F32R)
        self.w_lo = sb("w_lo", [P, SLOTS, UNIT, P], F32R)
        self.ada_w = sb("ada_w", [P, ADA_SLOTS, D])
        self.ada_raw = sb("ada_raw", [P, self.n_ada])
        self.x = sb("x", [P, KD, T])
        self.h_hi = sb("h_hi", [P, KD, T], F32R)
        self.h_lo = sb("h_lo", [P, KD, T], F32R)
        self.tmp = sb("tmp", [P, KD, T])
        self.c_row = self.tmp[:, 0:4].rearrange("p m n -> p (m n)")
        self.rinv = sb("rinv", [P, T])
        self.var = sb("var", [P, T])
        self.mean = sb("mean", [P, 2])
        self.root = sb("root", [P, 2])
        self.const = sb("const", [P, N_CONST])
        self.par1 = sb("par1", [P, DEPTH, N_PAR1])
        self.par2 = sb("par2", [P, DEPTH, N_PAR2])
        self.scols = sb("scols", [P, 2, 2, 64])
        self.mod = sb("mod", [P, N_MOD, KD])
        self.mod_a = sb("mod_a", [P, 3, KD])
        self.mod_g = sb("mod_g", [P, 3, KD])
        self.cos = sb("cos", [P, T])
        self.sin = sb("sin", [P, T])
        self.rows = sb("rows", [P, T])
        self.rows2 = self.rinv
        self.soft = sb("soft", [P, T])
        self.exp_a = sb("exp_a", [P, 1])
        self.cols = sb("cols", [P, 2, 2, HEADS])
        self.exp_cols = sb("exp_cols", [P, HEADS])
        self.beta_exp = sb("beta_exp", [P, HEADS])
        self.mx, self.nmx, self.den, self.rden = (sb(n, [P, 2, 2]) for n in ("mx", "nmx", "den", "rden"))
        self.u_hi = self.over("u_hi", 0, [P, FT, T], F32R)
        self.u_lo = self.over("u_lo", 22528, [P, FT, T], F32R)
        self.mid = self.over("mid", 45056, [P, 2, T])
        self.gate = self.over("gate", 47104, [P, 2, T])
        self.qkv = self.over("qkv", 0, [P, 24, T])
        self.z = self.over("z", 24576, [P, HEADS, T])
        self.lat = self.over("lat", 32768, [P, 7, T])
        self.conv_in = self.over("conv_in", 39936, [P, 4, 264])
        self.inv = self.over("inv", 44160, [P, 16, T])
        self.kb = self.over("kb", 44160, [P, GROUP, T])
        self.decay = self.over("decay", 48256, [P, GROUP, T])
        self.exp_row = self.over("exp_row", 52352, [P, GROUP, P])
        self.a_t = self.over("a_t", 54400, [P, GROUP, T])
        self.qk_t = self.over("qk_t", 58496, [P, GROUP, T])
        self.v_beta = self.over("v_beta", 62592, [P, GROUP, T])
        self.k_tok = self.over("k_tok", 66688, [P, GROUP, T])
        self.w_s = self.over("w_s", 70784, [P, GROUP, T])
        self.lat_hi = self.over("lat_hi", 8192, [P, 5, T], F32R)
        self.lat_lo = self.over("lat_lo", 13312, [P, 5, T], F32R)
        self.lat_sq = self.over("lat_sq", 18432, [P, 5, T])
        self.pt = self.over("pt", 18432, [P, 2, 3 * P])
        self.kn = self.over("kn", 24576, [P, HEADS, T])
        self.qn = self.over("qn", 39936, [P, HEADS, T])
        self.qr = self.over("qr", 48128, [P, HEADS // 2, T])
        self.vt = self.over("vt", 52224, [P, 2, D])
        self.krz = self.over("krz", 60416, [P, HEADS, T])
        self.kr = self.over("kr", 68608, [P, T])
        self.work = self.over("work", 69632, [P, 2, T])
        self.rinv_lat = self.work
        self.rinv16 = self.soft
        self.sm = self.over("sm", 71680, [P, 2, 3 * P])
        self.o_lo = self.over("o_lo", 8192, [P, 16, T], F32R)
        self.o_hi = self.over("o_hi", 48128, [P, 16, T], F32R)
        self.y = self.over("y", 24576, [P, KD, T])
        self.gate_t = self.over("gate_t", 64512, [P, 2, T])
        self.ctx_x = self.over("ctx_x", 49152, [P, KD, T])
        self.xl = self.over("xl", 0, [P, 16, T])
        self.x_tok = self.over("x_tok", 16384, [P, 2, 2048])
        self.sconv_in = self.over("sconv_in", 32768, [P, 4, 264])
        self.bc = self.over("bc", 40960, [P, 8, T])
        self.b_tok = self.over("b_tok", 45056, [P, 2, 512])
        self.xw = self.over("xw", 0, [P, 2, 2048])
        self.state = self.over("state", 49152, [P, 2, 2048])
        self.cbt = self.over("cbt", 32768, [P, 4, 2, T])
        self.g_exp = self.over("g_exp", 40960, [P, 4, T])
        self.c_exp = self.over("c_exp", 71680, [P, 3, T])
        self.sw = self.over("sw", 65536, [P, 4, 3 * P])
        self.gy_hi = self.over("gy_hi", 16384, [P, 16, T], F32R)
        self.gy_lo = self.over("gy_lo", 32768, [P, 16, T], F32R)
        self.sz = self.over("sz", 65536, [P, 2, T])
        self.means = self.over("means", 49152, [P, 2, 4, T])
        self.h_f32 = self.tmp
        self.h_tok = self.over("h_tok", 0, [P, 2, D])
        self.p_hi = self.over("p_hi", 32768, [P, KD, T], F32R)
        self.p_lo = self.over("p_lo", 40960, [P, KD, T], F32R)
        self.angle = self.over("angle", 0, [P, T])
        self.positions = self.over("positions", 4 * T, [P, T], I32)
        self.inv_t = self.tmp[:].rearrange("p (i b) n -> p i b n", b=2)
        self.psum = ctx.enter_context(nc.psum_tensor("psum", [P, 8, 512], F32))
        self.sem = {}
        for name in (
            ["loaded", "tables_loaded", "stored", "trig_step", "angles_ready", "trig_done", "rows_cleared", "hi_ready", "lo_ready", "unit_done", "ctx_loaded", "means_loaded"]
            + [f"raw_full_{s}" for s in range(RAW)]
            + [f"ada_full_{s}" for s in range(ADA_SLOTS)]
            + sorted({n for st in stages for n in signals(st)})
        ):
            self.sem[name] = ctx.enter_context(nc.semaphore(name))

    def over(self, name, offset, shape, dt=F32):
        if not offset:
            with self.nc.sbuf_tensor(name, shape, dt) as t:
                return t
        with self.nc.sbuf_tensor(name + "_before", [P, offset // 4], F32):
            with self.nc.sbuf_tensor(name, shape, dt) as t:
                return t

    def c(self, name):
        at, n = CONST[name]
        return self.const[:, at : at + n]

    def pick(self, name, t):
        at = CONST[name][0]
        return self.const[:, at + 15 - t : at + 31 - t]

    def sxbc(self, t):
        return self.xl[:, t] if t < 16 else self.bc[:, t - 16]

    def up_tile(self, j):
        if j < 8:
            return self.qn[:, j]
        return self.qr[:, j - 8] if j < 12 else self.kn[:, j - 12]


def groups(eng, n, per, body):
    whole = n // per
    for c in range(per):
        body(0, c)
    if whole > 1:
        with eng.Fori(1, whole) as g:
            for c in range(per):
                body(g, c)
    for c in range(n - whole * per):
        body(whole, c)




def split_hi(p, act, s, g=0):
    if isinstance(g, int):
        s, g = s + 8 * g, 0
        if s >= p.n_units:
            return
    slot, turn = (s // 2) % RAW, (s // 2) // RAW
    act.wait_ge(p.sem[f"raw_full_{slot}"], g * 16 + (turn + 1) * 16)
    if not isinstance(g, int) or s >= SLOTS:
        act.wait_ge(p.sem["unit_done"], g * 8 + (s - SLOTS + 1))
    p.nc.scalar.activation(
        p.w_hi[:, s % SLOTS].rearrange("p k m -> p (k m)"), p.raw[:, slot, s % 2], ACT.Copy
    ).then_inc(p.sem["hi_ready"], 1)


def split_lo(p, dve, s, g=0):
    if isinstance(g, int):
        s, g = s + 8 * g, 0
        if s >= p.n_units:
            return
    slot = (s // 2) % RAW
    dve.wait_ge(p.sem["hi_ready"], g * 8 + (s + 1))
    p.nc.vector.tensor_tensor(
        p.w_lo[:, s % SLOTS].rearrange("p k m -> p (k m)"), p.raw[:, slot, s % 2],
        p.w_hi[:, s % SLOTS].rearrange("p k m -> p (k m)").bitcast(F32), ALU.subtract,
    ).then_inc(p.sem["lo_ready"], 1)


def load_units(p, sp):
    w = p.dram["stream"]

    def load(g, c):
        if not isinstance(g, int) or g > 0:
            sp.wait_ge(p.sem["lo_ready"], g * (2 * RAW) + 2 * (c - RAW + 1))
        sp.dma_start(
            p.raw[:, c].rearrange("p h n -> p (h n)"), w[g * RAW + c]
        ).then_inc(p.sem[f"raw_full_{c}"], 16)

    for c in range(RAW):
        load(0, c)
    turns = p.n_blocks // RAW
    with sp.Fori(1, turns) as g:
        for c in range(RAW):
            load(g, c)
    for c in range(p.n_blocks - turns * RAW):
        load(turns, c)


def three_pass(p, out, slot, k, hi, lo, start, stop, skip=False):
    mm = p.nc.tensor.matmul
    mm(out, p.w_hi[:, slot, k], hi, start=start, stop=False, skip_group_check=skip)
    mm(out, p.w_lo[:, slot, k], hi, start=False, stop=False, skip_group_check=skip)
    return mm(out, p.w_hi[:, slot, k], lo, start=False, stop=stop, skip_group_check=skip)


def first_pair(p, pe, st, outs):
    a, u0, mm = st.at, st.unit0, p.nc.tensor.matmul
    one_bank = len(outs) == 1
    halves = [outs[0][:, 0:T], outs[0][:, T : 2 * T]] if one_bank else outs
    for b, out in enumerate(halves):
        pe.wait_ge(p.sem["lo_ready"], u0 + b + 1)
        for k in range(UNIT):
            if b == 0:
                pe.wait_ge(p.sem["h_rounded"], a("h_rounded") - KD + k + 1)
            slot = (u0 + b) % SLOTS
            start = k == 0 and not (b and one_bank)
            mm(out, p.w_hi[:, slot, k], p.h_hi[:, k], start=start, stop=False, skip_group_check=True)
            mm(out, p.w_lo[:, slot, k], p.h_hi[:, k], start=False, stop=False, skip_group_check=True)
    for b, out in enumerate(halves):
        for k in range(UNIT):
            if b == 0:
                pe.wait_ge(p.sem["h_ready"], a("h_ready") - KD + k + 1)
            ins = mm(out, p.w_hi[:, (u0 + b) % SLOTS, k], p.h_lo[:, k], start=False, stop=k == UNIT - 1,
                     skip_group_check=True)
        ins.then_inc(p.sem["unit_done"], 1)




def ada_load(p, act, s, g=0, per=4):
    if isinstance(g, int):
        s, g = s + per * g, 0
        if s >= p.n_ada:
            return
    act.dma_start(p.ada_w[:, s % ADA_SLOTS], p.dram["ada"][g * per + s]).then_inc(p.sem[f"ada_full_{s % ADA_SLOTS}"], 16)


def ada_product(p, eng, mult, s, g=0, per=4):
    slot = s % ADA_SLOTS
    eng.wait_ge(p.sem[f"ada_full_{slot}"], g * (16 * per // ADA_SLOTS) + 16 * (s // ADA_SLOTS + 1))
    mult(p.ada_w[:, slot], p.ada_w[:, slot], p.c_row, ALU.mult).then_inc(p.sem["ada_product"], 1)


def ada_sum(p, act, s, g=0, per=4):
    if isinstance(g, int):
        s, g = s + per * g, 0
    slot = s % ADA_SLOTS
    act.wait_ge(p.sem["ada_product"], g * per + (s + 1))
    act.wait_ge(p.sem["loaded"], p.n_loads)
    p.nc.scalar.activation(
        p.ada_w[:, slot], p.ada_w[:, slot], ACT.Copy, accum_out=p.ada_raw[:, bass.ds(g * per + s, 1)]
        if not isinstance(g, int) else p.ada_raw[:, s : s + 1]
    ).then_inc(p.sem["ada_summed"], 1)
    if s or not isinstance(g, int):
        act.wait_ge(p.sem["ada_summed"], g * per + s)
    ada_load(p, act, s + ADA_SLOTS - 1, g, per)


def c_row_silu(p, act, st):
    act.wait_ge(p.sem["c_row_full"], st.at("c_row_full") + 16)
    p.nc.scalar.activation(p.c_row, p.c_row, ACT.Silu).then_inc(p.sem["c_row_ready"], 1)


def head_scalar(p, act, st):
    c_row_silu(p, act, st)
    for s in range(st.ada_n):
        ada_sum(p, act, s)


def head_vector(p, dve, st):
    dve.wait_ge(p.sem["c_row_ready"], 1)
    for s in range(st.ada_n):
        ada_product(p, dve, p.nc.vector.tensor_tensor, s)


def prep_vector(p, dve, st):
    v, n, prep = p.nc.vector, st.n, st.at("mod_prep")
    k = st.n_vec * KD
    dve.wait_ge(p.sem["ada_summed"], st.ada0 + 3 * n * KD + k)
    raw = p.ada_raw[:, st.ada0 + 3 * n * KD : st.ada0 + 3 * n * KD + k]
    mod = p.mod[:, 3 * n : 3 * n + st.n_vec]
    v.tensor_tensor(
        mod.rearrange("p v m -> p (v m)"), raw, st.par(p, "ada_b")[:, 3 * n * KD : 3 * n * KD + k], ALU.add
    ).then_inc(p.sem["mod_prep"], 1)
    dve.wait_ge(p.sem["mod_prep"], prep + 1)
    v.scalar_tensor_tensor(
        p.mod_a[:, n], mod[:, 1], 1.0, st.par(p, "gain")[:, n * KD : n * KD + KD], ALU.add, ALU.mult
    ).then_inc(p.sem["mod_prep"], 1)
    if st.n_vec == 3:
        v.tensor_scalar(p.mod_g[:, n], mod[:, 2], st.gate_add, st.gate_scale[n], ALU.add, ALU.mult).then_inc(
            p.sem["mod_prep"], 1)
    dve.wait_ge(p.sem["mod_prep"], prep + st.n_vec)




def norm_gpsimd(p, pool, st):
    a, x = st.at, st.x(p)
    pool.wait_ge(p.sem["ada_product"], a("ada_product"))
    if a("h_ready"):
        pool.wait_ge(p.sem["h_ready"], a("h_ready"))
    if st.on_ctx:
        pool.wait_ge(p.sem["ctx_loaded"], 16)
    for m in range(KD):
        if a("x_ready"):
            pool.wait_ge(p.sem["x_ready"], a("x_ready") - KD + m + 1)
        p.nc.gpsimd.tensor_tensor(p.tmp[:, m], x[:, m], x[:, m], ALU.mult).then_inc(p.sem["sq_ready"], 1)


def norm_tensor(p, pe, st):
    a, mm, ones = st.at, p.nc.tensor.matmul, p.c("ones")[:, 0:1]
    for m in range(KD):
        pe.wait_ge(p.sem["sq_ready"], a("sq_ready") + m + 1)
        for c in range(2):
            ins = mm(p.psum[:, 2, c : c + 1], p.tmp[:, m, c * P : c * P + P], ones, start=m == 0 and c == 0,
                     stop=m == KD - 1, skip_group_check=True)
    ins.then_inc(p.sem["sum_done"], 1)
    pe.wait_ge(p.sem["root_ready"], a("root_ready") + 1)
    for c in range(2):
        ins = mm(p.psum[:, 3, c * P : c * P + P], p.root[:, c : c + 1].to_broadcast([P, P]), p.c("ident"),
                 start=True, stop=True)
    ins.then_inc(p.sem["rinv_ready"], 1)


def root_scalar(p, act, st):
    act.wait_ge(p.sem["norm_step"], st.at("norm_step") + 2)
    p.nc.scalar.activation(p.root[:], p.mean[:], ACT.Sqrt).then_inc(p.sem["root_ready"], 1)


def root_vector(p, dve, st):
    a, v = st.at, p.nc.vector
    dve.wait_ge(p.sem["sum_done"], a("sum_done") + 1)
    v.tensor_scalar(p.mean[:], p.psum[:, 2, 0:2], 1.0 / D, EPS, ALU.mult, ALU.add).then_inc(p.sem["norm_step"], 1)
    dve.wait_ge(p.sem["norm_step"], a("norm_step") + 1)
    v.reciprocal(p.mean[:], p.mean[:]).then_inc(p.sem["norm_step"], 1)
    dve.wait_ge(p.sem["rinv_ready"], a("rinv_ready") + 1)


def norm_scalar(p, act, st):
    a = st.at
    for s in range(2, 4):
        split_hi(p, act, st.unit0 + s)
    root_scalar(p, act, st)
    for m in range(KD):
        act.wait_ge(p.sem["scaled"], a("scaled") + m + 1)
        p.nc.scalar.activation(
            p.h_hi[:, m], p.tmp[:, m], ACT.Identity, bias=p.mod[:, 3 * st.n, m : m + 1]
        ).then_inc(p.sem["h_rounded"], 1)


def norm_vector(p, dve, st):
    nc, a, x = p.nc, st.at, st.x(p)
    if st.on_ctx:
        dve.wait_ge(p.sem["ctx_loaded"], 16)
    if st.unit0:
        dve.wait_ge(p.sem["unit_done"], st.unit0)
    for s in range(2, 4):
        split_lo(p, dve, st.unit0 + s)
    root_vector(p, dve, st)
    for m in range(KD):
        nc.vector.scalar_tensor_tensor(
            p.tmp[:, m], x[:, m], p.mod_a[:, st.n, m : m + 1], p.psum[:, 3, 0:T], ALU.mult, ALU.mult
        ).then_inc(p.sem["scaled"], 1)
    for m in range(KD):
        norm_lo(p, dve, st, m)


def norm_lo(p, dve, st, m):
    dve.wait_ge(p.sem["h_rounded"], st.at("h_rounded") + m + 1)
    p.nc.vector.scalar_tensor_tensor(
        p.h_lo[:, m], p.tmp[:, m], p.mod[:, 3 * st.n, m : m + 1], p.h_hi[:, m].bitcast(F32), ALU.add, ALU.subtract
    ).then_inc(p.sem["h_ready"], 1)




def ffn_tensor(p, pe, st):
    a, u0 = st.at, st.unit0

    def up(g, c):
        for b in range(2):
            s = u0 + 2 * c + b
            if b == 0 and (not isinstance(g, int) or g * 4 + c >= 2):
                pe.wait_ge(p.sem["mid_ready"], g * 4 + (a("mid_ready") + c - 1))
            pe.wait_ge(p.sem["lo_ready"], g * 8 + (s + 1))
            for k in range(UNIT):
                ins = three_pass(p, p.psum[:, c % 2, b * T : b * T + T], s % SLOTS, k,
                                 p.h_hi[:, k], p.h_lo[:, k], k == 0, k == UNIT - 1)
            ins.then_inc(p.sem["unit_done"], 1)

    first_pair(p, pe, st, [p.psum[:, 0]])
    for c in range(1, 4):
        up(0, c)
    with pe.Fori(1, FT // 4) as g:
        for c in range(4):
            up(g, c)
    for c in range(FT % 4):
        up(FT // 4, c)

    for m in range(KD):
        if m >= 4:
            pe.wait_ge(p.sem["x_ready"], a("x_ready") + m - 3)
        for k in range(FT):
            unit, chunk = divmod(m * FT + k, UNIT)
            s = u0 + 2 * FT + unit
            if chunk == 0:
                pe.wait_ge(p.sem["lo_ready"], s + 1)
            if m == 0:
                pe.wait_ge(p.sem["mid_ready"], a("mid_ready") + k + 1)
            ins = three_pass(p, p.psum[:, 4 + m % 4, 0:T], s % SLOTS, chunk, p.u_hi[:, k], p.u_lo[:, k],
                             k == 0, k == FT - 1)
            if chunk == UNIT - 1:
                ins.then_inc(p.sem["unit_done"], 1)


def ffn_scalar(p, act, st):
    a, u0, nc, s0 = st.at, st.unit0, p.nc, st.ada0
    if st.ada_n:
        act.wait_ge(p.sem["h_ready"], a("h_ready"))
        act.dma_start(p.c_row, p.dram["c"][st.vec]).then_inc(p.sem["c_row_full"], 16)

    def up(g, c):
        if c or not isinstance(g, int) or g:
            split_hi(p, act, u0 + 2 * c + 2, g)
            split_hi(p, act, u0 + 2 * c + 3, g)
        act.wait_ge(p.sem["unit_done"], g * 8 + (u0 + 2 * c + 2))
        if not isinstance(g, int) or g * 4 + c >= 2:
            act.wait_ge(p.sem["mid_step"], g * 8 + (a("mid_step") + 2 * c - 3))
        nc.scalar.activation(p.gate[:, c % 2], p.psum[:, c % 2, 0:T], ACT.Silu).then_inc(p.sem["gate_act"], 1)
        if st.ada_n and isinstance(g, int):
            if g == 0 and c == 0:
                c_row_silu(p, act, st)
            if g < 5:
                ada_sum(p, act, s0 + 4 * g + c)
            else:
                ada_sum(p, act, s0 + 20 + 2 * c)
                ada_sum(p, act, s0 + 21 + 2 * c)
        elif st.ada_n:
            ada_sum(p, act, s0 + c, g)

    groups(act, FT, 4, up)
    for s in range(2):
        split_hi(p, act, u0 + 2 * FT + 2 + s)
        if st.ada_n in (28, 44):
            ada_sum(p, act, s0 + 24 + 2 * s)
            ada_sum(p, act, s0 + 25 + 2 * s)

    def down(g, c):
        split_hi(p, act, u0 + 2 * FT + 4 + 2 * c, g)
        split_hi(p, act, u0 + 2 * FT + 5 + 2 * c, g)
        for b in range(2):
            if st.ada_n >= 40 and not (isinstance(g, int) and g == 2):
                ada_sum(p, act, s0 + st.ada_n - 16 + 2 * c + b, g, 8)

    groups(act, FT // 2 - 1, 4, down)


def ffn_gpsimd(p, pool, st):
    if st.ada_n:
        pool.wait_ge(p.sem["c_row_ready"], st.at("c_row_ready") + 1)
        with pool.Fori(0, st.ada_n // 4) as g:
            for c in range(4):
                ada_product(p, pool, p.nc.gpsimd.tensor_tensor, st.ada0 + c, g)


def ffn_vector(p, dve, st):
    a, u0, nc, x = st.at, st.unit0, p.nc, st.x(p)

    def up(g, c):
        t = g * 4 + c
        ahead = c or not isinstance(g, int) or g
        if ahead:
            split_lo(p, dve, u0 + 2 * c + 2, g)
        dve.wait_ge(p.sem["gate_act"], t + (a("gate_act") + 1))
        dve.wait_ge(p.sem["unit_done"], g * 8 + (u0 + 2 * c + 2))
        if not isinstance(g, int) or g * 4 + c >= 2:
            dve.wait_ge(p.sem["mid_ready"], t + (a("mid_ready") - 1))
        nc.vector.tensor_tensor(
            p.mid[:, c % 2], p.gate[:, c % 2], p.psum[:, c % 2, T : 2 * T], ALU.mult
        ).then_inc(p.sem["mid_step"], 1)
        if ahead:
            split_lo(p, dve, u0 + 2 * c + 3, g)
        dve.wait_ge(p.sem["mid_step"], g * 8 + (a("mid_step") + 2 * c + 1))
        nc.vector.tensor_scalar(p.u_hi[:, t], p.mid[:, c % 2], 1.0, None, ALU.mult).then_inc(p.sem["mid_step"], 1)
        dve.wait_ge(p.sem["mid_step"], g * 8 + (a("mid_step") + 2 * c + 2))
        nc.vector.tensor_tensor(
            p.u_lo[:, t], p.mid[:, c % 2], p.u_hi[:, t].bitcast(F32), ALU.subtract
        ).then_inc(p.sem["mid_ready"], 1)

    groups(dve, FT, 4, up)
    ends = [(m * FT + FT - 1) // UNIT for m in range(KD)]
    for j in range(FT):
        split_lo(p, dve, u0 + 2 * FT + 2 + j)
        for m, end in enumerate(ends):
            if j == min(end + 1, FT - 1):
                dve.wait_ge(p.sem["unit_done"], u0 + 2 * FT + end + 1)
                nc.vector.scalar_tensor_tensor(
                    x[:, m], p.psum[:, 4 + m % 4, 0:T], p.mod_g[:, st.n, m : m + 1], x[:, m], ALU.mult, ALU.add
                ).then_inc(p.sem["x_ready"], 1)



PROJ_BANKS = (0, 1, 4, 5)


def project_tensor(p, pe, st):
    a, u0, nc = st.at, st.unit0, p.nc

    def one(g, c):
        if not isinstance(g, int) or 8 * g + c >= 4:
            pe.wait_ge(p.sem["proj_out"], g * 8 + (a("proj_out") + c - 3))
        pe.wait_ge(p.sem["lo_ready"], g * 8 + (u0 + c + 1))
        for k in range(UNIT):
            ins = three_pass(p, p.psum[:, PROJ_BANKS[c % 4], 0:T], (u0 + c) % SLOTS, k,
                             p.h_hi[:, k], p.h_lo[:, k], k == 0, k == UNIT - 1)
        ins.then_inc(p.sem["unit_done"], 1)

    first_pair(p, pe, st, [p.psum[:, PROJ_BANKS[c], 0:T] for c in range(2)])
    for c in range(2, 8):
        one(0, c)
    with pe.Fori(1, 4) as g:
        for c in range(8):
            one(g, c)
    for t in range(16):
        pe.wait_ge(p.sem["sq_done"], a("sq_done") + t + 1)
        ins = nc.tensor.matmul(p.psum[0:16, 6, 0:T], p.pick("row", t), p.inv[:, t], start=t == 0, stop=t == 15)
    ins.then_inc(p.sem["sums_done"], 1)
    for c in range(8):
        for t in range(3 * (c - 3), 3 * (c - 2)) if c >= 3 else ():
            length_row(p, pe, st, t)
        one(4, c)
    length_row(p, pe, st, 15)


LENGTH_BANKS = (2, 3, 6, 7)


def length_row(p, pe, st, t):
    if t == 0:
        pe.wait_ge(p.sem["unit_len"], st.at("unit_len") + 1)
    if t >= 4:
        pe.wait_ge(p.sem["normed"], st.at("normed") + t - 3)
    p.nc.tensor.matmul(
        p.psum[:, LENGTH_BANKS[t % 4], 0:T], p.c("ident")[0:16, t : t + 1].to_broadcast([16, P]), p.rinv[0:16],
        start=True, stop=True).then_inc(p.sem["len_row"], 1)


def project_scalar(p, act, st):
    a, u0, nc = st.at, st.unit0, p.nc
    w = st.par(p, "conv").rearrange("p (t j) -> p t j", j=4)

    def head(g, c):
        if c > 1 or not isinstance(g, int) or g:
            split_hi(p, act, u0 + c + 2, g)
        act.wait_ge(p.sem["unit_done"], g * 8 + (u0 + c + 1))
        if not isinstance(g, int) or 8 * g + c >= 4:
            act.wait_ge(p.sem["conv_done"], g * 8 + (a("conv_done") + c - 3))
        act.wait_ge(p.sem["loaded"], p.n_loads)
        raw, t = p.psum[:, PROJ_BANKS[c % 4], 0:T], g * 8 + c
        nc.scalar.activation(p.qkv[:, t], raw, ACT.Copy, scale=w[:, t, 3:4])
        nc.scalar.activation(p.conv_in[:, c % 4, 3 : 3 + T], raw, ACT.Copy).then_inc(
            p.sem["proj_out"], 1)
        if not isinstance(g, int) or 8 * g + c >= 1:
            silu(g, c - 1)

    def silu(g, c):
        act.wait_ge(p.sem["conv_done"], g * 8 + (a("conv_done") + c + 1))
        act.wait_ge(p.sem["loaded"], p.n_loads)
        t = g * 8 + c
        nc.scalar.activation(p.qkv[:, t], p.qkv[:, t], ACT.Silu).then_inc(p.sem["act_done"], 1)

    for c in range(8):
        head(0, c)
    for t in range(8, 24):
        head(t // 8, t % 8)
    for t in range(24, 39):
        split_hi(p, act, u0 + t + 2)
        if t == 24:
            silu(0, 23)
        act.wait_ge(p.sem["unit_done"], u0 + t + 1)
        out, func = (p.z[:, t - 24], ACT.Silu) if t < 32 else (p.lat[:, t - 32], ACT.Copy)
        nc.scalar.activation(out, p.psum[:, PROJ_BANKS[t % 4], 0:T], func).then_inc(p.sem["proj_out"], 1)
        if t == 33:
            act.wait_ge(p.sem["inv_ready"], a("inv_ready") + 1)
            nc.scalar.activation(p.rinv[0:16], p.rinv[0:16], ACT.Sqrt).then_inc(p.sem["unit_len"], 1)
    split_hi(p, act, u0 + 41)


def project_gpsimd(p, pool, st):
    a, nc = st.at, p.nc

    def one(g, c):
        t = g * 4 + c
        pool.wait_ge(p.sem["act_done"], t + (a("act_done") + 1))
        nc.gpsimd.tensor_tensor(p.inv[:, t], p.qkv[:, t], p.qkv[:, t], ALU.mult).then_inc(p.sem["sq_done"], 1)

    if st.unit0:
        pool.wait_ge(p.sem["unit_done"], st.unit0)
    for s in range(4):
        nc.gpsimd.memset(p.conv_in[:, s, 0:3], 0.0).then_inc(p.sem["conv_pad"], 1)
    groups(pool, 16, 4, one)


def project_vector(p, dve, st):
    a, u0, nc = st.at, st.unit0, p.nc
    w = st.par(p, "conv").rearrange("p (t j) -> p t j", j=4)
    dve.wait_ge(p.sem["conv_pad"], a("conv_pad") + 4)

    def conv(g, c):
        t = g * 8 + c
        if c > 1 or not isinstance(g, int) or g:
            split_lo(p, dve, u0 + c + 2, g)
        dve.wait_ge(p.sem["proj_out"], g * 8 + (a("proj_out") + c + 1))
        out, src = p.qkv[:, t], p.conv_in[:, c % 4]
        for j in range(3):
            if j:
                dve.wait_ge(p.sem["conv_step"], g * 16 + (a("conv_step") + 2 * c + j))
            nc.vector.scalar_tensor_tensor(
                out, src[:, j : j + T], w[:, t, j : j + 1], out, ALU.mult, ALU.add
            ).then_inc(p.sem["conv_step" if j < 2 else "conv_done"], 1)

    groups(dve, 24, 8, conv)
    for t in range(24, 40):
        split_lo(p, dve, u0 + t + 2)
        if t == 32:
            rows, step = p.rinv[0:16], a("inv_step")
            dve.wait_ge(p.sem["sums_done"], a("sums_done") + 1)
            nc.vector.tensor_scalar(rows, p.psum[0:16, 6, 0:T], 1.0, EPS, ALU.mult, ALU.add).then_inc(
                p.sem["inv_step"], 1)
            dve.wait_ge(p.sem["inv_step"], step + 1)
            nc.vector.reciprocal(rows, rows).then_inc(p.sem["inv_step"], 1)
            dve.wait_ge(p.sem["inv_step"], step + 2)
            nc.vector.tensor_scalar(rows, rows, p.c("q_scale")[0:16], None, ALU.mult).then_inc(p.sem["inv_ready"], 1)
        if t >= 35:
            for h in range(3 * (t - 35), 3 * (t - 34) if t < 39 else 16):
                dve.wait_ge(p.sem["act_done"], a("act_done") + h + 1)
                dve.wait_ge(p.sem["len_row"], a("len_row") + h + 1)
                nc.vector.tensor_tensor(
                    p.qkv[:, h], p.qkv[:, h], p.psum[:, LENGTH_BANKS[h % 4], 0:T], ALU.mult
                ).then_inc(p.sem["normed"], 1)




GROWN = GROUP * (LEVELS + 1)


def gdn_vector(p, dve, st):
    a, nc, v = st.at, p.nc, p.nc.vector
    step = a("gdn_step")

    def link(ins):
        nonlocal step
        step += 1
        ins.then_inc(p.sem["gdn_step"], 1)
        dve.wait_ge(p.sem["gdn_step"], step)

    beta, raw_g, cum = p.rows[0:HEADS], p.rows2[32 : 32 + HEADS], p.rows[32 : 32 + HEADS]
    dt_bias = st.par(p, "dt_bias")[32 : 32 + HEADS]
    dve.wait_ge(p.sem["gate_fn"], a("gate_fn") + 1)
    link(v.tensor_scalar(beta, beta, 0.5, 0.5, ALU.mult, ALU.add))
    dve.wait_ge(p.sem["gate_fn"], a("gate_fn") + 5)
    link(v.tensor_scalar(raw_g, p.lat[32 : 32 + HEADS, 6], dt_bias, 0.0, ALU.add, ALU.max))
    link(v.tensor_tensor(raw_g, raw_g, p.soft[32 : 32 + HEADS], ALU.add))
    link(v.tensor_scalar(raw_g, raw_g, p.exp_a[32 : 32 + HEADS], -1.0, ALU.mult, ALU.mult))
    for c in range(2):
        part = slice(c * P, c * P + P)
        v.tensor_tensor_scan(
            cum[:, part], p.c("ones")[32 : 32 + HEADS], raw_g[:, part], 0.0, ALU.mult, ALU.add
        ).then_inc(p.sem["rows_ready"], 1)
    dve.wait_ge(p.sem["cols_done"], a("cols_done") + 1)
    v.tensor_copy(p.cols[:].rearrange("p c b h -> p (c b h)"), p.psum[:, 2, 0 : 4 * HEADS]).then_inc(
        p.sem["cols_ready"], 1)
    dve.wait_ge(p.sem["cols_ready"], a("cols_ready") + 1)
    dve.wait_ge(p.sem["exp_cum"], a("exp_cum") + 1)
    v.tensor_tensor(p.beta_exp[:], p.cols[:, 1, 0], p.exp_cols[:], ALU.mult).then_inc(p.sem["cols_ready"], 1)
    dve.wait_ge(p.sem["cols_ready"], a("cols_ready") + 2)

    for gq in range(HEADS // GROUP):
        at = lambda name, per: a(name) + gq * per
        for i in range(GROUP):
            h = gq * GROUP + i
            dve.wait_ge(p.sem["rows_done"], at("rows_done", 4) + i + 1)
            if gq:
                dve.wait_ge(p.sem["out_ready"], a("out_ready") + gq * GROUP)
            v.tensor_tensor(p.kb[:, i], p.qkv[:, 8 + h], p.psum[:, i, T : 2 * T], ALU.mult).then_inc(
                p.sem["kb_ready"], 1)
            for c in range(2):
                v.scalar_tensor_tensor(
                    p.decay[:, i, c * P : c * P + P], p.psum[:, i, c * P : c * P + P],
                    p.cols[:, c, 1, h : h + 1], p.c("neg")[:, 0:P], ALU.subtract, ALU.add,
                ).then_inc(p.sem["exponent_ready"], 1)
        for i in range(GROUP):
            h = gq * GROUP + i
            dve.wait_ge(p.sem["pairs_done"], at("pairs_done", 4) + i + 1)
            dve.wait_ge(p.sem["decay_ready"], at("decay_ready", 4) + i + 1)
            v.tensor_tensor(p.a_t[:, i], p.psum[:, 4 + i, 0:T], p.decay[:, i], ALU.mult).then_inc(
                p.sem["pairs_used"], 1)
            v.tensor_tensor(p.qk_t[:, i], p.psum[:, 4 + i, T : 2 * T], p.decay[:, i], ALU.mult).then_inc(
                p.sem["pairs_used"], 1)
            v.tensor_tensor(p.qkv[:, h, P:T], p.qkv[:, h, P:T], p.exp_row[:, i], ALU.mult).then_inc(
                p.sem["q_dec_ready"], 1)
            dve.wait_ge(p.sem["pairs_used"], at("pairs_used", 8) + 2 * i + 1)
            link(v.tensor_tensor(p.kb[:, i], p.a_t[:, i], p.c("first_t"), ALU.mult))
            v.tensor_tensor(
                p.inv_t[:, i, 0].rearrange("p (c j) -> p c j", c=2),
                p.c("ident").unsqueeze(1).broadcast_to([P, 2, P]),
                p.kb[:, i].rearrange("p (c j) -> p c j", c=2), ALU.subtract,
            ).then_inc(p.sem["inv_grown"], 1)
        for i in range(GROUP):
            h = gq * GROUP + i
            dve.wait_ge(p.sem["turned_done"], at("turned_done", 4) + i + 1)
            k0, k1, v0, v1 = (p.psum[:, i, n * P : n * P + P] for n in range(4))
            v.tensor_scalar(p.v_beta[:, i, 0:P], v0, p.cols[:, 0, 0, h : h + 1], None, ALU.mult)
            v.tensor_scalar(p.v_beta[:, i, P:T], v1, p.cols[:, 1, 0, h : h + 1], None, ALU.mult)
            v.tensor_scalar(p.k_tok[:, i, P:T], k1, p.beta_exp[:, h : h + 1], None, ALU.mult)
            v.tensor_scalar(p.k_tok[:, i, 0:P], k0, p.decay[:, i, P - 1 : P], None, ALU.mult).then_inc(
                p.sem["turned_used"], 1)
        masks = p.c("masks").rearrange("p (l n) -> p l n", n=P)
        with dve.Fori(0, LEVELS) as level:
            for i in range(GROUP):
                dve.wait_ge(p.sem["lp_done"], level * GROUP + (at("lp_done", 4 * LEVELS) + i + 1))
                v.tensor_tensor(
                    p.kb[:, i].rearrange("p (c j) -> p c j", c=2),
                    p.psum[:, i, 0:T].rearrange("p (c j) -> p c j", c=2),
                    masks[:, level].unsqueeze(1).broadcast_to([P, 2, P]), ALU.mult,
                ).then_inc(p.sem["new_ready"], 1)
            for i in range(GROUP):
                dve.wait_ge(p.sem["lq_done"], level * GROUP + (at("lq_done", 4 * LEVELS) + i + 1))
                both = p.inv_t[:, i].rearrange("p b n -> p (b n)")
                v.tensor_tensor(both, both, p.psum[:, 4 + i], ALU.subtract).then_inc(p.sem["inv_grown"], 1)
        for i in range(GROUP):
            dve.wait_ge(p.sem["v1_done"], at("v1_done", 4) + i + 1)
            v.tensor_copy(p.decay[:, i, P:T], p.psum[:, i, 0:P]).then_inc(p.sem["v1_ready"], 1)
    for h in range(HEADS):
        dve.wait_ge(p.sem["o_sq"], a("o_sq") + h + 1)
        v.tensor_tensor(p.qkv[:, h], p.qkv[:, h], p.z[:, h], ALU.mult).then_inc(p.sem["o_gated"], 1)
    rows = p.rinv[0:16]
    dve.wait_ge(p.sem["o_sum"], a("o_sum") + 1)
    link(v.tensor_scalar(rows, p.psum[0:16, 0, 0:T], 1.0 / P, EPS, ALU.mult, ALU.add))
    v.reciprocal(rows, rows).then_inc(p.sem["o_inv"], 1)
    for h in range(HEADS):
        dve.wait_ge(p.sem["o_gated"], a("o_gated") + h + 1)
        dve.wait_ge(p.sem["len_row"], a("len_row") + h + 1)
        v.scalar_tensor_tensor(
            p.qkv[:, h], p.qkv[:, h], st.par(p, "out_gain"), p.psum[:, h % 4, 0:T], ALU.mult, ALU.mult
        ).then_inc(p.sem["oa_ready"], 1)


def gdn_scalar(p, act, st):
    a, nc, f = st.at, p.nc, p.nc.scalar.activation
    ba, dt_bias = p.lat[:, 6], st.par(p, "dt_bias")[32 : 32 + HEADS]
    soft, fn = p.soft[32 : 32 + HEADS], a("gate_fn")
    act.wait_ge(p.sem["proj_out"], a("proj_out"))
    f(p.rows[0:HEADS], ba[0:HEADS], ACT.Tanh, scale=0.5).then_inc(p.sem["gate_fn"], 1)
    f(p.exp_a[32 : 32 + HEADS], st.par(p, "a_log")[32 : 32 + HEADS], ACT.Exp).then_inc(p.sem["gate_fn"], 1)
    f(soft, ba[32 : 32 + HEADS], ACT.Abs, bias=dt_bias).then_inc(p.sem["gate_fn"], 1)
    act.wait_ge(p.sem["gate_fn"], fn + 3)
    f(soft, soft, ACT.Exp, scale=-1.0).then_inc(p.sem["gate_fn"], 1)
    act.wait_ge(p.sem["gate_fn"], fn + 4)
    f(soft, soft, ACT.Ln, bias=1.0).then_inc(p.sem["gate_fn"], 1)
    act.wait_ge(p.sem["cols_ready"], a("cols_ready") + 1)
    f(p.exp_cols[:], p.cols[:, 1, 1], ACT.Exp).then_inc(p.sem["exp_cum"], 1)
    for gq in range(HEADS // GROUP):
        at = lambda name, per: a(name) + gq * per
        for i in range(GROUP):
            act.wait_ge(p.sem["exponent_ready"], at("exponent_ready", 8) + 2 * i + 2)
            f(p.exp_row[:, i], p.psum[:, i, P:T], ACT.Exp).then_inc(p.sem["row_exp"], 1)
            f(p.decay[:, i], p.decay[:, i], ACT.Exp).then_inc(p.sem["decay_ready"], 1)
        for i in range(GROUP):
            act.wait_ge(p.sem["first_turned"], at("first_turned", 4) + i + 1)
            f(p.inv_t[:, i, 1], p.psum[:, 4 + i, 0:T], ACT.Copy).then_inc(p.sem["first_both"], 1)
        for i in range(GROUP):
            act.wait_ge(p.sem["wu_done"], at("wu_done", 4) + i + 1)
            f(p.w_s[:, i, 0:P], p.psum[:, 4 + i, 0:P], ACT.Copy, scale=-1.0).then_inc(p.sem["w_ready"], 1)
            f(p.decay[:, i, 0:P], p.psum[:, 4 + i, P:T], ACT.Copy).then_inc(p.sem["v0_ready"], 1)
        for i in range(GROUP):
            act.wait_ge(p.sem["state_done"], at("state_done", 4) + i + 1)
            f(p.w_s[:, i, P:T], p.psum[:, 4 + i, T : T + P], ACT.Copy).then_inc(p.sem["state_ready"], 1)
        for i in range(GROUP):
            h = gq * GROUP + i
            act.wait_ge(p.sem["o_done"], at("o_done", 4) + i + 1)
            f(p.qkv[:, h], p.psum[:, 4 + i, 0:T], ACT.Copy).then_inc(p.sem["out_ready"], 1)
    for h in range(HEADS):
        act.wait_ge(p.sem["out_ready"], a("out_ready") + HEADS)
        f(p.inv[:, h], p.qkv[:, h], ACT.Square).then_inc(p.sem["o_sq"], 1)
    act.wait_ge(p.sem["o_inv"], a("o_inv") + 1)
    f(p.rinv[0:16], p.rinv[0:16], ACT.Sqrt).then_inc(p.sem["o_root"], 1)


def gdn_tensor(p, pe, st):
    a, nc, mm = st.at, p.nc, p.nc.tensor.matmul
    ident = p.c("ident")
    rows = p.rows[0 : 32 + HEADS]
    pe.wait_ge(p.sem["rows_ready"], a("rows_ready") + 2)
    pe.wait_ge(p.sem["rows_cleared"], 1)
    for c in range(2):
        for b in range(2):
            ins = mm(p.psum[:, 2, (2 * c + b) * HEADS : (2 * c + b + 1) * HEADS], rows[:, c * P : c * P + P],
                     ident[0 : 32 + HEADS, 32 * b : 32 * b + HEADS], start=True, stop=True)
    ins.then_inc(p.sem["cols_done"], 1)
    pe.wait_ge(p.sem["normed"], a("normed"))
    pe.wait_ge(p.sem["cols_ready"], a("cols_ready") + 1)
    for gq in range(HEADS // GROUP):
        at = lambda name, per: a(name) + gq * per
        if gq:
            pe.wait_ge(p.sem["out_ready"], a("out_ready") + gq * GROUP)
        for i in range(GROUP):
            h = gq * GROUP + i
            for b in range(2):
                pick = ident[0 : 32 + HEADS, 32 - 32 * b + h : 33 - 32 * b + h].to_broadcast([32 + HEADS, P])
                ins = mm(p.psum[:, i, b * T : b * T + T], pick, rows, start=True, stop=True)
            ins.then_inc(p.sem["rows_done"], 1)
        for i in range(GROUP):
            h = gq * GROUP + i
            pe.wait_ge(p.sem["kb_ready"], at("kb_ready", 4) + i + 1)
            for c in range(2):
                part = slice(c * P, c * P + P)
                k = p.qkv[:, 8 + h, part]
                mm(p.psum[:, 4 + i, part], k, p.kb[:, i, part], start=True, stop=True)
                ins = mm(p.psum[:, 4 + i, T + c * P : T + c * P + P], k, p.qkv[:, h, part], start=True, stop=True)
            ins.then_inc(p.sem["pairs_done"], 1)
        for i in range(GROUP):
            h = gq * GROUP + i
            pe.wait_ge(p.sem["row_exp"], at("row_exp", 4) + i + 1)
            for n, src in enumerate((8 + h, 8 + h, 16 + h, 16 + h)):
                part = slice(n % 2 * P, n % 2 * P + P)
                ins = nc.tensor.transpose(p.psum[:, i, n * P : n * P + P], p.qkv[:, src, part], ident)
            ins.then_inc(p.sem["turned_done"], 1)
        for i in range(GROUP):
            pe.wait_ge(p.sem["inv_grown"], at("inv_grown", GROWN) + i + 1)
            for c in range(2):
                part = slice(c * P, c * P + P)
                ins = nc.tensor.transpose(p.psum[:, 4 + i, part], p.inv_t[:, i, 0, part], ident)
            ins.then_inc(p.sem["first_turned"], 1)
        pe.wait_ge(p.sem["turned_used"], at("turned_used", 4) + 4)
        pe.wait_ge(p.sem["first_both"], at("first_both", 4) + 4)
        with pe.Fori(0, LEVELS) as level:
            for i in range(GROUP):
                pe.wait_ge(p.sem["inv_grown"], level * GROUP + (at("inv_grown", GROWN) + i + 1))
                for c in range(2):
                    part = slice(c * P, c * P + P)
                    ins = mm(p.psum[:, i, part], p.a_t[:, i, part], p.inv_t[:, i, 1, part], start=True, stop=True)
                ins.then_inc(p.sem["lp_done"], 1)
            for i in range(GROUP):
                pe.wait_ge(p.sem["new_ready"], level * GROUP + (at("new_ready", 4 * LEVELS) + i + 1))
                for c in range(2):
                    part = slice(c * P, c * P + P)
                    t_t, t = p.inv_t[:, i, 0, part], p.inv_t[:, i, 1, part]
                    mm(p.psum[:, 4 + i, part], p.kb[:, i, part], t_t, start=True, stop=True)
                    ins = mm(p.psum[:, 4 + i, T + c * P : T + c * P + P], t_t, p.kb[:, i, part], start=True, stop=True)
                ins.then_inc(p.sem["lq_done"], 1)
        grown = at("inv_grown", GROWN) + GROWN
        for i in range(GROUP):
            pe.wait_ge(p.sem["inv_grown"], grown - GROUP + i + 1)
            t0, t1 = p.inv_t[:, i, 0, 0:P], p.inv_t[:, i, 0, P:T]
            mm(p.psum[:, 4 + i, 0:P], p.k_tok[:, i, P:T], t1, start=True, stop=True)
            mm(p.psum[:, 4 + i, P:T], t0, p.v_beta[:, i, 0:P], start=True, stop=True).then_inc(p.sem["wu_done"], 1)
        for i in range(GROUP):
            pe.wait_ge(p.sem["v0_ready"], at("v0_ready", 4) + i + 1)
            mm(p.psum[:, 4 + i, T : T + P], p.k_tok[:, i, 0:P], p.decay[:, i, 0:P], start=True, stop=True).then_inc(
                p.sem["state_done"], 1)
        for i in range(GROUP):
            pe.wait_ge(p.sem["state_ready"], at("state_ready", 4) + i + 1)
            mm(p.psum[:, i, 0:P], p.inv_t[:, i, 0, P:T], p.v_beta[:, i, P:T], start=True, stop=False)
            mm(p.psum[:, i, 0:P], p.w_s[:, i, 0:P], p.w_s[:, i, P:T], start=False, stop=True).then_inc(
                p.sem["v1_done"], 1)
        for i in range(GROUP):
            h = gq * GROUP + i
            pe.wait_ge(p.sem["v1_ready"], at("v1_ready", 4) + i + 1)
            mm(p.psum[:, 4 + i, 0:P], p.decay[:, i, 0:P], p.qk_t[:, i, 0:P], start=True, stop=True)
            mm(p.psum[:, 4 + i, P:T], p.w_s[:, i, P:T], p.qkv[:, h, P:T], start=True, stop=False)
            mm(p.psum[:, 4 + i, P:T], p.decay[:, i, P:T], p.qk_t[:, i, P:T], start=False, stop=True).then_inc(
                p.sem["o_done"], 1)
    for h in range(HEADS):
        pe.wait_ge(p.sem["o_sq"], a("o_sq") + h + 1)
        ins = mm(p.psum[0:16, 0, 0:T], p.pick("row", h), p.inv[:, h], start=h == 0, stop=h == HEADS - 1)
    ins.then_inc(p.sem["o_sum"], 1)
    pe.wait_ge(p.sem["o_root"], a("o_root") + 1)
    for h in range(HEADS):
        if h >= 4:
            pe.wait_ge(p.sem["oa_ready"], a("oa_ready") + h - 3)
        mm(p.psum[:, h % 4, 0:T], ident[0:16, h : h + 1].to_broadcast([16, P]), p.rinv[0:16], start=True,
           stop=True).then_inc(p.sem["len_row"], 1)



TWO_PI = (6.28125, 0.0019350051879882812, 3.0199159819567e-07)
ROUND = 12582912.0


def trig_vector(p, dve):
    v, step = p.nc.vector, 0

    def link(ins):
        nonlocal step
        step += 1
        ins.then_inc(p.sem["trig_step"], 1)
        dve.wait_ge(p.sem["trig_step"], step)

    link(v.tensor_copy(p.angle[:], p.positions[:]))
    link(v.tensor_scalar(p.angle[:], p.angle[:], p.c("inv_freq"), None, ALU.mult))
    for out, shift in ((p.sin, 0.0), (p.cos, 0.25)):
        turns = p.var
        link(v.tensor_scalar(turns[:], p.angle[:], 1.0 / (2 * math.pi), shift, ALU.mult, ALU.add))
        link(v.tensor_scalar(turns[:], turns[:], ROUND, None, ALU.add))
        link(v.tensor_scalar(turns[:], turns[:], -ROUND, None, ALU.add))
        src = p.angle
        for part in TWO_PI:
            link(v.scalar_tensor_tensor(out[:], turns[:], -part, src[:], ALU.mult, ALU.add))
            src = out
        link(v.tensor_scalar(out[:], out[:], 2 * math.pi * shift, 3.1415925, ALU.add, ALU.min))
        v.tensor_scalar(out[:], out[:], -3.1415925, None, ALU.max).then_inc(p.sem["angles_ready"], 1)


def trig_scalar(p, act):
    act.wait_ge(p.sem["angles_ready"], 2)
    p.nc.scalar.activation(p.sin[:], p.sin[:], ACT.Sin)
    p.nc.scalar.activation(p.cos[:], p.cos[:], ACT.Sin).then_inc(p.sem["trig_done"], 1)



N_UP = 12 + 8


def up_gpsimd(p, pool, st):
    a, nc = st.at, p.nc
    pool.wait_ge(p.sem["oa_ready"], a("oa_ready"))
    for t in range(LAT_Q + LAT_KV):
        nc.gpsimd.tensor_tensor(p.lat_sq[:, t], p.lat[:, t], p.lat[:, t], ALU.mult).then_inc(p.sem["lat_sq"], 1)
    nc.gpsimd.tensor_tensor(p.kr[:], p.lat[:, 5], p.lat[:, 5], ALU.mult).then_inc(p.sem["kpe_sq"], 1)
    for j in range(N_UP):
        pool.wait_ge(p.sem["up_out"], a("up_out") + j + 1)
        if j >= 8:
            pool.wait_ge(p.sem["up_summed"], a("up_summed") + j - 7)
        src = p.up_tile(j)
        nc.gpsimd.tensor_tensor(p.tmp[:, j % 8], src, src, ALU.mult).then_inc(p.sem["up_sq"], 1)


def up_tensor(p, pe, st):
    a, u0, nc, mm = st.at, st.unit0, p.nc, p.nc.tensor.matmul
    ones, halves = p.c("ones"), (p.c("half_0"), p.c("half_1"))
    for b, (t0, n) in enumerate(((0, LAT_Q), (LAT_Q, LAT_KV))):
        for k in range(n):
            pe.wait_ge(p.sem["lat_sq"], a("lat_sq") + t0 + k + 1)
            ins = mm(p.psum[:, 6 + b, 0:T], ones, p.lat_sq[:, t0 + k], start=k == 0, stop=k == n - 1)
        ins.then_inc(p.sem["lat_sum"], 1)

    def tile(j, n_k, chunk, t0):
        for k in range(n_k):
            if j == 0:
                pe.wait_ge(p.sem["lat_ready"], a("lat_ready") + LAT_Q)
            if j == 12:
                pe.wait_ge(p.sem["lat_ready"], a("lat_ready") + LAT_Q + LAT_KV)
            if k == 0 and j >= 4:
                pe.wait_ge(p.sem["up_out"], a("up_out") + j - 3)
            ins = three_pass(p, p.psum[:, j % 4, 0:T], (u0 + chunk // UNIT) % SLOTS, (chunk + k) % UNIT,
                             p.lat_hi[:, t0 + k], p.lat_lo[:, t0 + k], k == 0, k == n_k - 1)
        return ins

    def total(j):
        pe.wait_ge(p.sem["up_sq"], a("up_sq") + j + 1)
        sq = p.tmp[:, j % 8]
        if j < 8:
            ins = mm(rows, p.pick("row", j), sq, start=j == 0, stop=False, skip_group_check=True)
        elif j < 12:
            for b in range(2):
                ins = mm(rows, p.pick(f"row_{b}", 2 * (j - 8) + b), sq, start=False, stop=False, skip_group_check=True)
        else:
            h = j - 12
            mm(rows, p.pick("row_0", 8 + h), p.kr[:], start=False, stop=False, skip_group_check=True)
            ins = mm(rows, p.pick("row", 8 + h), sq, start=False, stop=j == N_UP - 1, skip_group_check=True)
        ins.then_inc(p.sem["up_summed"], 1)

    rows = p.psum[0:16, 6, 0:T]
    pe.wait_ge(p.sem["lat_var"], a("lat_var") + 4)
    for u in range(6):
        pe.wait_ge(p.sem["lo_ready"], u0 + u + 1)
        for b in range(2):
            ins = tile(2 * u + b, LAT_Q, u * UNIT + 4 * b, 0)
        ins.then_inc(p.sem["unit_done"], 1)
        if u:
            total(2 * u - 2)
            total(2 * u - 1)
    pe.wait_ge(p.sem["kpe_sq"], a("kpe_sq") + 1)
    for u in range(2):
        pe.wait_ge(p.sem["lo_ready"], u0 + 6 + u + 1)
        for b in range(4):
            ins = tile(12 + 4 * u + b, LAT_KV, (6 + u) * UNIT + 2 * b, LAT_Q)
        ins.then_inc(p.sem["unit_done"], 1)
        for j in ((10, 11), (12, 13, 14, 15))[u]:
            total(j)
    for k in range(LAT_KV):
        s = (u0 + 8 + k) % SLOTS
        pe.wait_ge(p.sem["lo_ready"], u0 + 8 + k + 1)
        for c in range(2):
            hi, lo = (x[:, LAT_Q + k, c * P : c * P + P] for x in (p.lat_hi, p.lat_lo))
            for b in range(2):
                out = p.psum[:, (4, 5, 2, 3)[2 * c + b]]
                if k == 0 and c == 1 and b == 0:
                    pe.wait_ge(p.sem["up_out"], a("up_out") + N_UP)
                w_hi, w_lo = (w[:, s, 4 * b : 4 * b + 4].rearrange("p k m -> p (k m)") for w in (p.w_hi, p.w_lo))
                mm(out, hi, w_hi, start=k == 0, stop=False)
                mm(out, hi, w_lo, start=False, stop=False)
                ins = mm(out, lo, w_hi, start=False, stop=k == LAT_KV - 1)
        ins.then_inc(p.sem["unit_done"], 1)
    for j in range(16, N_UP):
        total(j)
    for j in range(5):
        pe.wait_ge(p.sem["rope_in"], a("rope_in") + j + 1)
        if j >= 2:
            pe.wait_ge(p.sem["rope_out"], a("rope_out") + j - 1)
        src = p.kr[:] if j == 4 else p.qr[:, j]
        mm(p.psum[:, j % 2, 0:T], p.c("rot"), src, start=True, stop=True).then_inc(p.sem["rope_turned"], 1)
    pe.wait_ge(p.sem["rinv_rows"], a("rinv_rows") + 1)
    pe.wait_ge(p.sem["values_out"], a("values_out") + 4)
    ident = p.c("ident")
    for t in range(2 * HEADS):
        if t >= 4:
            pe.wait_ge(p.sem["head_normed"], a("head_normed") + t - 3)
        else:
            pe.wait_ge(p.sem["rope_out"], a("rope_out") + 5)
        mm(p.psum[:, t % 4, 0:T], ident[0:16, t : t + 1].to_broadcast([16, P]), p.rinv16[0:16],
           start=True, stop=True).then_inc(p.sem["head_rinv"], 1)


def up_scalar(p, act, st):
    a, u0, nc, f = st.at, st.unit0, p.nc, p.nc.scalar.activation
    for b in range(2):
        act.wait_ge(p.sem["lat_var"], a("lat_var") + 2 * b + 2)
        f(p.rinv_lat[:, b], p.rinv_lat[:, b], ACT.Sqrt).then_inc(p.sem["lat_root"], 1)
    for t in range(LAT_Q + LAT_KV):
        act.wait_ge(p.sem["lat_scaled"], a("lat_scaled") + t + 1)
        f(p.lat_hi[:, t], p.lat[:, t], ACT.Copy).then_inc(p.sem["lat_rounded"], 1)
    for j in range(N_UP):
        if j < 12:
            if j % 2 == 0:
                split_hi(p, act, u0 + j // 2 + 2)
        elif j % 4 == 0:
            split_hi(p, act, u0 + 6 + (j - 12) // 4 + 2)
        act.wait_ge(p.sem["unit_done"], u0 + (j // 2 if j < 12 else 6 + (j - 12) // 4) + 1)
        f(p.up_tile(j), p.psum[:, j % 4, 0:T], ACT.Copy).then_inc(p.sem["up_out"], 1)
    split_hi(p, act, u0 + 10)
    split_hi(p, act, u0 + 11)
    act.wait_ge(p.sem["unit_done"], u0 + 10)
    for c in range(2):
        for b in range(2):
            f(p.vt[:, c, b * 512 : b * 512 + 512], p.psum[:, (4, 5, 2, 3)[2 * c + b]], ACT.Copy).then_inc(
                p.sem["values_out"], 1)
    act.wait_ge(p.sem["head_var"], a("head_var") + 2)
    f(p.rinv16[0:16], p.rinv16[0:16], ACT.Sqrt).then_inc(p.sem["rinv_rows"], 1)


def up_vector(p, dve, st):
    a, u0, nc, v = st.at, st.unit0, p.nc, p.nc.vector
    dve.wait_ge(p.sem["trig_done"], 1)
    gain = st.par(p, "lat_gain")
    for b, n in enumerate((LAT_Q, LAT_KV)):
        dve.wait_ge(p.sem["lat_sum"], a("lat_sum") + b + 1)
        v.tensor_scalar(p.rinv_lat[:, b], p.psum[:, 6 + b, 0:T], 1.0 / (n * P), EPS, ALU.mult, ALU.add).then_inc(
            p.sem["lat_var"], 1)
        dve.wait_ge(p.sem["lat_var"], a("lat_var") + 2 * b + 1)
        v.reciprocal(p.rinv_lat[:, b], p.rinv_lat[:, b]).then_inc(p.sem["lat_var"], 1)
    for t in range(LAT_Q + LAT_KV):
        b = t // LAT_Q
        dve.wait_ge(p.sem["lat_root"], a("lat_root") + b + 1)
        v.scalar_tensor_tensor(
            p.lat[:, t], p.lat[:, t], gain[:, t : t + 1], p.rinv_lat[:, b], ALU.mult, ALU.mult
        ).then_inc(p.sem["lat_scaled"], 1)
    for t in range(LAT_Q + LAT_KV):
        dve.wait_ge(p.sem["lat_rounded"], a("lat_rounded") + t + 1)
        v.tensor_tensor(p.lat_lo[:, t], p.lat[:, t], p.lat_hi[:, t].bitcast(F32), ALU.subtract).then_inc(
            p.sem["lat_ready"], 1)
    for s in range(10):
        split_lo(p, dve, u0 + 2 + s)
    dve.wait_ge(p.sem["up_summed"], a("up_summed") + N_UP)
    v.tensor_scalar(p.rinv16[0:16], p.psum[0:16, 6, 0:T], 1.0 / 192, EPS, ALU.mult, ALU.add).then_inc(
        p.sem["head_var"], 1)
    dve.wait_ge(p.sem["head_var"], a("head_var") + 1)
    v.reciprocal(p.rinv16[0:16], p.rinv16[0:16]).then_inc(p.sem["head_var"], 1)
    q_norm, k_norm = st.par(p, "q_norm"), st.par(p, "k_norm")
    for j in range(5):
        out, src, g = (p.kr[:], p.lat[:, 5], k_norm) if j == 4 else (p.qr[:, j], p.qr[:, j], q_norm)
        v.tensor_scalar(out, src, g[:, 1:2], None, ALU.mult).then_inc(p.sem["rope_in"], 1)
    for j in range(5):
        out = p.kr[:] if j == 4 else p.qr[:, j]
        dve.wait_ge(p.sem["rope_turned"], a("rope_turned") + j + 1)
        v.tensor_tensor(out, out, p.cos[:], ALU.mult).then_inc(p.sem["rope_step"], 1)
        v.tensor_tensor(p.work[:, j % 2], p.psum[:, j % 2, 0:T], p.sin[:], ALU.mult).then_inc(p.sem["rope_step"], 1)
        dve.wait_ge(p.sem["rope_step"], a("rope_step") + 2 * j + 2)
        v.tensor_tensor(out, out, p.work[:, j % 2], ALU.add).then_inc(p.sem["rope_out"], 1)
    dve.wait_ge(p.sem["rope_out"], a("rope_out") + 5)
    for t in range(2 * HEADS):
        dve.wait_ge(p.sem["head_rinv"], a("head_rinv") + t + 1)
        rinv, h = p.psum[:, t % 4, 0:T], t % HEADS
        if t < HEADS:
            v.scalar_tensor_tensor(p.qn[:, h], p.qn[:, h], q_norm[:, 0:1], rinv, ALU.mult, ALU.mult)
            half = slice(ROPE * (h % 2), ROPE * (h % 2) + ROPE)
            ins = v.tensor_tensor(p.qr[half, h // 2], p.qr[half, h // 2], p.psum[half, t % 4, 0:T], ALU.mult)
        else:
            v.scalar_tensor_tensor(p.kn[:, h], p.kn[:, h], k_norm[:, 0:1], rinv, ALU.mult, ALU.mult)
            ins = v.scalar_tensor_tensor(
                p.krz[:, h], p.kr[:], p.c(f"half_{h % 2}"), rinv, ALU.mult, ALU.mult)
        ins.then_inc(p.sem["head_normed"], 1)



SCALE = 192.0 ** -0.5


def attn_tensor(p, pe, st):
    a, nc, mm = st.at, p.nc, p.nc.tensor.matmul
    pe.wait_ge(p.sem["head_normed"], a("head_normed"))
    q0, q1, both = slice(0, P), slice(P, T), slice(0, T)
    for i in range(HEADS + 2):
        if i < HEADS:
            h = i
            if h >= 2:
                pe.wait_ge(p.sem["masked"], a("masked") + h - 1)
            for part, keys, lo, hi in ((q0, q0, 0, P), (q1, both, P, 3 * P)):
                out = p.psum[:, h % 2, lo:hi]
                mm(out, p.qn[:, h, part], p.kn[:, h, keys], start=True, stop=False)
                ins = mm(out, p.qr[:, h // 2, part], p.krz[:, h, keys], start=False, stop=True)
            ins.then_inc(p.sem["scored"], 1)
        if 1 <= i <= HEADS:
            h = i - 1
            pe.wait_ge(p.sem["weighed"], a("weighed") + h + 1)
            if h >= 2:
                pe.wait_ge(p.sem["weights_out"], a("weights_out") + h - 1)
            for n in range(3):
                part = slice(n * P, n * P + P)
                ins = nc.tensor.transpose(p.psum[:, 2 + h % 2, part], p.sm[:, h % 2, part], p.c("ident"))
            ins.then_inc(p.sem["weights_turned"], 1)
        if i >= 2:
            h = i - 2
            pe.wait_ge(p.sem["weights_out"], a("weights_out") + h + 1)
            if h >= 2:
                pe.wait_ge(p.sem["ob_out"], a("ob_out") + h - 1)
            out, cols = p.psum[:, 4 + h % 2], slice(h * P, h * P + P)
            mm(out[:, 0:T], p.vt[:, 0, cols], p.pt[:, h % 2, 0:T], start=True, stop=False)
            mm(out[:, P:T], p.vt[:, 1, cols], p.pt[:, h % 2, T : 3 * P], start=False, stop=True).then_inc(
                p.sem["mixed"], 1)


def attn_vector(p, dve, st):
    a, v = st.at, p.nc.vector
    for i in range(HEADS + 1):
        if i < HEADS:
            h = i
            dve.wait_ge(p.sem["scored"], a("scored") + h + 1)
            if h >= 2:
                dve.wait_ge(p.sem["weights_turned"], a("weights_turned") + h - 1)
            sm = p.sm[:, h % 2]
            v.tensor_tensor(sm, p.psum[:, h % 2, 0 : 3 * P], p.c("attn"), ALU.add).then_inc(p.sem["masked"], 1)
            dve.wait_ge(p.sem["masked"], a("masked") + h + 1)
            v.tensor_reduce(p.mx[:, h % 2, 0:1], sm[:, 0:P], AX.X, ALU.max).then_inc(p.sem["max_step"], 1)
            v.tensor_reduce(p.mx[:, h % 2, 1:2], sm[:, P : 3 * P], AX.X, ALU.max).then_inc(p.sem["max_step"], 1)
            dve.wait_ge(p.sem["max_step"], a("max_step") + 2 * h + 2)
            v.tensor_scalar(p.nmx[:, h % 2], p.mx[:, h % 2], -SCALE, None, ALU.mult).then_inc(p.sem["max_ready"], 1)
        if i:
            h = i - 1
            dve.wait_ge(p.sem["exped"], a("exped") + h + 1)
            v.reciprocal(p.rden[:, h % 2], p.den[:, h % 2]).then_inc(p.sem["den_ready"], 1)
            dve.wait_ge(p.sem["den_ready"], a("den_ready") + h + 1)
            sm = p.sm[:, h % 2]
            v.tensor_scalar(sm[:, 0:P], sm[:, 0:P], p.rden[:, h % 2, 0:1], None, ALU.mult)
            v.tensor_scalar(sm[:, P : 3 * P], sm[:, P : 3 * P], p.rden[:, h % 2, 1:2], None, ALU.mult).then_inc(
                p.sem["weighed"], 1)


def attn_scalar(p, act, st):
    a, f = st.at, p.nc.scalar.activation
    for i in range(HEADS + 2):
        if i < HEADS:
            h = i
            act.wait_ge(p.sem["max_ready"], a("max_ready") + h + 1)
            sm = p.sm[:, h % 2]
            f(sm[:, 0:P], sm[:, 0:P], ACT.Exp, bias=p.nmx[:, h % 2, 0:1], scale=SCALE, accum_out=p.den[:, h % 2, 0:1])
            f(sm[:, P : 3 * P], sm[:, P : 3 * P], ACT.Exp, bias=p.nmx[:, h % 2, 1:2], scale=SCALE,
              accum_out=p.den[:, h % 2, 1:2]).then_inc(p.sem["exped"], 1)
        if 1 <= i <= HEADS:
            h = i - 1
            act.wait_ge(p.sem["weights_turned"], a("weights_turned") + h + 1)
            if h >= 2:
                act.wait_ge(p.sem["mixed"], a("mixed") + h - 1)
            f(p.pt[:, h % 2], p.psum[:, 2 + h % 2, 0 : 3 * P], ACT.Copy).then_inc(p.sem["weights_out"], 1)
        if i >= 2:
            h = i - 2
            act.wait_ge(p.sem["mixed"], a("mixed") + h + 1)
            f(p.qn[:, h], p.psum[:, 4 + h % 2, 0:T], ACT.Copy).then_inc(p.sem["ob_out"], 1)




def gates_tensor(p, pe, st):
    a, u0 = st.at, st.unit0
    banks = (0, 1, 2, 3)
    pe.wait_ge(p.sem["ob_out"], a("ob_out"))

    def product(g, c):
        b = c % 4
        src = ((p.h_hi, p.h_lo, 0), (p.o_hi, p.o_lo, 0), (p.h_hi, p.h_lo, 0), (p.o_hi, p.o_lo, 8))[b]
        if not isinstance(g, int) or 8 * g + c >= 4:
            sem = ("gate_tanh", "y_step")[b % 2]
            pe.wait_ge(p.sem[sem], g * 4 + (a(sem) + c // 2 - 1))
        pe.wait_ge(p.sem["lo_ready"], g * 8 + (u0 + c + 1))
        if isinstance(g, int) and g == 0 and c == 1:
            pe.wait_ge(p.sem["o_split"], a("o_split") + 1)
        if isinstance(g, int) and g == 0 and c == 3:
            pe.wait_ge(p.sem["o_split"], a("o_split") + 2)
        for k in range(UNIT):
            ins = three_pass(p, p.psum[:, banks[b], 0:T], (u0 + c) % SLOTS, k, src[0][:, src[2] + k],
                             src[1][:, src[2] + k], k == 0, k == UNIT - 1)
        ins.then_inc(p.sem["unit_done"], 1)

    for c in range(8):
        product(0, c)
    with pe.Fori(1, 4) as g:
        for c in range(8):
            product(g, c)
    for m in range(KD):
        s = u0 + 32 + m
        pe.wait_ge(p.sem["lo_ready"], s + 1)
        if m >= 4:
            pe.wait_ge(p.sem["x_ready"], a("x_ready") + m - 3)
        for k in range(UNIT):
            if m == 0 and k % 4 == 0:
                pe.wait_ge(p.sem["y_split"], a("y_split") + k // 4 + 1)
            ins = three_pass(p, p.psum[:, 4 + m % 4, 0:T], s % SLOTS, k, p.h_hi[:, k], p.h_lo[:, k], k == 0, k == UNIT - 1)
        ins.then_inc(p.sem["unit_done"], 1)


def gates_scalar(p, act, st):
    a, u0, f = st.at, st.unit0, p.nc.scalar.activation
    act.wait_ge(p.sem["ob_out"], a("ob_out"))
    act.wait_ge(p.sem["mixed"], a("mixed"))
    for b, src in enumerate((p.qkv[:, 0:HEADS], p.qn[:])):
        f(p.o_hi[:, 8 * b : 8 * b + 8], src, ACT.Copy).then_inc(p.sem["o_rounded"], 1)

    def gate(g, c):
        split_hi(p, act, u0 + 2 * c + 2, g)
        split_hi(p, act, u0 + 2 * c + 3, g)
        act.wait_ge(p.sem["unit_done"], g * 8 + (u0 + 2 * c + 1))
        if not isinstance(g, int) or 4 * g + c >= 2:
            act.wait_ge(p.sem["y_step"], g * 4 + (a("y_step") + c - 1))
        f(p.gate_t[:, c % 2], p.psum[:, 2 * (c % 2), 0:T], ACT.Tanh, scale=0.5).then_inc(p.sem["gate_tanh"], 1)

    groups(act, 16, 4, gate)
    for b in range(2):
        act.wait_ge(p.sem["y_ready"], a("y_ready") + 4 * b + 4)
        act.wait_ge(p.sem["unit_done"], u0 + 31)
        half = slice(4 * b, 4 * b + 4)
        f(p.h_hi[:, half], p.y[:, half], ACT.Copy).then_inc(p.sem["y_rounded"], 1)
    for m in range(KD):
        split_hi(p, act, u0 + 34 + m)


def gates_vector(p, dve, st):
    a, u0, v, x = st.at, st.unit0, p.nc.vector, st.x(p)
    for b, src in enumerate((p.qkv[:, 0:HEADS], p.qn[:])):
        dve.wait_ge(p.sem["o_rounded"], a("o_rounded") + b + 1)
        part = slice(8 * b, 8 * b + 8)
        v.tensor_tensor(p.o_lo[:, part], src, p.o_hi[:, part].bitcast(F32), ALU.subtract).then_inc(p.sem["o_split"], 1)

    def branch(g, c):
        split_lo(p, dve, u0 + 2 * c + 2, g)
        split_lo(p, dve, u0 + 2 * c + 3, g)
        m = g * 2 + c // 2
        dve.wait_ge(p.sem["unit_done"], g * 8 + (u0 + 2 * c + 2))
        dve.wait_ge(p.sem["gate_tanh"], g * 4 + (a("gate_tanh") + c + 1))
        out = p.work[:, 0] if c % 2 else p.y[:, m]
        v.scalar_tensor_tensor(
            out, p.gate_t[:, c % 2], 1.0, p.psum[:, 2 * (c % 2) + 1, 0:T], ALU.add, ALU.mult
        ).then_inc(p.sem["y_step"], 1)
        if c % 2:
            dve.wait_ge(p.sem["y_step"], g * 4 + (a("y_step") + c + 1))
            v.tensor_tensor(p.y[:, m], p.y[:, m], p.work[:, 0], ALU.add).then_inc(p.sem["y_ready"], 1)

    groups(dve, 16, 4, branch)
    for b in range(2):
        dve.wait_ge(p.sem["y_rounded"], a("y_rounded") + b + 1)
        half = slice(4 * b, 4 * b + 4)
        v.tensor_tensor(p.h_lo[:, half], p.y[:, half], p.h_hi[:, half].bitcast(F32), ALU.subtract).then_inc(
            p.sem["y_split"], 1)
    for m in range(KD):
        split_lo(p, dve, u0 + 34 + m)
        dve.wait_ge(p.sem["unit_done"], u0 + 33 + m)
        v.scalar_tensor_tensor(
            x[:, m], p.psum[:, 4 + m % 4, 0:T], p.mod_g[:, 1, m : m + 1], x[:, m], ALU.mult, ALU.add
        ).then_inc(p.sem["x_ready"], 1)



SH = 32
ROWS = 2 * SH
N_X, N_BC = 16, 4


def ssd_in_tensor(p, pe, st):
    a, u0 = st.at, st.unit0

    def one(g, c):
        if not isinstance(g, int) or 8 * g + c >= 4:
            pe.wait_ge(p.sem["proj_out"], g * 8 + (a("proj_out") + c - 3))
        pe.wait_ge(p.sem["lo_ready"], g * 8 + (u0 + c + 1))
        for k in range(UNIT):
            ins = three_pass(p, p.psum[:, PROJ_BANKS[c % 4], 0:T], (u0 + c) % SLOTS, k,
                             p.h_hi[:, k], p.h_lo[:, k], k == 0, k == UNIT - 1)
        ins.then_inc(p.sem["unit_done"], 1)

    first_pair(p, pe, st, [p.psum[:, PROJ_BANKS[c], 0:T] for c in range(2)])
    for c in range(2, 8):
        one(0, c)
    if st.n_conv >= 24:
        with pe.Fori(1, 3) as g:
            for c in range(8):
                one(g, c)
    else:
        for c in range(8):
            one(1, c)
    for c in range(st.n_conv % 8 + 1):
        one(st.n_conv // 8, c)
    if st.on_ctx:
        skip_unit(p, pe, u0 + 21)


def skip_unit(p, pe, s):
    pe.wait_ge(p.sem["lo_ready"], s + 1)
    p.nc.tensor.matmul(p.psum[:, 7, 0:T], p.w_hi[:, s % SLOTS, 0], p.h_hi[:, 0], start=True, stop=True).then_inc(
        p.sem["unit_done"], 1)


def ssd_in_scalar(p, act, st):
    a, u0, f = st.at, st.unit0, p.nc.scalar.activation

    w = st.par(p, "conv").rearrange("p (t j) -> p t j", j=5)
    bias = st.par(p, "conv_b")

    def silu(g, c):
        act.wait_ge(p.sem["conv_done"], g * 4 + (a("conv_done") + c + 1))
        act.wait_ge(p.sem["loaded"], p.n_loads)
        t = g * 4 + c
        tile = p.sxbc(t)
        f(tile, tile, ACT.Silu).then_inc(p.sem["act_done"], 1)

    for t in range(st.n_conv):
        if t > 1:
            split_hi(p, act, u0 + t + 2)
        act.wait_ge(p.sem["unit_done"], u0 + t + 1)
        if t >= 4:
            act.wait_ge(p.sem["conv_done"], a("conv_done") + t - 3)
        raw = p.psum[:, PROJ_BANKS[t % 4], 0:T]
        f(p.sxbc(t), raw, ACT.Identity, scale=w[:, t, 2:3], bias=bias[:, t : t + 1])
        f(p.sconv_in[:, t % 4, 2 : 2 + T], raw, ACT.Copy).then_inc(p.sem["proj_out"], 1)
        if t:
            silu(0, t - 1)
    t = st.n_conv
    split_hi(p, act, u0 + t + 2)
    silu(0, t - 1)
    act.wait_ge(p.sem["unit_done"], u0 + t + 1)
    f(p.rows[0:ROWS], p.psum[0:ROWS, PROJ_BANKS[t % 4], 0:T], ACT.Copy).then_inc(p.sem["proj_out"], 1)
    if st.on_ctx:
        split_hi(p, act, u0 + t + 3)
    fn, e = a("gate_fn"), p.var[0:ROWS]
    act.wait_ge(p.sem["proj_out"], a("proj_out") + t + 1)
    f(p.exp_a[0:ROWS], st.par(p, "a_log")[0:ROWS], ACT.Exp).then_inc(p.sem["gate_fn"], 1)
    f(e, p.rows[0:ROWS], ACT.Abs, bias=st.par(p, "dt_bias")[0:ROWS]).then_inc(p.sem["gate_fn"], 1)
    act.wait_ge(p.sem["gate_fn"], fn + 2)
    f(e, e, ACT.Exp, scale=-1.0).then_inc(p.sem["gate_fn"], 1)
    act.wait_ge(p.sem["gate_fn"], fn + 3)
    f(e, e, ACT.Ln, bias=1.0).then_inc(p.sem["gate_fn"], 1)
    if st.on_ctx:
        act.wait_ge(p.sem["dt_step"], a("dt_step") + 6)
        f(e, e, ACT.Exp).then_inc(p.sem["gate_fn"], 1)


def ssd_in_gpsimd(p, pool, st):
    pool.wait_ge(p.sem["unit_done"], st.unit0)
    for s in range(4):
        p.nc.gpsimd.memset(p.sconv_in[:, s, 0:2], 0.0)
        p.nc.gpsimd.memset(p.sconv_in[:, s, 2 + T : 4 + T], 0.0).then_inc(p.sem["conv_pad"], 1)


def ssd_in_vector(p, dve, st):
    a, u0, v = st.at, st.unit0, p.nc.vector
    w = st.par(p, "conv").rearrange("p (t j) -> p t j", j=5)
    dve.wait_ge(p.sem["conv_pad"], a("conv_pad") + 4)
    for t in range(st.n_conv):
        if t > 1:
            split_lo(p, dve, u0 + t + 2)
        dve.wait_ge(p.sem["proj_out"], a("proj_out") + t + 1)
        out, src = p.sxbc(t), p.sconv_in[:, t % 4]
        for i, j in enumerate((0, 1, 3, 4)):
            if i:
                dve.wait_ge(p.sem["conv_step"], a("conv_step") + 3 * t + i)
            v.scalar_tensor_tensor(out, src[:, j : j + T], w[:, t, j : j + 1], out, ALU.mult, ALU.add).then_inc(
                p.sem["conv_step" if i < 3 else "conv_done"], 1)
    split_lo(p, dve, u0 + st.n_conv + 2)
    if st.on_ctx:
        split_lo(p, dve, u0 + st.n_conv + 3)
    step = a("dt_step")

    def link(ins):
        nonlocal step
        step += 1
        ins.then_inc(p.sem["dt_step"], 1)
        dve.wait_ge(p.sem["dt_step"], step)

    rows, dt, decay, e = p.rows[0:ROWS], p.soft[0:ROWS], p.rinv[0:ROWS], p.var
    fwd, bwd = slice(0, SH), slice(SH, ROWS)
    dve.wait_ge(p.sem["gate_fn"], a("gate_fn") + 4)
    link(v.tensor_scalar(dt, rows, st.par(p, "dt_bias")[0:ROWS], 0.0, ALU.add, ALU.max))
    link(v.tensor_tensor(dt, dt, e[0:ROWS], ALU.add))
    link(v.tensor_scalar(decay, dt, p.exp_a[0:ROWS], -1.0, ALU.mult, ALU.mult))
    link(v.tensor_tensor_scan(rows, p.c("ones")[0:ROWS, 0:1].to_broadcast([ROWS, T]), decay, 0.0, ALU.mult, ALU.add))
    left = v.tensor_scalar
    if st.on_ctx:
        link(left(e[fwd], p.rows[fwd], p.rows[fwd, T - 1 : T], -1.0, ALU.subtract, ALU.mult))
        link(v.tensor_tensor(e[bwd], p.rows[bwd], p.rinv[bwd], ALU.subtract))
        dve.wait_ge(p.sem["gate_fn"], a("gate_fn") + 5)
        v.tensor_tensor(p.rows[0:ROWS], e[0:ROWS], dt, ALU.mult).then_inc(p.sem["dt_ready"], 1)
    else:
        link(left(e[bwd], p.rows[bwd], p.rows[bwd, T - 1 : T], -1.0, ALU.subtract, ALU.mult))
        v.tensor_tensor(p.rows[bwd], e[bwd], p.rinv[bwd], ALU.add).then_inc(p.sem["dt_ready"], 1)




def turn_tiles(p, pe, st, sources, sem_done, sem_out):
    a = st.at
    for i, (s0, s1) in enumerate(sources):
        if i >= 4:
            pe.wait_ge(p.sem[sem_out], a(sem_out) + i - 3)
        for n in range(4):
            src = (s0, s1)[n // 2][:, n % 2 * P : n % 2 * P + P]
            ins = p.nc.tensor.transpose(p.psum[:, i % 4, n * P : n * P + P], src, p.c("ident"))
        ins.then_inc(p.sem[sem_done], 1)


def state_tensor(p, pe, st):
    a, mm = st.at, p.nc.tensor.matmul
    pe.wait_ge(p.sem["act_done"], a("act_done"))
    pe.wait_ge(p.sem["proj_out"], a("proj_out"))
    pairs = [(p.sxbc(2 * i), p.sxbc(2 * i + 1)) for i in range(10)]
    turn_tiles(p, pe, st, pairs, "sturned", "sturn_out")
    pe.wait_ge(p.sem["dt_ready"], a("dt_ready"))
    for c in range(2):
        ins = mm(p.psum[:, 4, c * ROWS : c * ROWS + ROWS], p.rows[0:ROWS, c * P : c * P + P],
                 p.c("ident")[0:ROWS, 0:ROWS], start=True, stop=True)
    ins.then_inc(p.sem["cols_done"], 1)
    pe.wait_ge(p.sem["sturn_out"], a("sturn_out") + 10)
    for d in range(2):
        pe.wait_ge(p.sem["xw_ready"], a("xw_ready") + 2 * d + 2)
        for g in range(4):
            if d:
                pe.wait_ge(p.sem["state_out"], a("state_out") + g + 1)
            for c in range(2):
                ins = mm(p.psum[:, g], p.b_tok[:, c, g * P : g * P + P], p.xw[:, c, g * 512 : g * 512 + 512],
                         start=c == 0, stop=c == 1)
            ins.then_inc(p.sem["state_sum"], 1)
    pe.wait_ge(p.sem["state_out"], a("state_out") + 8)


def state_scalar(p, act, st):
    a, f = st.at, p.nc.scalar.activation
    for i in range(10):
        act.wait_ge(p.sem["sturned"], a("sturned") + i + 1)
        to = p.x_tok[:, :, 2 * i * P : 2 * i * P + 2 * P] if i < 8 else p.b_tok[:, :, 2 * (i - 8) * P : 2 * (i - 7) * P]
        for c in range(2):
            ins = f(to[:, c].rearrange("p (j n) -> p j n", j=2),
                    p.psum[:, i % 4].rearrange("p (j c n) -> p j c n", j=2, c=2)[:, :, c], ACT.Copy)
        ins.then_inc(p.sem["sturn_out"], 1)
    for d in range(2):
        for g in range(4):
            act.wait_ge(p.sem["state_sum"], a("state_sum") + 4 * d + g + 1)
            f(p.state[:, d, g * 512 : g * 512 + 512], p.psum[:, g], ACT.Copy).then_inc(p.sem["state_out"], 1)


def state_vector(p, dve, st):
    a, v = st.at, p.nc.vector
    dve.wait_ge(p.sem["cols_done"], a("cols_done") + 1)
    v.tensor_copy(p.scols[:, 0].rearrange("p c r -> p (c r)"), p.psum[:, 4, 0 : 2 * ROWS]).then_inc(
        p.sem["cols_ready"], 1)
    dve.wait_ge(p.sem["cols_ready"], a("cols_ready") + 1)
    dve.wait_ge(p.sem["sturn_out"], a("sturn_out") + 10)
    for d in range(2):
        if d:
            dve.wait_ge(p.sem["state_sum"], a("state_sum") + 4)
        for c in range(2):
            v.tensor_tensor(
                p.xw[:, c].rearrange("p (h n) -> p h n", h=SH), p.x_tok[:, c].rearrange("p (h n) -> p h n", h=SH),
                p.scols[:, 0, c, d * SH : d * SH + SH].unsqueeze(2).broadcast_to([P, SH, 64]), ALU.mult,
            ).then_inc(p.sem["xw_ready"], 1)




def spans(d):
    if d == 0:
        return ((0, 0, T, 0, 0), (1, P, T, 0, T))
    return ((1, 0, T, P, 0), (0, 0, P, 2 * P, T))


def mix_tensor(p, pe, st):
    a, mm, ident = st.at, p.nc.tensor.matmul, p.c("ident")
    pe.wait_ge(p.sem["act_done"], a("act_done"))
    pe.wait_ge(p.sem["proj_out"], a("proj_out"))
    turn_tiles(p, pe, st, [(p.sxbc(2 * i), p.sxbc(2 * i + 1)) for i in range(8)], "sturned", "sturn_out")
    pe.wait_ge(p.sem["dt_ready"], a("dt_ready"))
    for b, rows in enumerate((p.rows, p.soft)):
        for c in range(2):
            at = (2 * b + c) * ROWS
            ins = mm(p.psum[:, 4, at : at + ROWS], rows[0:ROWS, c * P : c * P + P], ident[0:ROWS, 0:ROWS],
                     start=True, stop=True)
    ins.then_inc(p.sem["cols_done"], 1)
    for g in range(4):
        for s in range(2):
            ins = mm(p.psum[:, 5 + g % 2, s * T : s * T + T], p.sxbc(N_X + g)[:, s * P : s * P + P],
                     p.sxbc(N_X + N_BC + g), start=True, stop=True)
        ins.then_inc(p.sem["cb_done"], 1)
        if g >= 1:
            pe.wait_ge(p.sem["cb_out"], a("cb_out") + g)
    pe.wait_ge(p.sem["cb_out"], a("cb_out") + 4)
    pe.wait_ge(p.sem["sturn_out"], a("sturn_out") + 8)
    n = 2 * SH
    for i in range(n + 3):
        if i < n:
            h, d = i // 2, i % 2
            if i >= 4:
                pe.wait_ge(p.sem["g_exp"], a("g_exp") + i - 3)
            r = d * SH + h
            mm(p.psum[:, i % 4, 0:T], ident[0:ROWS, r : r + 1].to_broadcast([ROWS, P]), p.rows[0:ROWS],
               start=True, stop=True).then_inc(p.sem["g_row"], 1)
        if i >= 3:
            k = i - 3
            h, d = k // 2, k % 2
            part = slice(64 * (h % 2), 64 * (h % 2) + 64)
            bank = 5 + h // 2 % 2
            if h % 2 == 0 and d == 0 and h >= 4:
                pe.wait_ge(p.sem["sy_out"], a("sy_out") + h // 2 - 1)
            pe.wait_ge(p.sem["sw_ready"], a("sw_ready") + k + 1)
            pe.wait_ge(p.sem["c_dec"], a("c_dec") + k + 1)
            heads = slice(64 * h, 64 * h + 64)
            for j, (s, lo, hi, _, at) in enumerate(spans(d)):
                mm(p.psum[part, bank, lo:hi], p.x_tok[:, s, heads], p.sw[:, k % 4, at : at + hi - lo],
                   start=d == 0 and j == 0, stop=False)
            mm(p.psum[part, bank, 0:T], p.state[:, d, heads], p.c_exp[:, k % 3], start=False,
               stop=d == 1).then_inc(p.sem["sy_part"], 1)


def mix_scalar(p, act, st):
    a, f = st.at, p.nc.scalar.activation
    for i in range(8):
        act.wait_ge(p.sem["sturned"], a("sturned") + i + 1)
        for c in range(2):
            ins = f(p.x_tok[:, c, 2 * i * P : 2 * i * P + 2 * P].rearrange("p (j n) -> p j n", j=2),
                    p.psum[:, i % 4].rearrange("p (j c n) -> p j c n", j=2, c=2)[:, :, c], ACT.Copy)
        ins.then_inc(p.sem["sturn_out"], 1)
    for g in range(4):
        act.wait_ge(p.sem["cb_done"], a("cb_done") + g + 1)
        f(p.cbt[:, g].rearrange("p s t -> p (s t)"), p.psum[:, 5 + g % 2], ACT.Copy).then_inc(p.sem["cb_out"], 1)
    for i in range(2 * SH):
        act.wait_ge(p.sem["sx_ready"], a("sx_ready") + i + 1)
        f(p.sw[:, i % 4], p.sw[:, i % 4], ACT.Exp).then_inc(p.sem["sx_exp"], 1)
        if i >= 4:
            act.wait_ge(p.sem["c_dec"], a("c_dec") + i - 3)
        f(p.g_exp[:, i % 4], p.psum[:, i % 4, 0:T], ACT.Exp).then_inc(p.sem["g_exp"], 1)


def mix_gpsimd(p, pool, st):
    a = st.at
    for i in range(2 * SH):
        pool.wait_ge(p.sem["g_exp"], a("g_exp") + i + 1)
        if i >= 3:
            pool.wait_ge(p.sem["sy_part"], a("sy_part") + i - 2)
        p.nc.gpsimd.tensor_tensor(p.c_exp[:, i % 3], p.sxbc(N_X + N_BC + i // 16), p.g_exp[:, i % 4], ALU.mult).then_inc(
            p.sem["c_dec"], 1)


def mix_vector(p, dve, st):
    a, v = st.at, p.nc.vector
    dve.wait_ge(p.sem["cols_done"], a("cols_done") + 1)
    v.tensor_copy(p.scols[:].rearrange("p b c r -> p (b c r)"), p.psum[:, 4, 0 : 4 * ROWS]).then_inc(
        p.sem["cols_ready"], 1)
    dve.wait_ge(p.sem["cols_ready"], a("cols_ready") + 1)
    dve.wait_ge(p.sem["cb_out"], a("cb_out") + 4)
    n = 2 * SH
    for i in range(n + 2):
        if i < n:
            h, d = i // 2, i % 2
            dve.wait_ge(p.sem["g_row"], a("g_row") + i + 1)
            if i >= 4:
                dve.wait_ge(p.sem["sy_part"], a("sy_part") + i - 3)
            for j, (s, lo, hi, mask, at) in enumerate(spans(d)):
                ins = v.scalar_tensor_tensor(
                    p.sw[:, i % 4, at : at + hi - lo], p.psum[:, i % 4, lo:hi],
                    p.scols[:, 0, s, d * SH + h : d * SH + h + 1], p.c("neg")[:, mask : mask + hi - lo],
                    ALU.subtract, ALU.add)
            ins.then_inc(p.sem["sx_ready"], 1)
        if 1 <= i <= n:
            k = i - 1
            h, d = k // 2, k % 2
            dve.wait_ge(p.sem["sx_exp"], a("sx_exp") + k + 1)
            for j, (s, lo, hi, mask, at) in enumerate(spans(d)):
                part = p.sw[:, k % 4, at : at + hi - lo]
                ins = v.scalar_tensor_tensor(
                    part, part, p.scols[:, 1, s, d * SH + h : d * SH + h + 1], p.cbt[:, h // 8, s, lo:hi],
                    ALU.mult, ALU.mult)
            ins.then_inc(p.sem["sw_ready"], 1)
        if i >= 7 and (i - 7) % 4 == 0:
            j = (i - 7) // 4
            sy_out(p, dve, st, j)
    for j in range((n + 1 - 7) // 4 + 1, N_X):
        sy_out(p, dve, st, j)


def sy_out(p, dve, st, j):
    dve.wait_ge(p.sem["sy_part"], st.at("sy_part") + 4 * j + 4)
    p.nc.vector.scalar_tensor_tensor(
        p.sxbc(j), p.sxbc(j), st.par(p, "d_skip")[:, j : j + 1], p.psum[:, 5 + j % 2, 0:T], ALU.mult, ALU.add
    ).then_inc(p.sem["sy_out"], 1)




def ssd_out_tensor(p, pe, st):
    a, u0, mm = st.at, st.unit0, p.nc.tensor.matmul
    pe.wait_ge(p.sem["sy_out"], a("sy_out"))
    for t in range(N_X):
        s = u0 + t
        if t >= 2:
            pe.wait_ge(p.sem["gate_act"], a("gate_act") + t - 1)
        pe.wait_ge(p.sem["lo_ready"], s + 1)
        for k in range(UNIT):
            ins = three_pass(p, p.psum[:, t % 2, 0:T], s % SLOTS, k, p.h_hi[:, k], p.h_lo[:, k], k == 0, k == UNIT - 1)
        ins.then_inc(p.sem["unit_done"], 1)
        if t >= 2:
            sz_sum(p, pe, st, t - 2)
    skip_unit(p, pe, u0 + N_X)
    sz_sum(p, pe, st, N_X - 2)
    sz_sum(p, pe, st, N_X - 1)
    pe.wait_ge(p.sem["o_root"], a("o_root") + 1)
    for g in range(4):
        mm(p.psum[:, g, 0:T], p.c("ident")[0:16, g : g + 1].to_broadcast([16, P]), p.rinv16[0:16],
           start=True, stop=True).then_inc(p.sem["len_row"], 1)
    for m in range(KD):
        if m >= 2:
            pe.wait_ge(p.sem["x_ready"], a("x_ready") + m - 1)
        for b in range(2):
            s = u0 + N_X + 1 + 2 * m + b
            pe.wait_ge(p.sem["lo_ready"], s + 1)
            for k in range(UNIT):
                if m == 0:
                    pe.wait_ge(p.sem["gy_split"], a("gy_split") + 8 * b + k + 1)
                ins = three_pass(p, p.psum[:, 4 + m % 2, 0:T], s % SLOTS, k, p.gy_hi[:, 8 * b + k], p.gy_lo[:, 8 * b + k],
                                 k == 0 and b == 0, k == UNIT - 1 and b == 1)
            ins.then_inc(p.sem["unit_done"], 1)


def sz_sum(p, pe, st, t):
    pe.wait_ge(p.sem["sz_sq"], st.at("sz_sq") + t + 1)
    p.nc.tensor.matmul(p.psum[0:16, 6, 0:T], p.pick("row", t // 4), p.tmp[:, t % 8], start=t == 0, stop=t == N_X - 1,
                       skip_group_check=True).then_inc(p.sem["sz_summed"], 1)


def ssd_out_scalar(p, act, st):
    a, u0, f = st.at, st.unit0, p.nc.scalar.activation
    for t in range(N_X):
        split_hi(p, act, u0 + t + 2)
        act.wait_ge(p.sem["unit_done"], u0 + t + 1)
        if t >= 2:
            act.wait_ge(p.sem["sz_gated"], a("sz_gated") + t - 1)
        f(p.sz[:, t % 2], p.psum[:, t % 2, 0:T], ACT.Silu).then_inc(p.sem["gate_act"], 1)
    split_hi(p, act, u0 + N_X + 2)
    act.wait_ge(p.sem["sz_var"], a("sz_var") + 2)
    f(p.rinv16[0:16], p.rinv16[0:16], ACT.Sqrt).then_inc(p.sem["o_root"], 1)
    for t in range(N_X):
        act.wait_ge(p.sem["gy_scaled"], a("gy_scaled") + t + 1)
        f(p.gy_hi[:, t], p.sxbc(t), ACT.Copy).then_inc(p.sem["gy_rounded"], 1)
        if t < 2:
            split_hi(p, act, u0 + N_X + 3 + t)
    for t in range(2, N_X):
        split_hi(p, act, u0 + N_X + 3 + t)


def ssd_out_gpsimd(p, pool, st):
    a = st.at
    for t in range(N_X):
        pool.wait_ge(p.sem["sz_gated"], a("sz_gated") + t + 1)
        if t >= 8:
            pool.wait_ge(p.sem["sz_summed"], a("sz_summed") + t - 7)
        p.nc.gpsimd.tensor_tensor(p.tmp[:, t % 8], p.sxbc(t), p.sxbc(t), ALU.mult).then_inc(p.sem["sz_sq"], 1)


def ssd_out_vector(p, dve, st):
    a, u0, v, x = st.at, st.unit0, p.nc.vector, st.x(p)
    for t in range(N_X):
        split_lo(p, dve, u0 + t + 2)
        dve.wait_ge(p.sem["gate_act"], a("gate_act") + t + 1)
        v.tensor_tensor(p.sxbc(t), p.sxbc(t), p.sz[:, t % 2], ALU.mult).then_inc(p.sem["sz_gated"], 1)
    split_lo(p, dve, u0 + N_X + 2)
    dve.wait_ge(p.sem["sz_summed"], a("sz_summed") + N_X)
    v.tensor_scalar(p.rinv16[0:16], p.psum[0:16, 6, 0:T], 1.0 / 512, EPS, ALU.mult, ALU.add).then_inc(p.sem["sz_var"], 1)
    dve.wait_ge(p.sem["sz_var"], a("sz_var") + 1)
    v.reciprocal(p.rinv16[0:16], p.rinv16[0:16]).then_inc(p.sem["sz_var"], 1)
    gain = st.par(p, "norm_g")

    def low(t):
        dve.wait_ge(p.sem["gy_rounded"], a("gy_rounded") + t + 1)
        v.tensor_tensor(p.gy_lo[:, t], p.sxbc(t), p.gy_hi[:, t].bitcast(F32), ALU.subtract).then_inc(p.sem["gy_split"], 1)

    for t in range(N_X):
        dve.wait_ge(p.sem["len_row"], a("len_row") + t // 4 + 1)
        v.scalar_tensor_tensor(
            p.sxbc(t), p.sxbc(t), gain[:, t : t + 1], p.psum[:, t // 4, 0:T], ALU.mult, ALU.mult
        ).then_inc(p.sem["gy_scaled"], 1)
        if t:
            low(t - 1)
        if t % 8 == 7:
            split_lo(p, dve, u0 + N_X + 3 + t // 8)
    low(N_X - 1)
    for t in range(2, N_X):
        split_lo(p, dve, u0 + N_X + 3 + t)
        if t % 2:
            out_x(p, dve, st, x, t // 2 - 1)
    out_x(p, dve, st, x, KD - 1)


def out_x(p, dve, st, x, m):
    dve.wait_ge(p.sem["unit_done"], st.unit0 + N_X + 1 + 2 * m + 2)
    p.nc.vector.scalar_tensor_tensor(
        x[:, m], p.psum[:, 4 + m % 2, 0:T], p.mod_g[:, 1, m : m + 1], x[:, m], ALU.mult, ALU.add
    ).then_inc(p.sem["x_ready"], 1)




def pool_tensor(p, pe, st):
    a, u0, mm = st.at, st.unit0, p.nc.tensor.matmul
    pe.wait_ge(p.sem["h_whole"], a("h_whole") + 1)
    turn_tiles(p, pe, st, [(p.h_f32[:, 2 * i], p.h_f32[:, 2 * i + 1]) for i in range(4)], "sturned", "sturn_out")
    pe.wait_ge(p.sem["sturn_out"], a("sturn_out") + 4)
    pe.wait_ge(p.sem["means_loaded"], 16)
    for t in range(KD):
        for c in range(2):
            ins = mm(p.psum[:, 4 + t % 4, 0:T], p.h_tok[:, c, t * P : t * P + P], p.means[:, c, t // 2],
                     start=c == 0, stop=c == 1)
        ins.then_inc(p.sem["pooled"], 1)
        if t >= 3:
            pe.wait_ge(p.sem["pool_split"], a("pool_split") + t - 2)
    pe.wait_ge(p.sem["pool_split"], a("pool_split") + KD)
    for t in range(KD):
        g, b = t // 2, t % 2
        s = u0 + g // 2
        if t % 4 == 0:
            pe.wait_ge(p.sem["lo_ready"], s + 1)
        if t >= 4:
            pe.wait_ge(p.sem["x_ready"], a("x_ready") + t - 3)
        for k in range(2):
            ins = three_pass(p, p.psum[:, PROJ_BANKS[t % 4], 0:T], s % SLOTS, 4 * (g % 2) + 2 * b + k,
                             p.p_hi[:, 2 * g + k], p.p_lo[:, 2 * g + k], k == 0, k == 1)
        if t % 4 == 3:
            ins.then_inc(p.sem["unit_done"], 1)
        else:
            ins.then_inc(p.sem["pool_out"], 1)


def pool_scalar(p, act, st):
    a, u0, f = st.at, st.unit0, p.nc.scalar.activation
    for i in range(4):
        act.wait_ge(p.sem["sturned"], a("sturned") + i + 1)
        for c in range(2):
            ins = f(p.h_tok[:, c, 2 * i * P : 2 * i * P + 2 * P].rearrange("p (j n) -> p j n", j=2),
                    p.psum[:, i % 4].rearrange("p (j c n) -> p j c n", j=2, c=2)[:, :, c], ACT.Copy)
        ins.then_inc(p.sem["sturn_out"], 1)
    for t in range(KD):
        act.wait_ge(p.sem["pooled"], a("pooled") + t + 1)
        f(p.p_hi[:, t], p.psum[:, 4 + t % 4, 0:T], ACT.Copy).then_inc(p.sem["pool_rounded"], 1)


def pool_vector(p, dve, st):
    a, u0, v, x = st.at, st.unit0, p.nc.vector, st.x(p)
    dve.wait_ge(p.sem["h_ready"], a("h_ready"))
    v.tensor_tensor(p.h_f32[:], p.h_hi[:].bitcast(F32), p.h_lo[:].bitcast(F32), ALU.add).then_inc(p.sem["h_whole"], 1)
    for t in range(KD):
        dve.wait_ge(p.sem["pool_rounded"], a("pool_rounded") + t + 1)
        v.tensor_tensor(p.p_lo[:, t], p.psum[:, 4 + t % 4, 0:T], p.p_hi[:, t].bitcast(F32), ALU.subtract).then_inc(
            p.sem["pool_split"], 1)
    v.tensor_tensor(p.mod_g[:, 1], p.mod_g[:, 1], st.par(p, "pool_scale"), ALU.mult).then_inc(p.sem["pool_factor"], 1)
    dve.wait_ge(p.sem["pool_factor"], a("pool_factor") + 1)
    bias = st.par(p, "pool_b")
    for t in range(KD):
        if t % 4 == 3:
            dve.wait_ge(p.sem["unit_done"], u0 + t // 4 + 1)
        else:
            dve.wait_ge(p.sem["pool_out"], a("pool_out") + t - t // 4 + 1)
        v.tensor_scalar(
            p.sz[:, t % 2], p.psum[:, PROJ_BANKS[t % 4], 0:T], bias[:, t : t + 1], p.mod_g[:, 1, t : t + 1], ALU.add, ALU.mult
        ).then_inc(p.sem["pool_step"], 1)
        dve.wait_ge(p.sem["pool_step"], a("pool_step") + t + 1)
        v.tensor_tensor(x[:, t], x[:, t], p.sz[:, t % 2], ALU.add).then_inc(p.sem["x_ready"], 1)




def final_vector(p, dve, st):
    root_vector(p, dve, st)
    for m in range(KD):
        p.nc.vector.scalar_tensor_tensor(
            p.tmp[:, m], p.x[:, m], st.par(p, "final_g")[:, m : m + 1], p.psum[:, 3, 0:T], ALU.mult, ALU.mult
        ).then_inc(p.sem["y_normed"], 1)






def fetch_scalar(p, act, st):
    if st.at("x_ready"):
        act.wait_ge(p.sem["x_ready"], st.at("x_ready"))
    if st.what == "ctx":
        act.dma_start(p.ctx_x[:], p.dram["ctx"]).then_inc(p.sem["ctx_loaded"], 16)
    else:
        act.dma_start(p.means[:], p.dram["means"]).then_inc(p.sem["means_loaded"], 16)


STAGES = {
    "tensor": dict(norm=norm_tensor, ffn=ffn_tensor, project=project_tensor, gdn=gdn_tensor,
                   up=up_tensor, attn=attn_tensor, gates=gates_tensor, ssd_in=ssd_in_tensor, state=state_tensor,
                   mix=mix_tensor, ssd_out=ssd_out_tensor, pool=pool_tensor, final=norm_tensor),
    "scalar": dict(norm=norm_scalar, ffn=ffn_scalar, project=project_scalar, gdn=gdn_scalar, up=up_scalar,
                   attn=attn_scalar, gates=gates_scalar, ssd_in=ssd_in_scalar, state=state_scalar, mix=mix_scalar,
                   ssd_out=ssd_out_scalar, pool=pool_scalar, final=root_scalar, fetch=fetch_scalar),
    "vector": dict(prep=prep_vector, norm=norm_vector, ffn=ffn_vector, project=project_vector, gdn=gdn_vector,
                   up=up_vector, attn=attn_vector, gates=gates_vector, ssd_in=ssd_in_vector, state=state_vector,
                   mix=mix_vector, ssd_out=ssd_out_vector, pool=pool_vector, final=final_vector),
    "gpsimd": dict(norm=norm_gpsimd, final=norm_gpsimd, ffn=ffn_gpsimd,
                   project=project_gpsimd, up=up_gpsimd, ssd_in=ssd_in_gpsimd, mix=mix_gpsimd, ssd_out=ssd_out_gpsimd),
}


ADA_FIRST = (0, 72, 144, 184, 256)
ADA_HEAD = 28


def plan():
    stages = []
    tile = 0

    def add(kind, **more):
        stages.append(Stage(kind, **more))

    def branch(n, vec, tiles, which, n_vec=3, **more):
        nonlocal tile
        add("prep", n=n, n_vec=n_vec, ada0=ADA_FIRST[which], **more)
        add("norm", n=n, **more)
        if n != 1:
            add("ffn", n=n, vec=vec, ada0=tile, ada_n=tiles, **more)
            tile += tiles

    more = dict(block=1, layer=0, gate_add=1.0, gate_scale=(0.5, 0.5, 0.5))
    add("head", ada_n=ADA_HEAD, **more)
    tile += ADA_HEAD
    for layer in range(DEPTH):
        more["layer"] = layer
        branch(0, 0, (44, 28)[layer], layer, **more)
        branch(1, 0, 0, layer, **more)
        for kind in ("project", "gdn", "up", "attn", "gates"):
            add(kind, n=1, **more)
        if layer == DEPTH - 1:
            add("fetch", what="ctx", **more)
        branch(2, (0, 2)[layer], (44, 40)[layer], layer, **more)

    more = dict(block=2, layer=0, gate_add=0.0, gate_scale=(0.5, 1.0, 0.5))
    branch(0, 1, 40, 2, on_ctx=True, **more)
    branch(1, 1, 0, 2, n_vec=2, on_ctx=True, **more)
    add("ssd_in", n=1, n_conv=20, on_ctx=True, **more)
    add("state", n=1, **more)
    branch(0, 1, 40, 3, **more)
    branch(1, 1, 0, 3, **more)
    add("ssd_in", n=1, n_conv=24, **more)
    add("mix", n=1, **more)
    add("ssd_out", n=1, **more)
    add("fetch", what="means", **more)
    branch(2, 1, 40, 3, **more)
    more["layer"] = 1
    branch(0, 1, 24, 4, **more)
    branch(1, 1, 0, 4, **more)
    add("pool", n=1, **more)
    branch(2, 1, 0, 4, **more)
    add("final", **more)
    return stages


def build(nc, dram, out, stages):
    with ExitStack() as ctx:
        p = Program(nc, ctx, stages, dram)
        tables = [(p.positions[:], dram["positions"]), (p.const[:], dram["const"])]
        loads = [(p.par1[:], dram["par1"]), (p.par2[:], dram["par2"]), (p.x[:], dram["x"])]
        n_loads = p.n_loads = 16 * len(loads)
        block = ctx.enter_context(nc.Block())

        def walk(eng, which):
            for st in stages:
                if st.kind in STAGES[which]:
                    STAGES[which][st.kind](p, eng, st)

        @block.sync
        def _(sp):
            sp.dma_start(p.c_row, dram["c"][0]).then_inc(p.sem["c_row_full"], 16)
            for to, src in tables:
                sp.dma_start(to, src).then_inc(p.sem["tables_loaded"], 16)
            for to, src in loads:
                sp.dma_start(to, src).then_inc(p.sem["loaded"], 16)
            load_units(p, sp)
            if "x_ready" in p.total:
                sp.wait_ge(p.sem["x_ready"], p.total["x_ready"])
            if "y_normed" in p.total:
                sp.wait_ge(p.sem["y_normed"], p.total["y_normed"])
            sp.dma_start(out, (p.tmp if "y_normed" in p.total else p.x)[:]).then_inc(p.sem["stored"], 16)
            sp.wait_ge(p.sem["stored"], 16)

        @block.gpsimd
        def _(pool):
            nc.gpsimd.memset(p.rows[:], 0.0).then_inc(p.sem["rows_cleared"], 1)
            pool.wait_ge(p.sem["loaded"], n_loads)
            walk(pool, "gpsimd")

        @block.scalar
        def _(act):
            for s in range(ADA_SLOTS - 1):
                ada_load(p, act, s)
            act.wait_ge(p.sem["tables_loaded"], 32)
            head_scalar(p, act, stages[0])
            trig_scalar(p, act)
            act.wait_ge(p.sem["rows_cleared"], 1)
            split_hi(p, act, 0)
            split_hi(p, act, 1)
            walk(act, "scalar")

        @block.vector
        def _(dve):
            dve.wait_ge(p.sem["tables_loaded"], 32)
            trig_vector(p, dve)
            head_vector(p, dve, stages[0])
            dve.wait_ge(p.sem["loaded"], n_loads)
            dve.wait_ge(p.sem["rows_cleared"], 1)
            split_lo(p, dve, 0)
            split_lo(p, dve, 1)
            walk(dve, "vector")

        @block.tensor
        def _(pe):
            pe.wait_ge(p.sem["tables_loaded"], 32)
            pe.wait_ge(p.sem["loaded"], n_loads)
            walk(pe, "tensor")


def gather_inputs(i):
    layers = range(DEPTH)
    f = lambda name: np.asarray(i[name])
    units = []
    for l in layers:
        units += ffn_units(f("ffn1_w1")[l], f("ffn1_w3")[l], f("ffn1_w2")[l])
        units += first_mix_units(*(f(n)[l] for n in (
            "w_in", "mla_w_q_up", "mla_w_kv_up", "w_branch_a", "w_branch_b", "w_out")))
        units += ffn_units(f("ffn2_w1")[l], f("ffn2_w3")[l], f("ffn2_w2")[l])
    g = lambda name: np.asarray(i[name + "_2"])
    ffn = lambda l, n: ffn_units(g("ffn_w_gate")[l, n], g("ffn_w_up")[l, n], g("ffn_w_down")[l, n])
    w_in = g("ssd_w_in")[0]
    units += ffn(0, 0) + ssd_in_units(w_in, True) + ffn(0, 0) + ssd_in_units(w_in, False)
    units += ssd_out_units(w_in, g("ssd_w_out")[0]) + ffn(0, 1) + ffn(1, 0) + pool_units(g("pool_w")[0]) + ffn(1, 1)
    stream = np.concatenate(units, 0)
    stream = stream.reshape(-1, 2, P, UNIT * P).transpose(0, 2, 1, 3).reshape(-1, P, 2 * UNIT * P)
    ada = np.concatenate([ada_tiles(f("ada_w")[l]) for l in layers] + [
        ada_tiles(g("ada_w")[0][:, : 5 * D]), ada_tiles(g("ada_w")[0]), ada_tiles(g("ada_w")[1])], 0)
    par1 = np.stack([np.concatenate([
        columns(f("ada_b")[l]), columns(f("norm_ffn1")[l]), columns(f("norm_mix")[l]), columns(f("norm_ffn2")[l]),
        f("gdn_conv")[l].reshape(4, 24, P).transpose(2, 1, 0).reshape(P, 96),
        f("gdn_out_gain")[l][:, None], columns(f("mla_q_lat_gain")[l]), columns(f("mla_kv_lat_gain")[l]),
        f("mla_q_norm")[l][:P, None], np.tile(f("mla_q_norm")[l][P:], 2)[:, None],
        f("mla_k_norm")[l][:P, None], np.tile(f("mla_k_norm")[l][P:], 2)[:, None],
        rows_at((32, f("gdn_a_log")[l])), rows_at((32, f("gdn_dt_bias")[l])),
    ], 1) for l in layers], 1)
    par2 = np.stack([np.concatenate([
        columns(g("ada_b")[l]), columns(g("norm_g")[l].reshape(-1)),
        g("ssd_conv_w")[0].reshape(5, 24, P).transpose(2, 1, 0).reshape(P, 120), columns(g("ssd_conv_b")[0]),
        columns(np.repeat(g("ssd_d")[0], 64)), columns(g("ssd_norm_g")[0]),
        rows_at((0, g("ssd_a_log")[0].reshape(-1))), rows_at((0, g("ssd_dt_bias")[0].reshape(-1))),
        columns(g("pool_b")[0].reshape(-1)), columns(g("pool_scale")[0]), columns(g("final_g")),
    ], 1) for l in layers], 1)
    c = np.stack([np.broadcast_to(row, (P, D)) for row in (f("c")[0], g("c")[0], g("c_ctx"))])
    tokens = lambda x: x.T.reshape(KD, P, T).transpose(1, 0, 2)
    return dict(stream=stream, ada=ada, par1=par1, par2=par2, c=c, x=tokens(f("x")[0]), ctx=tokens(g("ctx")[0]), means=window_means(), const=constants(),
                positions=np.broadcast_to(f("positions").astype(np.int32), (P, T)))


def kernel(**inputs):
    from concourse import bacc
    from concourse.bass_utils import run_bass_kernel_spmd

    arrays = {k: np.ascontiguousarray(v) for k, v in gather_inputs(inputs).items()}
    nc = bacc.Bacc("TRN2", target_bir_lowering=False, num_devices=1)
    dram = {
        k: nc.dram_tensor(k + "_dram", v.shape, mybir.dt.from_np(v.dtype), kind="ExternalInput").ap()
        for k, v in arrays.items()
    }
    out = nc.dram_tensor("out_dram", (P, KD, T), F32, kind="ExternalOutput").ap()
    build(nc, dram, out, plan())
    r = run_bass_kernel_spmd(nc, [{k + "_dram": v for k, v in arrays.items()}], core_ids=[0])
    y = r.results[0]["out_dram"]
    return y.transpose(1, 0, 2).reshape(D, T).T.reshape(1, T, D)
```
